# Optimizing a Trainium2 kernel written in Bass

```python
import jax
import jax.numpy as jnp
from jax import lax
import numpy as np

D_MODEL = 1024
BATCH = 1
SEQ = 256
DEPTH = 2

N_MIXERS = 2
N_RWKV = (DEPTH + N_MIXERS - 1) // N_MIXERS
N_NSA = DEPTH // N_MIXERS
N_VRES = N_RWKV - 1

NORM_EPS = 1e-6
MLP_HIDDEN = 4 * D_MODEL

RWKV_HEAD_DIM = 64
RWKV_HEADS = D_MODEL // RWKV_HEAD_DIM
RWKV_GN_EPS = 64e-5
LORA_DECAY = max(32, int(round(1.8 * D_MODEL ** 0.5 / 32)) * 32)
LORA_ICLR = max(32, int(round(1.8 * D_MODEL ** 0.5 / 32)) * 32)
LORA_VRES = max(32, int(round(1.3 * D_MODEL ** 0.5 / 32)) * 32)
LORA_GATE = max(32, int(round(0.6 * D_MODEL ** 0.8 / 32)) * 32)

NSA_HEAD_DIM = 64
NSA_HEADS = D_MODEL // NSA_HEAD_DIM
NSA_KV_HEADS = NSA_HEADS // 4
NSA_GROUP = NSA_HEADS // NSA_KV_HEADS
CMP_BLOCK = 32
CMP_STRIDE = 16
CMP_HIDDEN = 2 * NSA_HEAD_DIM
SLC_BLOCK = 64
N_SELECT = 16
WINDOW = 512
Q_BLOCK = 64
SEL_BIG = 1e9
NSA_Q_COLS = NSA_HEADS * NSA_HEAD_DIM
NSA_KV_COLS = NSA_KV_HEADS * NSA_HEAD_DIM
NSA_IN_COLS = NSA_Q_COLS + 6 * NSA_KV_COLS + 3 * NSA_HEADS

kernel_name = "rwkv7_nsa_interleaved_hybrid"

def rms_norm(x, g):
    xf = x.astype(jnp.float32)
    y = xf * lax.rsqrt(jnp.mean(xf * xf, axis=-1, keepdims=True) + NORM_EPS)
    return (y * g.astype(jnp.float32)).astype(x.dtype)

def masked_softmax(s, mask):
    s = jnp.where(mask, s.astype(jnp.float32), -jnp.inf)
    m = jnp.max(s, axis=-1, keepdims=True)
    m = jnp.where(jnp.isfinite(m), m, 0.0)
    e = jnp.where(mask, jnp.exp(s - m), 0.0)
    return e / jnp.maximum(jnp.sum(e, axis=-1, keepdims=True), 1e-30)

def alibi_slopes(n):
    return jnp.exp2(-8.0 * (jnp.arange(n, dtype=jnp.float32) + 1.0) / n)

def squared_relu_mlp(x, w1, w2):
    return jnp.square(jax.nn.relu(x @ w1)) @ w2

def wkv7_scan(r, w, k, v, a, b):
    B, T, H, N = r.shape

    def step(S, inp):
        r_t, w_t, k_t, v_t, a_t, b_t = inp
        sa = jnp.einsum('bhij,bhj->bhi', S, a_t)
        S = S * w_t[:, :, None, :] + sa[..., None] * b_t[:, :, None, :] + v_t[..., None] * k_t[:, :, None, :]
        return S, jnp.einsum('bhij,bhj->bhi', S, r_t)

    seq = tuple(jnp.moveaxis(t.astype(jnp.float32), 1, 0) for t in (r, w, k, v, a, b))
    S0 = jnp.zeros((B, H, N, N), jnp.float32)
    _, y = lax.scan(step, S0, seq)
    return jnp.moveaxis(y, 0, 1)

def rwkv7_time_mix(x, mu, w_in, w0, w1, w2, a0, a1, a2, g1, g2, k_k, k_a, r_k, ln_w, ln_b, w_out,
                   v_first, vres):
    B, T, C = x.shape
    H, N = RWKV_HEADS, RWKV_HEAD_DIM
    dx = jnp.pad(x, ((0, 0), (1, 0), (0, 0)))[:, :-1] - x
    xr, xw, xk, xv, xa, xg = (x + dx * mu[i] for i in range(6))
    rkv = jnp.einsum('nbtc,cnf->nbtf', jnp.stack([xr, xk, xv]), w_in.reshape(C, 3, C))
    r, k, v = rkv[0], rkv[1], rkv[2]
    v_raw = v
    if vres is not None:
        v0, v1, v2 = vres
        v = v + (v_first - v) * jax.nn.sigmoid(v0 + (xv @ v1) @ v2)
    w_log = -jax.nn.softplus(-(w0 + jnp.tanh(xw @ w1) @ w2)) - 0.5
    decay = jnp.exp(-jnp.exp(w_log.astype(jnp.float32)))
    a = jax.nn.sigmoid(a0 + (xa @ a1) @ a2)
    g = jax.nn.sigmoid(xg @ g1) @ g2

    def heads(t):
        return t.reshape(B, T, H, N)

    kk = heads(k * k_k).astype(jnp.float32)
    kk = kk / jnp.maximum(jnp.sqrt(jnp.sum(kk * kk, axis=-1, keepdims=True)), 1e-12)
    k = k * (1 + (a - 1) * k_a)
    r_h, k_h, v_h = heads(r), heads(k), heads(v)
    y = wkv7_scan(r_h, heads(decay), k_h, v_h, -kk, kk * heads(a).astype(jnp.float32))
    mean = jnp.mean(y, axis=-1, keepdims=True)
    var = jnp.mean(jnp.square(y - mean), axis=-1, keepdims=True)
    y = ((y - mean) * lax.rsqrt(var + RWKV_GN_EPS)).reshape(B, T, C) * ln_w.astype(jnp.float32) \
        + ln_b.astype(jnp.float32)
    bonus = jnp.sum((r_h * k_h * r_k).astype(jnp.float32), axis=-1, keepdims=True) * v_h.astype(jnp.float32)
    y = (y + bonus.reshape(B, T, C)) * g.astype(jnp.float32)
    return y.astype(x.dtype) @ w_out, v_raw

def nsa_compress(t, pe, w1, w2):
    B, T, HKV, DH = t.shape
    tr = t.reshape(B, T // CMP_STRIDE, CMP_STRIDE, HKV, DH)
    blocks = jnp.concatenate([tr[:, :-1], tr[:, 1:]], axis=2) + pe[None, None, :, None, :]
    n_blk = blocks.shape[1]
    flat = jnp.moveaxis(blocks, 3, 2).reshape(B, n_blk, HKV, CMP_BLOCK * DH)
    return jax.nn.gelu(flat @ w1) @ w2

def nsa_mix(x, w_in, cmp_pe, cmp_w1, cmp_w2, q_norm, k_norm, w_out):
    B, T, C = x.shape
    H, HKV, G, DH = NSA_HEADS, NSA_KV_HEADS, NSA_GROUP, NSA_HEAD_DIM
    proj = x @ w_in
    q = rms_norm(proj[..., :NSA_Q_COLS].reshape(B, T, HKV, G, DH), q_norm)
    kvs = proj[..., NSA_Q_COLS:NSA_Q_COLS + 6 * NSA_KV_COLS].reshape(B, T, 6, HKV, DH)
    kc, vc, ks, vs, kw, vw = (kvs[:, :, i] for i in range(6))
    gates = jax.nn.sigmoid(proj[..., NSA_Q_COLS + 6 * NSA_KV_COLS:].astype(jnp.float32)).reshape(B, T, HKV, G, 3)

    k_cmp = rms_norm(nsa_compress(kc, cmp_pe[0], cmp_w1[0], cmp_w2[0]), k_norm[0])
    v_cmp = nsa_compress(vc, cmp_pe[1], cmp_w1[1], cmp_w2[1])
    n_blk = k_cmp.shape[1]
    cmp_start = jnp.arange(n_blk) * CMP_STRIDE
    cmp_end = cmp_start + CMP_BLOCK - 1

    n_slc = T // SLC_BLOCK
    n_sel = min(N_SELECT, n_slc)
    ks_blocks = rms_norm(ks, k_norm[1]).reshape(B, n_slc, SLC_BLOCK, HKV, DH).transpose(0, 3, 1, 2, 4)
    vs_blocks = vs.reshape(B, n_slc, SLC_BLOCK, HKV, DH).transpose(0, 3, 1, 2, 4)
    slc_start = jnp.arange(n_slc) * SLC_BLOCK
    overlap = ((cmp_start[:, None] <= slc_start[None, :] + SLC_BLOCK - 1)
               & (cmp_end[:, None] >= slc_start[None, :])).astype(jnp.float32)

    pad = ((0, 0), (WINDOW, 0), (0, 0), (0, 0))
    kw_p = jnp.pad(rms_norm(kw, k_norm[2]), pad)
    vw_p = jnp.pad(vw, pad)

    slopes = alibi_slopes(H).reshape(HKV, G)[None, :, :, None, None]
    scale = DH ** -0.5
    b_ix = jnp.arange(B)[:, None, None, None]
    h_ix = jnp.arange(HKV)[None, :, None, None]
    blk = jnp.arange(n_slc)

    def q_block(i):
        q0 = i * Q_BLOCK
        t = q0 + jnp.arange(Q_BLOCK)
        qb = lax.dynamic_slice_in_dim(q, q0, Q_BLOCK, axis=1)

        dist_c = t[:, None] - cmp_end[None, :]
        s = jnp.einsum('bqhgd,bnhd->bhgqn', qb, k_cmp) * scale - slopes * dist_c
        p_c = masked_softmax(s, dist_c >= 0)
        o_c = jnp.einsum('bhgqn,bnhd->bqhgd', p_c, v_cmp.astype(jnp.float32))

        imp = jnp.einsum('bhgqn,nj->bhqj', p_c, overlap)
        cur = (t // SLC_BLOCK)[:, None]
        forced = (blk[None, :] == 0) | (blk[None, :] == cur) | (blk[None, :] == cur - 1)
        imp = jnp.where(forced, SEL_BIG, imp)
        imp = jnp.where(slc_start[None, :] <= t[:, None], imp, -SEL_BIG)
        _, top_idx = lax.top_k(imp, n_sel)
        k_sel = ks_blocks[b_ix, h_ix, top_idx].reshape(B, HKV, Q_BLOCK, n_sel * SLC_BLOCK, DH)
        v_sel = vs_blocks[b_ix, h_ix, top_idx].reshape(B, HKV, Q_BLOCK, n_sel * SLC_BLOCK, DH)
        s_pos = (top_idx[..., None] * SLC_BLOCK + jnp.arange(SLC_BLOCK)).reshape(B, HKV, Q_BLOCK, n_sel * SLC_BLOCK)
        dist_s = (t[:, None] - s_pos)[:, :, None]
        s = jnp.einsum('bqhgd,bhqkd->bhgqk', qb, k_sel) * scale - slopes * dist_s
        p_s = masked_softmax(s, dist_s >= 0)
        o_s = jnp.einsum('bhgqk,bhqkd->bqhgd', p_s, v_sel.astype(jnp.float32))

        kwb = lax.dynamic_slice_in_dim(kw_p, q0, WINDOW + Q_BLOCK, axis=1)
        vwb = lax.dynamic_slice_in_dim(vw_p, q0, WINDOW + Q_BLOCK, axis=1)
        w_pos = q0 - WINDOW + jnp.arange(WINDOW + Q_BLOCK)
        dist_w = t[:, None] - w_pos[None, :]
        mask_w = (dist_w >= 0) & (dist_w < WINDOW) & (w_pos[None, :] >= 0)
        s = jnp.einsum('bqhgd,bkhd->bhgqk', qb, kwb) * scale - slopes * dist_w
        p_w = masked_softmax(s, mask_w)
        o_w = jnp.einsum('bhgqk,bkhd->bqhgd', p_w, vwb.astype(jnp.float32))

        gb = lax.dynamic_slice_in_dim(gates, q0, Q_BLOCK, axis=1)
        o = gb[..., 0:1] * o_c + gb[..., 1:2] * o_s + gb[..., 2:3] * o_w
        return o.astype(x.dtype)

    outs = lax.map(q_block, jnp.arange(T // Q_BLOCK))
    o = jnp.moveaxis(outs, 0, 1).reshape(B, T, C)
    return o @ w_out

def setup_inputs(seed: int = 0) -> dict:
    key = jax.random.key(seed)
    keys = iter(jax.random.split(key, 64))
    f32 = jnp.float32
    D = D_MODEL
    NA, NB, NV = N_RWKV, N_NSA, N_VRES

    def nrm(shape, scale):
        return scale * jax.random.normal(next(keys), shape, f32)

    def unif(shape, lo, hi):
        return jax.random.uniform(next(keys), shape, f32, lo, hi)

    return {
        "x": nrm((BATCH, SEQ, D), 1.0),
        "mix_norm": 1.0 + nrm((DEPTH, D), 0.05),
        "mlp_norm": 1.0 + nrm((DEPTH, D), 0.05),
        "mlp_w1": nrm((DEPTH, D, MLP_HIDDEN), D ** -0.5),
        "mlp_w2": nrm((DEPTH, MLP_HIDDEN, D), 0.5 * MLP_HIDDEN ** -0.5),
        "rwkv_mu": unif((NA, 6, D), 0.0, 1.0),
        "rwkv_w_in": nrm((NA, D, 3 * D), D ** -0.5),
        "rwkv_w0": unif((NA, D), -6.5, -1.5),
        "rwkv_w1": nrm((NA, D, LORA_DECAY), D ** -0.5),
        "rwkv_w2": nrm((NA, LORA_DECAY, D), 0.1 * LORA_DECAY ** -0.5),
        "rwkv_a0": nrm((NA, D), 0.1),
        "rwkv_a1": nrm((NA, D, LORA_ICLR), D ** -0.5),
        "rwkv_a2": nrm((NA, LORA_ICLR, D), 0.5 * LORA_ICLR ** -0.5),
        "rwkv_v0": 1.0 + nrm((NV, D), 0.1),
        "rwkv_v1": nrm((NV, D, LORA_VRES), D ** -0.5),
        "rwkv_v2": nrm((NV, LORA_VRES, D), 0.5 * LORA_VRES ** -0.5),
        "rwkv_g1": nrm((NA, D, LORA_GATE), D ** -0.5),
        "rwkv_g2": nrm((NA, LORA_GATE, D), LORA_GATE ** -0.5),
        "rwkv_k_k": 0.85 + nrm((NA, D), 0.02),
        "rwkv_k_a": 1.0 + nrm((NA, D), 0.02),
        "rwkv_r_k": nrm((NA, RWKV_HEADS, RWKV_HEAD_DIM), 0.1),
        "rwkv_ln_w": 1.0 + nrm((NA, D), 0.05),
        "rwkv_ln_b": nrm((NA, D), 0.02),
        "rwkv_w_out": nrm((NA, D, D), 0.5 * D ** -0.5),
        "nsa_w_in": nrm((NB, D, NSA_IN_COLS), D ** -0.5),
        "nsa_cmp_pe": nrm((NB, 2, CMP_BLOCK, NSA_HEAD_DIM), 0.1),
        "nsa_cmp_w1": nrm((NB, 2, CMP_BLOCK * NSA_HEAD_DIM, CMP_HIDDEN), (CMP_BLOCK * NSA_HEAD_DIM) ** -0.5),
        "nsa_cmp_w2": nrm((NB, 2, CMP_HIDDEN, NSA_HEAD_DIM), CMP_HIDDEN ** -0.5),
        "nsa_q_norm": 1.0 + nrm((NB, NSA_HEAD_DIM), 0.05),
        "nsa_k_norm": 1.0 + nrm((NB, 3, NSA_HEAD_DIM), 0.05),
        "nsa_w_out": nrm((NB, D, D), 0.5 * D ** -0.5),
    }

def reference(x, mix_norm, mlp_norm, mlp_w1, mlp_w2,
              rwkv_mu, rwkv_w_in, rwkv_w0, rwkv_w1, rwkv_w2, rwkv_a0, rwkv_a1, rwkv_a2,
              rwkv_v0, rwkv_v1, rwkv_v2, rwkv_g1, rwkv_g2, rwkv_k_k, rwkv_k_a, rwkv_r_k,
              rwkv_ln_w, rwkv_ln_b, rwkv_w_out,
              nsa_w_in, nsa_cmp_pe, nsa_cmp_w1, nsa_cmp_w2, nsa_q_norm, nsa_k_norm, nsa_w_out):
    h = x
    v_first = None
    for i in range(DEPTH):
        xn = rms_norm(h, mix_norm[i])
        j = i // N_MIXERS
        if i % N_MIXERS == 0:
            vres = None if j == 0 else (rwkv_v0[j - 1], rwkv_v1[j - 1], rwkv_v2[j - 1])
            y, v_raw = rwkv7_time_mix(xn, rwkv_mu[j], rwkv_w_in[j], rwkv_w0[j], rwkv_w1[j], rwkv_w2[j],
                                      rwkv_a0[j], rwkv_a1[j], rwkv_a2[j], rwkv_g1[j], rwkv_g2[j],
                                      rwkv_k_k[j], rwkv_k_a[j], rwkv_r_k[j], rwkv_ln_w[j], rwkv_ln_b[j],
                                      rwkv_w_out[j], v_first, vres)
            if j == 0:
                v_first = v_raw
        else:
            y = nsa_mix(xn, nsa_w_in[j], nsa_cmp_pe[j], nsa_cmp_w1[j], nsa_cmp_w2[j],
                        nsa_q_norm[j], nsa_k_norm[j], nsa_w_out[j])
        h = h + y
        h = h + squared_relu_mlp(rms_norm(h, mlp_norm[i]), mlp_w1[i], mlp_w2[i])
    return h


_drawn_inputs = setup_inputs


def setup_inputs(seed=0):
    import zlib

    import numpy as np

    out = dict(_drawn_inputs(seed))
    spreads = {}
    factors = {'rwkv_w1': 8.0,
     'rwkv_w2': 8.0,
     'rwkv_a0': 5.087,
     'rwkv_k_k': 8.0,
     'rwkv_k_a': 8.0,
     'rwkv_ln_w': 3.803,
     'rwkv_ln_b': 8.0,
     'nsa_cmp_pe': 4.23,
     'nsa_q_norm': 8.0,
     'nsa_k_norm': 8.0}
    for name, (base, spread) in spreads.items():
        noise = np.random.default_rng([zlib.crc32(name.encode()), seed]).standard_normal(out[name].shape)
        drawn = base * np.exp(spread * noise) if base else spread * noise
        out[name] = jnp.asarray(drawn.astype(out[name].dtype))
    for name, factor in factors.items():
        out[name] = (out[name] * factor).astype(out[name].dtype)
    return out
```

```python
import math
from contextlib import ExitStack

import concourse.bass as bass
import numpy as np
from concourse import mybir

P = 128
D = 1024
T = 256
FT = D // P
TT = T // P
HID = 4 * D
HT = HID // P
HD = 64
H = D // HD
C = 64
NCH = T // C
SUB = 16
LD, LI, LG = 64, 64, 160
HKV = 4
GRP = H // HKV
CB, CS = 32, 16
NB = T // CS - 1
NQ, NKV = D, HKV * HD
NG = 3 * H
EPS, GN_EPS = 1e-6, 64e-5
DECAY = math.exp(-0.5)
GELU_A, GELU_B = 2 * math.sqrt(2 / math.pi), 0.044715
FAR = 1e30
FLOOR = -1e25
SLOPES = [2.0 ** (-8.0 * (h + 1) / H) for h in range(H)]

UE = 1024
RING = 4
GW = 256


def constants():
    i = np.arange(P)
    s = (i % C)[:, None]
    t = np.arange(C)[None, :]
    same = (s // SUB) == (t // SUB)
    tt = np.arange(C)[None, :]
    cols = {
        "ident": np.eye(P),
        "mean": np.full((P, P), 1.0 / D),
        "pair": (i[:, None] // HD) == (i[None, :] // HD),
        "gmask": np.concatenate([s < tt, s <= tt], 1),
        "dmask": (s < t) & same,
        "emask": (s < t) & ~same,
        "ldmask": (s > t) & same,
        "etmask": (s > t) & ~same,
        "eye64": s == t,
        "chunk": np.broadcast_to(np.arange(T)[None, :] % C != 0, (P, T)),
    }
    dist = []
    for q in range(TT):
        d = (q * P + i)[:, None] - np.arange((q + 1) * P)[None, :]
        dist.append(np.where(d >= 0, d, FAR))
    cols["dist"] = np.concatenate(dist, 1)
    end = np.arange(16) * CS + CB - 1
    adc = np.empty((P, TT, H, 16))
    for q in range(TT):
        d = (q * P + i)[:, None] - end[None, :]
        d = np.where((d >= 0) & (np.arange(16) < NB)[None, :], d, FAR)
        for h in range(H):
            adc[:, q, h] = -SLOPES[h] * d
    cols["adc"] = adc.reshape(P, -1)
    at, off = {}, 0
    for n, v in cols.items():
        at[n] = (off, v.shape[1])
        off += v.shape[1]
    return np.concatenate([np.asarray(v, np.float32) for v in cols.values()], 1), at


CONST_AT = {}
CONST_N = 0
_o = 0
for _n, _w in (("ident", P), ("mean", P), ("pair", P), ("gmask", 2 * C), ("dmask", C), ("emask", C),
               ("ldmask", C), ("etmask", C), ("eye64", C), ("chunk", T),
               ("dist", P * TT * (TT + 1) // 2), ("adc", TT * H * 16)):
    CONST_AT[_n] = (_o, _w)
    _o += _w
CONST_N = _o


def rwkv_nsa_trunk(nc, t, out):
    f32, r32 = mybir.dt.float32, mybir.dt.float32r
    ALU = mybir.AluOpType
    ACT = mybir.ActivationFunctionType
    AXX = mybir.AxisListType.X
    ds = bass.ds
    ctx = ExitStack()

    base = [(nc.sbuf_base + 63) // 64 * 64]

    def place(name, shape, off=None, dt=f32):
        size = 4 * int(np.prod(shape[1:]))
        if off is None:
            off = base[0]
            base[0] = (off + size + 63) // 64 * 64
        return nc.alloc_sbuf_tensor_at(name, shape, dt, offset=off)

    h = place("h", [P, FT, T])
    raw = place("raw", [P, RING, UE])
    whi = place("whi", [P, RING, UE], dt=r32)
    wlo = place("wlo", [P, RING, UE], dt=r32)
    cst = place("cst", [P, CONST_N])
    par = place("par", [P, 144])
    tiny = place("tiny", [P, 8])
    rs = place("rs", [P, T])
    ri = place("ri", [P, T])
    BLK = 4 * FT * T
    blk = base[0]
    off = lambda n, b=0: blk + n * BLK + b
    misc = blk + 16 * BLK
    A0, B0 = 12, 14
    xh = [place(f"xh{n}", [P, FT, T], off(12 + 2 * n), r32) for n in range(2)]
    xl = [place(f"xl{n}", [P, FT, T], off(13 + 2 * n), r32) for n in range(2)]

    xtok = place("xtok", [P, TT, D], off(1))
    prow = place("prow", [P, 2, P], off(2))
    sq = place("sq", [P, FT, T], off(0))
    xn = place("xn", [P, FT, T], off(11))
    dx = place("dx", [P, FT, T], off(1))
    mix = [place(f"mix{n}", [P, FT, T], off(2 + n)) for n in range(2)]
    R, K, V = (place(n, [P, FT, T], off(4 + i)) for i, n in enumerate("RKV"))
    lw = LD + LI + LG
    ldown = place("ldown", [P, FT, lw], off(7))
    lup_w = place("lup_w", [LD, D], off(7, 4 * FT * lw))
    lup_a = place("lup_a", [LI, D], off(7, 4 * FT * lw + 4 * D))
    lup_g0 = place("lup_g0", [P, D], off(7, 4 * FT * lw + 8 * D))
    lup_g1 = place("lup_g1", [LG - P, D], off(7, 4 * FT * lw + 12 * D))
    hw = place("hw", [LD, T], off(10, 2048))
    ha = place("ha", [LI, T], off(10, 2048 + 1024))
    hg0 = place("hg0", [P, T], off(10, 2048 + 2048))
    hg1 = place("hg1", [LG - P, T], off(10, 2048 + 3072))
    Sg = place("Sg", [P, FT, T], off(0))
    Ai = place("Ai", [P, FT, T], off(1))
    Gt = place("Gt", [P, FT, T], off(2))
    KK = place("KK", [P, FT, T], off(3))
    t11 = place("t11", [P, FT, T], off(11))
    CSm = place("CSm", [P, FT, T], off(14))
    sq2 = place("sq2", [P, FT, T], off(14))
    rn = place("rn", [P, FT, T], off(15))
    E1 = place("E1", [P, FT, T], off(12))
    E2 = place("E2", [P, FT, T], off(13))
    E3 = place("E3", [P, FT, T], off(15))
    AR = place("AR", [P, FT, NCH, 2, C], off(7))
    BK = place("BK", [P, FT, NCH, 2, C], off(9))
    UV = place("UV", [P, NCH, D], off(4))
    BKT = place("BKT", [P, NCH, D], off(0))
    Gs = place("Gs", [P, FT, NCH, 2 * C], off(14))
    NP_ = FT // 2 * NCH
    DPa = place("DPa", [P, NP_, 2, C], off(12))
    DPb = place("DPb", [P, NP_, 2, C], off(13))
    La = place("La", [P, NP_, C], off(3))
    Lb = place("Lb", [P, NP_, C], off(3, BLK // 2))
    Em = place("Em", [P, NP_, C], off(6))
    Et = place("Et", [P, NP_, C], off(6, BLK // 2))
    PC = place("PC", [P, FT, NCH], misc)
    XS = place("XS", [P, FT // 2, C], misc + 256)
    ST = place("ST", [P, FT // 2, C], misc + 256 + 1024)
    STt = place("STt", [P, FT // 2, C], misc + 256 + 2048)
    YC = place("YC", [P, FT, T], off(0))
    YQ = place("YQ", [P, FT, T], off(1))
    YR = place("YR", [P, FT, T], off(3))

    hh = place("hh", [P, HT, T], off(0), r32)
    hl = place("hl", [P, HT, T], off(4), r32)
    rl = place("rl", [P, 2, 2, T], off(8))
    s2 = place("s2", [P, 2, 2, T], off(8, 4096))
    cw1 = place("cw1", [P, 2, CB // 2, P], off(9))
    cw2 = place("cw2", [P, 2, 2, HD], off(14))
    gw = place("gw", [P, FT, NG], off(14, 1024))
    perow = place("perow", [2 * CB, 2, HD], off(14, 2560))
    pec = place("pec", [P, 2 * CB], off(14, 3072))
    Qn = place("Qn", [P, FT, T], off(1))
    kv = place("kv", [P, 4, 2, T], off(2))
    vt = place("vt", [P, 2, TT, NKV], off(3))
    gat = place("gat", [P, TT, NG], off(3, 4096))
    kcm = place("kcm", [P, HKV * NB], off(3, 4608))
    hid = place("hid", [P, 2, HKV * NB], off(3, 4864))
    gu = place("gu", [P, 2, HKV * NB], off(3, 5376))
    hpad = place("hpad", [P, HKV, 4, 32], off(3, 5888))
    kd = place("kd", [P, 2, HKV, T], off(4))
    Zc = place("Zc", [P, 2, CB // 2, HKV * NB], off(5))
    ksq = place("ksq", [P, 2, 2, T], off(6))
    krs = place("krs", [P, 2, 2, T], off(6, 4096))
    vblk = place("vblk", [P, HKV, 4 * HD], off(7))
    Sc = place("Sc", [P, TT, H, 32], off(8))
    PcT = place("PcT", [P, TT, HKV, P], off(8, 4096))
    csm = place("csm", [P, 4, TT, H], off(7, 4096))
    SB = place("SB", [P, 2, 4, T], off(0))
    PT = place("PT", [P, 2, 4, TT, P], off(5))
    qss = place("qss", [P, FT, T], off(0))
    qrs = place("qrs", [P, FT, T], off(15))
    nmx = place("nmx", [P, 2, 4], off(7, 5120))
    den = place("den", [P, TT, 2, H], off(7, 5376))
    cof = place("cof", [P, TT, 2, H], off(7, 5888))
    Ot = place("Ot", [P, TT, D], off(9))
    o1 = place("o1", [P, 2, GW], off(6, 0))
    otok = place("otok", [P, TT, D], off(9))

    ps = ctx.enter_context(nc.psum_tensor("ps", [P, 8, 512], f32))

    def cc(name, p0=0, p1=P):
        o, w = CONST_AT[name]
        return cst[p0:p1, o:o + w]

    names = ["mix0", "mix1", "mlp0", "mlp1", "mu0", "mu1", "mu2", "mu3", "mu4", "mu5", "w0", "a0",
             "k_k", "k_a", "r_k", "ln_w", "ln_b"]
    pcol = {n: FT * i for i, n in enumerate(names)}
    for i, n in enumerate(["qn", "kn0", "kn1", "kn2"]):
        pcol[n] = FT * len(names) + i
    NPAR = FT * len(names) + 4

    def pv(name, k=0):
        return par[:, pcol[name] + k:pcol[name] + k + 1]

    def kview(w):
        return w.rearrange("(k p) n -> p k n", p=P)

    w_in, w_o = kview(t["rwkv_w_in"][0]), kview(t["rwkv_w_out"][0])
    n_in, n_o = kview(t["nsa_w_in"][0]), kview(t["nsa_w_out"][0])
    m1 = [kview(t["mlp_w1"][i]) for i in range(2)]
    m2 = [kview(t["mlp_w2"][i]) for i in range(2)]
    UNITS = [("r", 8), ("k", 8), ("v", 8), ("o0", 8), ("a1", 32), ("a2", 32), ("q", 8), ("kv", 12),
             ("o1", 8), ("b1", 32), ("b2", 32)]
    U0, n = {}, 0
    for name, cnt in UNITS:
        U0[name] = n
        n += cnt
    NU = n
    GROUPS = [("x", 4, "act"), ("r", 4, "act"), ("k", 4, "act"), ("v", 4, "act"), ("up", 12, "act"),
              ("o0", 4, "dve"), ("a1", 16, "act"), ("a2", 4, "dve"), ("q", 4, "act"), ("kv", 6, "act"),
              ("o1", 4, "dve"), ("b1", 16, "act"), ("b2", 4, "dve")]
    G0, EV0, n, ev = {}, {}, 0, {"act": 0, "dve": 0}
    for name, cnt, who in GROUPS:
        G0[name], EV0[name] = n, ev[who]
        n += cnt
        ev[who] += cnt

    sems = {}

    def sem(name):
        if name not in sems:
            sems[name] = ctx.enter_context(nc.semaphore(name))
        return sems[name]

    with ctx:
        raw_in = [sem(f"raw_in{s}") for s in range(RING)]
        hi_ready = sem("hi_ready")
        lo_ready = sem("lo_ready")
        unit_used = sem("unit_used")
        ev_act = sem("ev_act")
        ev_dve = sem("ev_dve")
        block = ctx.enter_context(nc.Block())

        @block.sync
        def _(sp):
            sp.dma_start(xtok[:, :, :], t["x"][0].rearrange("(a p) n -> p a n", p=P)).then_inc(sem("x_in"), 16)
            sp.dma_start(cst[:, :], t["consts"]).then_inc(sem("cst_in"), 16)

            def rows(v, n):
                return v.rearrange("(k p) -> k p", p=P) if n else v

            def load(u, src):
                s = u % RING if isinstance(u, int) else None
                dst = raw[:, s, :].rearrange("p (k n) -> p k n", n=GW)
                if u >= RING:
                    sp.wait_ge(lo_ready, u - RING + 1)
                sp.dma_start(dst, src).then_inc(raw_in[s], 16)

            def pairs(name, view, col0, lo, hi):
                for j in range(lo, hi):
                    c0 = col0 + (j // 2) * GW
                    load(U0[name] + j, view[:, 4 * (j % 2):4 * (j % 2) + 4, c0:c0 + GW])

            pr = sem("par_in")
            for i, n in enumerate(["mix_norm", "mlp_norm"]):
                sp.dma_start(prow[16 * i:16 * i + 16, 0, :], t[n].rearrange("a (k p) -> (a k) p", p=P)).then_inc(pr, 16)
            sp.dma_start(prow[32:80, 0, :], t["rwkv_mu"][0].rearrange("a (k p) -> (a k) p", p=P)).then_inc(pr, 16)
            for i, n in enumerate(["rwkv_w0", "rwkv_a0", "rwkv_k_k", "rwkv_k_a"]):
                sp.dma_start(prow[80 + 8 * i:88 + 8 * i, 0, :], t[n][0].rearrange("(k p) -> k p", p=P)).then_inc(pr, 16)
            sp.dma_start(prow[112:120, 0, :], t["rwkv_r_k"][0].rearrange("(k a) n -> k (a n)", a=2)).then_inc(pr, 16)
            sp.dma_start(prow[120:128, 0, :], t["rwkv_ln_w"][0].rearrange("(k p) -> k p", p=P)).then_inc(pr, 16)
            sp.dma_start(prow[0:8, 1, :], t["rwkv_ln_b"][0].rearrange("(k p) -> k p", p=P)).then_inc(pr, 16)
            for a in range(2):
                sp.dma_start(prow[8:9, 1, a * HD:(a + 1) * HD], t["nsa_q_norm"]).then_inc(pr, 16)
                sp.dma_start(prow[9:12, 1, a * HD:(a + 1) * HD], t["nsa_k_norm"][0]).then_inc(pr, 16)
            lo = sem("lora_in")
            sp.dma_start(ldown[:, :, 0:LD], kview(t["rwkv_w1"][0])).then_inc(lo, 16)
            pairs("r", w_in, 0, 0, 4)
            sp.dma_start(ldown[:, :, LD:LD + LI], kview(t["rwkv_a1"][0])).then_inc(lo, 16)
            sp.dma_start(ldown[:, :, LD + LI:lw], kview(t["rwkv_g1"][0])).then_inc(lo, 16)
            sp.dma_start(lup_w[:, :], t["rwkv_w2"][0]).then_inc(lo, 16)
            sp.dma_start(lup_a[:, :], t["rwkv_a2"][0]).then_inc(lo, 16)
            sp.dma_start(lup_g0[:, :], t["rwkv_g2"][0][0:P, :]).then_inc(lo, 16)
            sp.dma_start(lup_g1[:, :], t["rwkv_g2"][0][P:LG, :]).then_inc(lo, 16)
            pairs("r", w_in, 0, 4, 8)
            pairs("k", w_in, D, 0, 8)
            pairs("v", w_in, 2 * D, 0, 8)
            pairs("o0", w_o, 0, 0, 8)

            def mlp_loads(n1, n2, v1, v2):
                pairs(n1, v1, 0, 0, 4)
                if n1 == "a1":
                    sp.wait_ge(ev_dve, EV0["o0"] + 4)
                    cs = sem("cmp_in")
                    for a in range(2):
                        src = t["nsa_cmp_w1"][0].rearrange("b (a l d) m -> a d b l m", a=2, l=CB // 2)[a]
                        for b in range(2):
                            sp.dma_start(cw1[64 * a:64 * a + 64, b, :, :], src[:, b, :, :]).then_inc(cs, 16)
                        sp.dma_start(cw2[:, :, a, :], t["nsa_cmp_w2"][0].rearrange("b m d -> m b d")).then_inc(cs, 16)
                        sp.dma_start(perow[:, a, :], t["nsa_cmp_pe"][0].rearrange("b l d -> (b l) d")).then_inc(cs, 16)
                    sp.dma_start(gw[:, :, :], n_in[:, :, NQ + 6 * NKV:]).then_inc(cs, 16)
                with sp.Fori(1, 8) as i:
                    for j in range(4):
                        sp.wait_ge(lo_ready, i * 4 + (U0[n1] + j - RING + 1))
                        sp.dma_start(raw[:, j, :].rearrange("p (k n) -> p k n", n=GW),
                                     v1[:, 4 * (j % 2):4 * (j % 2) + 4, ds(i * (2 * GW) + (j // 2) * GW, GW)])\
                          .then_inc(raw_in[j], 16)
                with sp.Fori(0, 4) as i:
                    for j in range(8):
                        sp.wait_ge(lo_ready, i * 8 + (U0[n2] + j - RING + 1))
                        sp.dma_start(raw[:, j % RING, :].rearrange("p (k n) -> p k n", n=GW),
                                     v2[:, 4 * j:4 * j + 4, ds(i * GW, GW)]).then_inc(raw_in[j % RING], 16)

            mlp_loads("a1", "a2", m1[0], m2[0])
            pairs("q", n_in, 0, 0, 8)
            pairs("kv", n_in, NQ, 0, 12)
            pairs("o1", n_o, 0, 0, 8)
            mlp_loads("b1", "b2", m1[1], m2[1])
            for q in range(TT):
                sp.wait_ge(sem("out_ready"), q + 1)
                sp.dma_start(out[0, q * P:(q + 1) * P, :], otok[:, q, :]).then_inc(sem("stored"), 16)
            sp.wait_ge(sem("stored"), 16 * TT)

        @block.tensor
        def _(pe):
            mm = nc.tensor.matmul

            def group_free(name, g):
                if EV0[name] + g - 1 > 0:
                    pe.wait_ge(ev_act if who[name] == "act" else ev_dve, EV0[name] + g - 1)

            who = {n: w for n, _, w in GROUPS}

            def unit_mm(slot, bank0, kbase, ktiles, hi, lo):
                for k in range(4):
                    kk = kbase + k
                    for m in range(2):
                        o = ps[:, bank0 + m, 0:T]
                        c0 = k * GW + m * P
                        wh, wl = whi[:, slot, c0:c0 + P], wlo[:, slot, c0:c0 + P]
                        mm(o, wh, hi[:, kk, :], start=(kk == 0), stop=False)
                        mm(o, wh, lo[:, kk, :], start=False, stop=False)
                        last = mm(o, wl, hi[:, kk, :], start=False, stop=(kk == ktiles - 1))
                return last

            def linear8(name, hi, lo, before_first=None):
                for g in range(4):
                    group_free(name, g)
                    for j in range(2):
                        u = U0[name] + 2 * g + j
                        pe.wait_ge(lo_ready, u + 1)
                        last = unit_mm(u % RING, 2 * (g % 2), 4 * j, FT, hi, lo)
                        last.then_inc(unit_used, 1)

            pe.wait_ge(sem("cst_in"), 16)
            pe.wait_ge(sem("x_in"), 16)
            for g in range(4):
                if g >= 2:
                    pe.wait_ge(ev_act, g - 1)
                for m in range(2):
                    for q in range(TT):
                        last = nc.tensor.transpose(ps[:, 2 * (g % 2) + m, q * P:(q + 1) * P],
                                                   xtok[:, q, (2 * g + m) * P:(2 * g + m + 1) * P], cc("ident"))
                last.then_inc(sem("x_pe0"), 1)
            pe.wait_ge(sem("par_in"), 16 * 14)
            nc.tensor.transpose(ps[:, 5, 0:P], prow[:, 0, :], cc("ident"))
            nc.tensor.transpose(ps[:, 5, P:P + 12], prow[0:12, 1, :], cst[0:12, 0:12]).then_inc(sem("par_t"), 1)

            def norm_pe(i):
                for k in range(FT):
                    if k % 4 == 0:
                        pe.wait_ge(sem("sq_ready"), 2 * i + 1 + k // 4)
                    last = mm(ps[:, 4, 0:T], cc("mean"), sq[:, k, :], start=(k == 0), stop=(k == FT - 1))
                last.then_inc(sem("ms_ready"), 1)

            norm_pe(0)

            def lora_down(n, src, c0, width, bank):
                for k in range(FT):
                    last = mm(ps[0:width, bank, 0:T], ldown[:, k, c0:c0 + width], src[:, k, :],
                              start=(k == 0), stop=(k == FT - 1))
                return last

            pe.wait_ge(sem("lora_in"), 16 * 7)
            pe.wait_ge(sem("mix_ready"), 1)
            lora_down("w", mix[0], 0, LD, 5).then_inc(sem("lora_h"), 1)
            pe.wait_ge(sem("xh_ready"), 1)
            pe.wait_ge(sem("xl_ready"), 1)
            linear8("r", xh[0], xl[0])
            pe.wait_ge(sem("mix_ready"), 3)
            lora_down("a", mix[0], LD, LI, 6).then_inc(sem("lora_h"), 1)
            pe.wait_ge(sem("xh_ready"), 2)
            pe.wait_ge(sem("xl_ready"), 2)
            linear8("k", xh[1], xl[1])
            pe.wait_ge(sem("mix_ready"), 5)
            lora_down("g", mix[0], LD + LI, P, 7)
            lora_down("g", mix[0], LD + LI + P, LG - P, 4).then_inc(sem("lora_h"), 1)
            pe.wait_ge(sem("xh_ready"), 3)
            pe.wait_ge(sem("xl_ready"), 3)
            linear8("v", xh[0], xl[0])
            ups = [(1, [(lup_w, hw)]), (2, [(lup_a, ha)]), (3, [(lup_g0, hg0), (lup_g1, hg1)])]
            for n, (need, parts) in enumerate(ups):
                pe.wait_ge(sem("lora_act"), need)
                for g in range(4):
                    pe.wait_ge(ev_act, EV0["up"] + 4 * n + g - 1)
                    for m in range(2):
                        c0 = (2 * g + m) * P
                        for i, (w, x) in enumerate(parts):
                            last = mm(ps[:, 2 * (g % 2) + m, 0:T], w[:, c0:c0 + P], x[:, :],
                                      start=(i == 0), stop=(i == len(parts) - 1))
                    last.then_inc(sem("up_pe"), 1)

            for n, (src, name) in enumerate([(sq2, "kksq"), (t11, "rk")]):
                pe.wait_ge(sem(name), 1)
                if n:
                    pe.wait_ge(sem("kkn"), 1)
                for j in range(4):
                    last = mm(ps[:, 4 + j, :], cc("pair"), src[:, 2 * j:2 * j + 2, :], start=True, stop=True)
                last.then_inc(sem("pair_sum"), 1)

            pe.wait_ge(ev_act, EV0["up"] + 12)
            for q in range(TT):
                for k in range(FT):
                    last = nc.tensor.transpose(ps[:, 2 * q + k // 4, (k % 4) * P:(k % 4 + 1) * P],
                                               V[:, k, q * P:(q + 1) * P], cc("ident"))
                last.then_inc(sem("vT"), 1)
            pe.wait_ge(sem("bk_ready"), 2)
            for c in range(NCH):
                if c < 2:
                    pe.wait_ge(sem("v_copied"), 2 * (c + 1))
                else:
                    pe.wait_ge(sem("bonus"), 1)
                for k in range(FT):
                    last = nc.tensor.transpose(ps[:, 2 * c + k // 4, (k % 4) * P:(k % 4 + 1) * P],
                                               BK[:, k, c, :, :], cc("ident"))
                last.then_inc(sem("bkT"), 1)

            pe.wait_ge(sem("ar_ready"), 2)
            for half in range(2):
                k0 = half * FT // 2
                for c_ in range(8):
                    kk_, e = c_ // 2, c_ % 2
                    k = k0 + kk_
                    if half == 0 and c_ % 2 == 0:
                        pe.wait_ge(sem("bkt_copied"), c_ // 2 + 1)
                    if half == 1 and c_ == 0:
                        pe.wait_ge(sem("y_copied"), NCH)
                        pe.wait_ge(sem("st_ready"), NCH - 1)
                    q = slice(HD * e, HD * e + HD)
                    for c in range(NCH):
                        last = mm(ps[:, c_, c * P:(c + 1) * P], BK[q, k, c, :, :], AR[q, k, c, :, :],
                                  start=True, stop=True)
                    last.then_inc(sem("g_done"), 1)

                def each(fn):
                    for i in range(NP_ // 2):
                        fn(i, 0)
                        fn(i + NP_ // 2, 1)
                    for i in range(NP_ // 2):
                        fn(i, 1)
                        last = fn(i + NP_ // 2, 0)
                    return last

                def at(e):
                    return slice(HD * e, HD * e + HD)

                def o1b(bank0):
                    return lambda p, e: ps[at(e), bank0 + p // 8, (p % 8) * C:(p % 8 + 1) * C]

                def o2b(bank0):
                    return lambda p, e: ps[at(e), bank0 + p // 4, (p % 4) * 2 * C:(p % 4 + 1) * 2 * C]

                def prod(o, lhs, rhs):
                    return each(lambda p, e: mm(o(p, e), lhs(p, e), rhs(p, e), start=True, stop=True))

                pe.wait_ge(sem("g_masked"), 8 * half + 8)
                prod(o1b(0), lambda p, e: BK[at(e), k0 + p // NCH, p % NCH, 0, :],
                     lambda p, e: AR[at(e), k0 + p // NCH, p % NCH, 0, :])
                prod(o1b(2), lambda p, e: AR[at(e), k0 + p // NCH, p % NCH, 0, :],
                     lambda p, e: BK[at(e), k0 + p // NCH, p % NCH, 0, :]).then_inc(sem("inv_pe"), 1)
                A_ = lambda p, e: DPa[at(e), p, 0, :]
                Ap = lambda p, e: DPa[at(e), p, :, :]
                AP_ = lambda p, e: DPa[at(e), p, 1, :]
                B_ = lambda p, e: DPb[at(e), p, 0, :]
                Bp = lambda p, e: DPb[at(e), p, :, :]
                BP_ = lambda p, e: DPb[at(e), p, 1, :]
                LA = lambda p, e: La[at(e), p, :]
                LB = lambda p, e: Lb[at(e), p, :]
                EE = lambda p, e: Em[at(e), p, :]
                ET = lambda p, e: Et[at(e), p, :]
                id64 = lambda p, e: cc("eye64", HD * e, HD * e + HD)
                steps = [
                    [(o1b(4), LA, A_), (o1b(6), A_, LA)],
                    [(o2b(0), LB, Bp), (o1b(4), B_, LB)],
                    [(o2b(0), LA, Ap), (o1b(6), A_, LA)],
                    [(o1b(4), LB, BP_)],
                    [(o1b(0), ET, AP_), (o1b(2), AP_, ET), (o1b(6), AP_, id64)],
                    [(o1b(4), LA, B_)],
                    [(o1b(0), LA, BP_)],
                    [(o1b(4), LB, A_)],
                ]
                for n, step in enumerate(steps):
                    pe.wait_ge(sem("inv_dve"), 9 * half + n + 1)
                    if n in (1, 2, 3, 5):
                        pe.wait_ge(sem("inv_act"), 4 * half + {1: 1, 2: 2, 3: 3, 5: 4}[n])
                    for o, lhs, rhs in step:
                        last = prod(o, lhs, rhs)
                    last.then_inc(sem("inv_pe"), 1)

                pe.wait_ge(sem("inv_dve"), 9 * half + 9)
                for c in range(NCH):
                    n = half * NCH + c
                    if n == 0:
                        pe.wait_ge(sem("u_zero"), 1)
                    if c:
                        pe.wait_ge(sem("st_ready"), half * (NCH - 1) + c)
                    for kk_ in range(FT // 2):
                        for e in range(2):
                            k, hd = k0 + kk_, 2 * (k0 + kk_) + e
                            o = ps[at(e), e, kk_ * C:(kk_ + 1) * C]
                            last = mm(o, Gs[:, 2 * kk_ + e, c, 0:C], UV[:, c, hd * HD:(hd + 1) * HD],
                                      start=True, stop=(c == 0))
                            if c:
                                last = mm(o, AR[at(e), k, c, 0, :], ST[at(e), kk_, :], start=False, stop=True)
                    last.then_inc(sem("x_pe"), 1)
                    pe.wait_ge(sem("x_sb"), n + 1)
                    for kk_ in range(FT // 2):
                        for e in range(2):
                            last = mm(ps[0:HD, 2 + e, kk_ * C:(kk_ + 1) * C], Em[at(e), kk_ * NCH + c, :],
                                      XS[at(e), kk_, :], start=True, stop=True)
                    last.then_inc(sem("u_pe"), 1)
                    pe.wait_ge(sem("u_sb"), n + 1)
                    if c < NCH - 1:
                        for kk_ in range(FT // 2):
                            for e in range(2):
                                hd = 2 * (k0 + kk_) + e
                                cols = slice(hd * HD, (hd + 1) * HD)
                                last = mm(ps[at(e), 4, kk_ * C:(kk_ + 1) * C], BKT[:, c, cols], UV[:, c, cols],
                                          start=True, stop=True)
                        last.then_inc(sem("s_pe"), 1)
                    if n >= 2:
                        pe.wait_ge(sem("y_copied"), n - 1)
                    for kk_ in range(FT // 2):
                        for e in range(2):
                            k, hd = k0 + kk_, 2 * (k0 + kk_) + e
                            o = ps[at(e), 6 + c % 2, kk_ * C:(kk_ + 1) * C]
                            last = mm(o, UV[:, c, hd * HD:(hd + 1) * HD], Gs[:, 2 * kk_ + e, c, C:2 * C],
                                      start=True, stop=(c == 0))
                            if c:
                                last = mm(o, ST[at(e), kk_, :], AR[at(e), k, c, 1, :], start=False, stop=True)
                    last.then_inc(sem("y_pe"), 1)

            pe.wait_ge(sem("y_copied"), 2 * NCH)
            for j in range(4):
                last = mm(ps[:, j, :], cc("pair"), AR[:, 2 * j:2 * j + 2, :, 1, :], start=True, stop=True)
            last.then_inc(sem("gn_pe"), 1)
            pe.wait_ge(sem("yq"), 1)
            for j in range(4):
                last = mm(ps[:, 4 + j, :], cc("pair"), YQ[:, 2 * j:2 * j + 2, :], start=True, stop=True)
            last.then_inc(sem("gn_pe"), 1)
            pe.wait_ge(sem("xh_ready"), 4)
            pe.wait_ge(sem("xl_ready"), 4)
            linear8("o0", xh[0], xl[0])

            def mlp_pe(n1, n2, hi, lo):
                with pe.Fori(0, 8) as i:
                    for g in range(2):
                        pe.wait_ge(ev_act, i * 2 + (EV0[n1] + g - 1))
                        for j in range(2):
                            pe.wait_ge(lo_ready, i * 4 + (U0[n1] + 2 * g + j + 1))
                            unit_mm(2 * g + j, 2 * g, 4 * j, FT, hi, lo).then_inc(unit_used, 1)
                pe.wait_ge(sem("hid_ready"), 16 if n1 == "a1" else 32)
                with pe.Fori(0, 2) as i:
                    for g in range(2):
                        pe.wait_ge(ev_dve, i * 2 + (EV0[n2] + g - 1))
                        for j in range(8):
                            pe.wait_ge(lo_ready, i * 16 + (U0[n2] + 8 * g + j + 1))
                            unit_mm(j % RING, 2 * g, 4 * j, HT, hh, hl).then_inc(unit_used, 1)

            norm_pe(1)
            pe.wait_ge(sem("xh_ready"), 5)
            pe.wait_ge(sem("xl_ready"), 5)
            mlp_pe("a1", "a2", xh[0], xl[0])

            norm_pe(2)
            pe.wait_ge(sem("xh_ready"), 6)
            pe.wait_ge(sem("xl_ready"), 6)
            linear8("q", xh[0], xl[0])
            for g, tok in enumerate([0, 0, 0, 1, 0, 1]):
                pe.wait_ge(ev_act, EV0["kv"] + g - 1)
                for j in range(2):
                    u = U0["kv"] + 2 * g + j
                    pe.wait_ge(lo_ready, u + 1)
                    if not tok:
                        last = unit_mm(u % RING, 2 * (g % 2), 4 * j, FT, xh[0], xl[0])
                    else:
                        for k in range(4):
                            kk_ = 4 * j + k
                            for q in range(TT):
                                o = ps[:, 2 * (g % 2) + q, 0:GW]
                                tq = slice(q * P, (q + 1) * P)
                                wh = whi[:, u % RING, k * GW:(k + 1) * GW]
                                wl = wlo[:, u % RING, k * GW:(k + 1) * GW]
                                mm(o, xh[0][:, kk_, tq], wh, start=(kk_ == 0), stop=False)
                                mm(o, xh[0][:, kk_, tq], wl, start=False, stop=False)
                                last = mm(o, xl[0][:, kk_, tq], wh, start=False, stop=(kk_ == FT - 1))
                    last.then_inc(unit_used, 1)
            pe.wait_ge(sem("cmp_in"), 16 * 9)
            for q in range(TT):
                for k in range(FT):
                    mm(ps[:, 4, q * 64:q * 64 + NG], xn[:, k, q * P:(q + 1) * P], gw[:, k, :],
                       start=(k == 0), stop=(k == FT - 1))
            nc.tensor.transpose(ps[:, 5, 0:2 * CB], perow[:, :, :], cst[0:2 * CB, 0:2 * CB]).then_inc(sem("gate_pe"), 1)
            pe.wait_ge(sem("qsq"), 1)
            pe.wait_ge(ev_act, EV0["kv"] + 6)
            for j, bank in enumerate([6, 7, 0, 1]):
                last = mm(ps[:, bank, :], cc("pair"), qss[:, 2 * j:2 * j + 2, :], start=True, stop=True)
            last.then_inc(sem("qn_pe"), 1)
            pe.wait_ge(sem("ksq_r"), 1)
            for a in range(2):
                last = mm(ps[:, 2 + a, :], cc("pair"), ksq[:, a, :, :], start=True, stop=True)
            last.then_inc(sem("kn_pe"), 1)
            pe.wait_ge(sem("zc"), 1)
            pe.wait_ge(sem("gates_r"), 1)
            for b in range(2):
                for l in range(CB // 2):
                    last = mm(ps[:, 4, b * 64:b * 64 + HKV * NB], cw1[:, b, l, :], Zc[:, b, l, :],
                              start=(l == 0), stop=(l == CB // 2 - 1))
            last.then_inc(sem("cmp_pe"), 1)
            pe.wait_ge(sem("hid_k"), 1)
            mm(ps[:, 5, 0:HKV * NB], cw2[:, 0, :, :], hid[:, 0, :], start=True, stop=True)
            for j in range(HKV):
                last = mm(ps[:, 5, 128 + j * HD:128 + (j + 1) * HD], hpad[:, j, :, :], cw2[:, 1, 0, :],
                          start=True, stop=True)
            last.then_inc(sem("cmp2_pe"), 1)
            pe.wait_ge(sem("kcsq"), 1)
            mm(ps[:, 4, 0:HKV * NB], cc("pair"), gu[:, 0, :], start=True, stop=True).then_inc(sem("kc_pe"), 1)
            pe.wait_ge(sem("kcm_r"), 1)
            pe.wait_ge(sem("q_ready"), 1)
            for q in range(TT):
                b0 = [6, 0][q]
                for k in range(FT):
                    for e in range(2):
                        qe = slice(HD * e, HD * e + HD)
                        j = (2 * k + e) // GRP
                        last = mm(ps[:, b0 + e, k * 16:k * 16 + NB], Qn[qe, k, q * P:(q + 1) * P],
                                  kcm[qe, j * NB:(j + 1) * NB], start=True, stop=True)
                last.then_inc(sem("sc_pe"), 1)
            pe.wait_ge(sem("pc_ready"), 1)
            for q in range(TT):
                for j in range(HKV):
                    last = nc.tensor.transpose(ps[:, 4 + q, j * P:(j + 1) * P], Sc[:, q, 4 * j:4 * j + 4, :], cc("ident"))
            last.then_inc(sem("pct_pe"), 1)

            items = [(j, q, b) for j in range(HKV) for q in range(TT) for b in range(2)]
            pe.wait_ge(sem("kd_ready"), 1)
            pe.wait_ge(sem("pct_r"), 1)

            def scores(n):
                j, q, b = items[n]
                if n >= 2:
                    pe.wait_ge(sem("s_read"), n - 1)
                w = (q + 1) * P
                for i in range(2):
                    for e in range(2):
                        k = 2 * j + i
                        qe = slice(HD * e, HD * e + HD)
                        last = mm(ps[:, 2 * (n % 2) + e, i * T:i * T + w], Qn[qe, k, q * P:(q + 1) * P],
                                  kd[qe, b, j, 0:w], start=True, stop=True)
                last.then_inc(sem("s_pe2"), 1)

            def transposes(n):
                j, q, b = items[n]
                pe.wait_ge(sem("p_ready"), n + 1)
                if n >= 1:
                    pe.wait_ge(sem("pt_read"), n)
                for s in range(q + 1):
                    for i in range(4):
                        last = nc.tensor.transpose(ps[:, 4 + s, i * P:(i + 1) * P],
                                                   SB[:, n % 2, i, s * P:(s + 1) * P], cc("ident"))
                last.then_inc(sem("t_pe"), 1)

            def weighted(n):
                j, q, b = items[n]
                pe.wait_ge(sem("pt_read"), n + 1)
                g = n // 2
                if b == 0 and g >= 2:
                    pe.wait_ge(sem("o_done"), g - 1)
                for i in range(4):
                    for s in range(q + 1):
                        last = mm(ps[:, 6 + g % 2, b * GW + i * HD:b * GW + (i + 1) * HD],
                                  PT[:, n % 2, i, s, :], vt[:, b, s, j * HD:(j + 1) * HD],
                                  start=(s == 0), stop=(s == q))
                last.then_inc(sem("pv_pe"), 1)

            scores(0)
            for n in range(len(items)):
                if n + 1 < len(items):
                    scores(n + 1)
                transposes(n)
                if n >= 1:
                    weighted(n - 1)
            weighted(len(items) - 1)
            pe.wait_ge(sem("s_read"), len(items))
            for q in range(TT):
                for j in range(HKV):
                    last = mm(ps[:, 2 * q + j // 2, (j % 2) * GW:(j % 2 + 1) * GW], PcT[:, q, j, :], vblk[:, j, :],
                              start=True, stop=True)
            last.then_inc(sem("oc_pe"), 1)
            pe.wait_ge(sem("ot_ready"), 1)
            pe.wait_ge(sem("pt_read"), len(items))
            for k in range(FT):
                for q in range(TT):
                    last = nc.tensor.transpose(ps[:, 4 + k // 2, (k % 2) * T + q * P:(k % 2) * T + (q + 1) * P],
                                               Ot[:, q, k * P:(k + 1) * P], cc("ident"))
            last.then_inc(sem("oT_pe"), 1)
            pe.wait_ge(sem("xh_ready"), 7)
            pe.wait_ge(sem("xl_ready"), 7)
            linear8("o1", xh[1], xl[1])

            norm_pe(3)
            pe.wait_ge(sem("xh_ready"), 8)
            pe.wait_ge(sem("xl_ready"), 8)
            mlp_pe("b1", "b2", xh[0], xl[0])
            for q in range(TT):
                for k in range(FT):
                    if q == 0 and k % 2 == 0:
                        pe.wait_ge(ev_dve, EV0["b2"] + k // 2 + 1)
                    last = nc.tensor.transpose(ps[:, 4 + 2 * q + k // 4, (k % 4) * P:(k % 4 + 1) * P],
                                               h[:, k, q * P:(q + 1) * P], cc("ident"))
                last.then_inc(sem("fin_pe"), 1)

        @block.scalar
        def _(act):
            A = nc.scalar.activation
            aown = sem("act_step")
            cnt = [0]

            def step(ins):
                cnt[0] += 1
                ins.then_inc(aown, 1)

            def settle():
                act.wait_ge(aown, cnt[0])

            def split(u):
                s = u % RING
                act.wait_ge(raw_in[s], 16 * (u // RING + 1))
                if u >= RING:
                    act.wait_ge(unit_used, u - RING + 1)
                A(whi[:, s, :], raw[:, s, :], ACT.Copy).then_inc(hi_ready, 1)

            def ahead(u):
                if u + RING < NU:
                    split(u + RING)

            def evac8(name, dst):
                for g in range(4):
                    act.wait_ge(unit_used, U0[name] + 2 * g + 2)
                    A(dst[:, 2 * g:2 * g + 2, :], ps[:, 2 * (g % 2):2 * (g % 2) + 2, 0:T], ACT.Copy).then_inc(ev_act, 1)
                    ahead(U0[name] + 2 * g)
                    ahead(U0[name] + 2 * g + 1)

            for g in range(4):
                act.wait_ge(sem("x_pe0"), g + 1)
                A(h[:, 2 * g:2 * g + 2, :], ps[:, 2 * (g % 2):2 * (g % 2) + 2, 0:T], ACT.Copy).then_inc(ev_act, 1)

            def norm_act(i):
                for m in range(2):
                    if i == 0:
                        act.wait_ge(ev_act, 2 * m + 2)
                    else:
                        act.wait_ge(ev_dve, 4 * (i - 1) + 2 * m + 2)
                    A(sq[:, 4 * m:4 * m + 4, :], h[:, 4 * m:4 * m + 4, :], ACT.Square).then_inc(sem("sq_ready"), 1)
                act.wait_ge(sem("ms_ready"), i + 1)
                act.wait_ge(sem("eps_set"), 2)
                if i:
                    act.wait_ge(sem("xn_done"), i)
                A(rs[:, :], ps[:, 4, 0:T], ACT.Sqrt, bias=tiny[:, 0:1]).then_inc(sem("rs_ready"), 1)

            norm_act(0)
            for u in range(RING):
                split(u)
            for n, m in enumerate([1, 1]):
                act.wait_ge(sem("mix_ready"), [2, 4][n])
                A(xh[n][:, :, :], mix[m][:, :, :], ACT.Copy).then_inc(sem("xh_ready"), 1)
            evac8("r", R)
            act.wait_ge(sem("mix_ready"), 6)
            act.wait_ge(unit_used, U0["r"] + 8)
            A(xh[0][:, :, :], mix[1][:, :, :], ACT.Copy).then_inc(sem("xh_ready"), 1)
            act.wait_ge(sem("lora_h"), 1)
            A(hw[:, :], ps[0:LD, 5, 0:T], ACT.Tanh).then_inc(sem("lora_act"), 1)
            act.wait_ge(sem("lora_h"), 2)
            A(ha[:, :], ps[0:LI, 6, 0:T], ACT.Copy).then_inc(sem("lora_act"), 1)
            evac8("k", K)
            act.wait_ge(sem("lora_h"), 3)
            step(A(hg0[:, :], ps[:, 7, 0:T], ACT.Sigmoid))
            settle()
            A(hg1[:, :], ps[0:LG - P, 4, 0:T], ACT.Sigmoid).then_inc(sem("lora_act"), 1)
            evac8("v", V)
            for n, (dst, bias) in enumerate([(Sg, "w0"), (Ai, "a0"), (Gt, None)]):
                for g in range(4):
                    act.wait_ge(sem("up_pe"), 4 * n + g + 1)
                    if bias is None:
                        A(dst[:, 2 * g:2 * g + 2, :], ps[:, 2 * (g % 2):2 * (g % 2) + 2, 0:T], ACT.Copy).then_inc(ev_act, 1)
                        continue
                    step(A(dst[:, 2 * g, :], ps[:, 2 * (g % 2), 0:T], ACT.Sigmoid, bias=pv(bias, 2 * g)))
                    settle()
                    A(dst[:, 2 * g + 1, :], ps[:, 2 * (g % 2) + 1, 0:T], ACT.Sigmoid, bias=pv(bias, 2 * g + 1))\
                        .then_inc(ev_act, 1)
            act.wait_ge(sem("kk_raw"), 1)
            A(sq2[:, :, :], KK[:, :, :], ACT.Square).then_inc(sem("kksq"), 1)
            act.wait_ge(sem("pair_sum"), 1)
            A(rn[:, :, :].rearrange("p (b k) t -> p b (k t)", b=4), ps[:, 4:8, :], ACT.Sqrt).then_inc(sem("kkn"), 1)
            act.wait_ge(sem("cs_ready"), 1)
            act.wait_ge(sem("kkn_used"), 1)
            A(E1[:, :, :], CSm[:, :, :], ACT.Exp, scale=-DECAY).then_inc(sem("e_ready"), 1)
            A(E2[:, :, :], CSm[:, :, :], ACT.Exp, scale=DECAY).then_inc(sem("e_ready"), 1)
            act.wait_ge(sem("ex_ready"), 1)
            A(E3[:, :, :], Sg[:, :, :], ACT.Exp, scale=-DECAY).then_inc(sem("e_ready"), 1)
            act.wait_ge(sem("rk_done"), 1)
            for q in range(TT):
                act.wait_ge(sem("vT"), q + 1)
                for c in range(2):
                    A(UV[HD:P, 2 * q + c, :].rearrange("p (b n) -> p b n", b=2), ps[HD * c:HD * c + HD, 2 * q:2 * q + 2, :],
                      ACT.Copy).then_inc(sem("v_copied"), 1)
            act.wait_ge(sem("ar_ready"), 2)
            act.wait_ge(sem("bk_ready"), 2)
            act.wait_ge(sem("e_ready"), 3)
            for c in range(NCH):
                act.wait_ge(sem("bkT"), c + 1)
                A(BKT[:, c, :].rearrange("p (b n) -> p b n", b=2), ps[:, 2 * c:2 * c + 2, :], ACT.Copy)\
                    .then_inc(sem("bkt_copied"), 1)
            for half in range(2):
                inv_pe, inv_act = sem("inv_pe"), sem("inv_act")

                def two(o, bank0):
                    return A(o, ps[:, bank0:bank0 + 2, :].rearrange("p b (k n) -> p (b k) n", n=C), ACT.Copy)

                act.wait_ge(inv_pe, 9 * half + 2)
                two(Lb[:, :, :], 6).then_inc(inv_act, 1)
                act.wait_ge(inv_pe, 9 * half + 3)
                two(La[:, :, :], 4).then_inc(inv_act, 1)
                act.wait_ge(inv_pe, 9 * half + 4)
                two(Lb[:, :, :], 6).then_inc(inv_act, 1)
                act.wait_ge(inv_pe, 9 * half + 6)
                step(two(Lb[:, :, :], 6))
                settle()
                two(La[:, :, :], 2).then_inc(inv_act, 1)
                for c in range(NCH):
                    n = half * NCH + c
                    act.wait_ge(sem("x_pe"), n + 1)
                    for e in range(2):
                        step(A(XS[HD * e:HD * e + HD, :, :], ps[HD * e:HD * e + HD, e, 0:GW].rearrange("p (k n) -> p k n", n=C),
                               ACT.Copy))
                        settle()
                    act.sem_inc(sem("x_sb"), 1)
                    act.wait_ge(sem("u_pe"), n + 1)
                    for e in range(2):
                        o = UV[0:HD, c, half * 512:half * 512 + 512].rearrange("p (k a n) -> p k a n", a=2, n=HD)[:, :, e, :]
                        step(A(o, ps[0:HD, 2 + e, 0:GW].rearrange("p (k n) -> p k n", n=C), ACT.Copy))
                        settle()
                    act.sem_inc(sem("u_sb"), 1)
                    act.wait_ge(sem("y_pe"), n + 1)
                    A(AR[:, half * 4:half * 4 + 4, c, 1, :], ps[:, 6 + c % 2, 0:GW].rearrange("p (k n) -> p k n", n=C), ACT.Copy)\
                        .then_inc(sem("y_copied"), 1)
            act.wait_ge(sem("yc"), 1)
            A(YQ[:, :, :], YC[:, :, :], ACT.Square).then_inc(sem("yq"), 1)
            act.wait_ge(sem("gn_pe"), 2)
            A(YR[:, :, :].rearrange("p (b k) t -> p b (k t)", b=4), ps[:, 4:8, :], ACT.Sqrt, bias=tiny[:, 1:2], scale=1.0 / HD)\
                .then_inc(sem("yr"), 1)
            act.wait_ge(sem("ynorm"), 1)
            for k in range(FT):
                A(YQ[:, k, :], YC[:, k, :], ACT.Identity, bias=pv("ln_b", k), scale=pv("ln_w", k)).then_inc(sem("yaff"), 1)
            act.wait_ge(sem("yfin"), 1)
            A(xh[0][:, :, :], YC[:, :, :], ACT.Copy).then_inc(sem("xh_ready"), 1)
            for j in range(8):
                ahead(U0["o0"] + j)

            def x_parts(n):
                for m in range(2):
                    act.wait_ge(sem("xn_ready"), 2 * n + m + 1)
                    o = A(xh[0][:, 4 * m:4 * m + 4, :], xn[:, 4 * m:4 * m + 4, :], ACT.Copy)
                    step(o)
                settle()
                act.sem_inc(sem("xh_ready"), 1)

            def mlp_act(n1, n2, base_):
                def turn(i, gg, steady):
                    act.wait_ge(unit_used, i * 4 + (U0[n1] + 2 * gg + 2))
                    if steady:
                        act.wait_ge(sem("sq_used"), i * 2 + (base_ + gg - 1))
                    A(rl[:, gg, :, :], ps[:, 2 * gg:2 * gg + 2, 0:T], ACT.Relu).then_inc(ev_act, 1)
                    for j in range(2):
                        u = U0[n1] + 2 * gg + j + RING
                        act.wait_ge(raw_in[2 * gg + j], i * 16 + 16 * (u // RING + 1))
                        act.wait_ge(unit_used, i * 4 + (u - RING + 1))
                        A(whi[:, 2 * gg + j, :], raw[:, 2 * gg + j, :], ACT.Copy).then_inc(hi_ready, 1)
                    act.wait_ge(ev_act, i * 2 + (EV0[n1] + gg + 1))
                    A(hh[:, ds(i * 4 + 2 * gg, 2), :], rl[:, gg, :, :], ACT.Square).then_inc(sem("hh_ready"), 1)

                for gg in range(2):
                    turn(0, gg, False)
                with act.Fori(1, 8) as i:
                    for gg in range(2):
                        turn(i, gg, True)
                with act.Fori(0, 3) as i:
                    for j in range(8):
                        u = U0[n2] + j + RING
                        act.wait_ge(raw_in[j % RING], i * 32 + 16 * (u // RING + 1))
                        act.wait_ge(unit_used, i * 8 + (u - RING + 1))
                        A(whi[:, j % RING, :], raw[:, j % RING, :], ACT.Copy).then_inc(hi_ready, 1)
                for j in range(24, 32):
                    ahead(U0[n2] + j)

            norm_act(1)
            x_parts(0)
            mlp_act("a1", "a2", 0)
            norm_act(2)
            x_parts(1)
            evac8("q", Qn)
            act.wait_ge(ev_act, EV0["q"] + 4)
            A(qss[:, :, :], Qn[:, :, :], ACT.Square).then_inc(sem("qsq"), 1)
            dst = [kv[:, 0, :, :], kv[:, 1, :, :], kv[:, 2, :, :], vt[:, 0, :, :], kv[:, 3, :, :], vt[:, 1, :, :]]
            for g in range(6):
                act.wait_ge(unit_used, U0["kv"] + 2 * g + 2)
                A(dst[g], ps[:, 2 * (g % 2):2 * (g % 2) + 2, 0:T], ACT.Copy).then_inc(ev_act, 1)
                ahead(U0["kv"] + 2 * g)
                ahead(U0["kv"] + 2 * g + 1)
            act.wait_ge(ev_act, EV0["kv"] + 6)
            A(ksq[:, :, :, :], kv[:, 2:4, :, :], ACT.Square).then_inc(sem("ksq_r"), 1)
            act.wait_ge(sem("gate_pe"), 1)
            A(gat[:, :, :], ps[:, 4, 0:128].rearrange("p (q n) -> p q n", q=TT)[:, :, 0:NG], ACT.Sigmoid)\
                .then_inc(sem("gates_r"), 1)
            act.wait_ge(sem("pe_col"), 1)
            act.wait_ge(sem("qn_pe"), 1)
            step(A(qrs[:, 0:4, :].rearrange("p (b k) t -> p b (k t)", b=2), ps[:, 6:8, :], ACT.Sqrt, bias=tiny[:, 0:1], scale=1.0 / HD))
            A(qrs[:, 4:8, :].rearrange("p (b k) t -> p b (k t)", b=2), ps[:, 0:2, :], ACT.Sqrt, bias=tiny[:, 0:1], scale=1.0 / HD)\
                .then_inc(sem("qrs_r"), 1)
            act.wait_ge(sem("kn_pe"), 1)
            A(krs[:, :, :, :].rearrange("p b k t -> p b (k t)"), ps[:, 2:4, :], ACT.Sqrt, bias=tiny[:, 0:1], scale=1.0 / HD)\
                .then_inc(sem("krs_r"), 1)
            act.wait_ge(sem("gelu_in"), 1)
            A(gu[:, :, :], gu[:, :, :], ACT.Sigmoid, scale=GELU_A).then_inc(sem("gelu_sig"), 1)
            act.wait_ge(sem("cmp2_pe"), 1)
            act.wait_ge(sem("hid_k"), 1)
            A(gu[:, 0, :], ps[:, 5, 0:HKV * NB], ACT.Square).then_inc(sem("kcsq"), 1)
            for a in range(4):
                o = vblk[32 * a:32 * a + 32, :, a * HD:(a + 1) * HD]
                if a == 0:
                    act.wait_ge(sem("vblk_0"), 1)
                i_ = ps[32 * a:32 * a + 32, 5, 128:128 + HKV * HD].rearrange("p (j n) -> p j n", n=HD)
                A(o, i_, ACT.Copy).then_inc(sem("vblk_r"), 1)
            act.wait_ge(sem("kc_pe"), 1)
            A(gu[:, 1, :], ps[:, 4, 0:HKV * NB], ACT.Sqrt, bias=tiny[:, 0:1], scale=1.0 / HD).then_inc(sem("kcrs"), 1)
            act.wait_ge(sem("csub"), 1)
            A(Sc[:, :, :, 0:16], Sc[:, :, :, 0:16], ACT.Exp).then_inc(sem("cexp"), 1)
            act.wait_ge(sem("pct_pe"), 1)
            A(PcT[:, :, :, :].rearrange("p q j n -> p q (j n)"), ps[:, 4:6, :], ACT.Copy).then_inc(sem("pct_r"), 1)
            items = [(j, q, b) for j in range(HKV) for q in range(TT) for b in range(2)]

            def exps(n):
                j, q, b = items[n]
                w = (q + 1) * P
                act.wait_ge(sem("mx_ready"), n + 1)
                for i in range(4):
                    hd = 4 * j + i
                    o = A(SB[:, n % 2, i, 0:w], SB[:, n % 2, i, 0:w], ACT.Exp, bias=nmx[:, n % 2, i:i + 1],
                          accum_out=den[:, q, b, hd:hd + 1])
                    step(o)
                settle()
                act.sem_inc(sem("p_ready"), 1)

            def pt_copy(n):
                j, q, b = items[n]
                act.wait_ge(sem("t_pe"), n + 1)
                if n >= 2:
                    act.wait_ge(sem("pv_pe"), n - 1)
                A(PT[:, n % 2, :, 0:q + 1, :].rearrange("p i s t -> p s i t"),
                  ps[:, 4:5 + q, :].rearrange("p s (i t) -> p s i t", t=P), ACT.Copy).then_inc(sem("pt_read"), 1)

            for n in range(len(items)):
                exps(n)
                if n >= 1:
                    pt_copy(n - 1)
            pt_copy(len(items) - 1)
            act.wait_ge(sem("oT_pe"), 1)
            A(xh[1][:, :, :].rearrange("p (b k) t -> p b (k t)", b=4), ps[:, 4:8, :], ACT.Copy).then_inc(sem("xh_ready"), 1)
            for j in range(8):
                ahead(U0["o1"] + j)
            norm_act(3)
            x_parts(2)
            mlp_act("b1", "b2", 16)
            for q in range(TT):
                act.wait_ge(sem("fin_pe"), q + 1)
                A(otok[:, q, :].rearrange("p (b n) -> p b n", b=2), ps[:, 4 + 2 * q:6 + 2 * q, :], ACT.Copy)\
                    .then_inc(sem("out_ready"), 1)

        @block.vector
        def _(dve):
            v = nc.vector
            down = sem("dve_step")
            cnt = [0]

            def step(ins):
                cnt[0] += 1
                ins.then_inc(down, 1)

            def settle():
                dve.wait_ge(down, cnt[0])

            def rest(slot, hi_count):
                dve.wait_ge(hi_ready, hi_count)
                v.tensor_tensor(wlo[:, slot, :], raw[:, slot, :], whi[:, slot, :].bitcast(f32), ALU.subtract)\
                    .then_inc(lo_ready, 1)

            def ahead(u):
                if u + RING < NU:
                    rest((u + RING) % RING, u + RING + 1)

            v.memset(tiny[:, 0:1], EPS).then_inc(sem("eps_set"), 1)
            v.memset(tiny[:, 1:2], GN_EPS).then_inc(sem("eps_set"), 1)
            dve.wait_ge(sem("par_t"), 1)
            v.tensor_copy(par[:, 0:NPAR], ps[:, 5, 0:NPAR]).then_inc(sem("par_r"), 1)
            dve.wait_ge(sem("par_r"), 1)

            def norm_dve(i, g):
                if i == 0:
                    dve.wait_ge(ev_act, 4)
                dve.wait_ge(sem("rs_ready"), i + 1)
                step(v.reciprocal(ri[:, :], rs[:, :]))
                settle()
                for k in range(FT):
                    step(v.scalar_tensor_tensor(xn[:, k, :], h[:, k, :], pv(g, k), ri[:, :], ALU.mult, ALU.mult))
                    if k % 4 == 3:
                        settle()
                        if i:
                            dve.sem_inc(sem("xn_ready"), 1)
                dve.sem_inc(sem("xn_done"), 1)

            norm_dve(0, "mix0")
            for u in range(RING):
                rest(u, u + 1)
            step(v.tensor_tensor(dx[:, :, 1:T], xn[:, :, 0:T - 1], xn[:, :, 1:T], ALU.subtract))
            step(v.tensor_scalar(dx[:, :, 0:1], xn[:, :, 0:1], -1.0, None, ALU.mult))
            settle()

            def mixing(mu, dst):
                for k in range(FT):
                    step(v.scalar_tensor_tensor(dst[:, k, :], dx[:, k, :], pv(f"mu{mu}", k), xn[:, k, :], ALU.mult, ALU.add))
                settle()
                dve.sem_inc(sem("mix_ready"), 1)

            mixing(1, mix[0])
            mixing(0, mix[1])
            dve.wait_ge(sem("lora_h"), 1)
            mixing(4, mix[0])
            dve.wait_ge(sem("xh_ready"), 1)
            dve.wait_ge(sem("xl_ready"), 1)
            mixing(2, mix[1])
            for j in range(8):
                ahead(U0["r"] + j)
            dve.wait_ge(sem("lora_h"), 2)
            mixing(5, mix[0])
            dve.wait_ge(sem("xh_ready"), 2)
            dve.wait_ge(sem("xl_ready"), 2)
            mixing(3, mix[1])
            for j in range(8):
                ahead(U0["k"] + j)
            for j in range(8):
                ahead(U0["v"] + j)
            dve.wait_ge(sem("xh_ready"), 3)
            dve.wait_ge(sem("xl_ready"), 3)
            dve.wait_ge(ev_act, EV0["k"] + 4)
            for k in range(FT):
                step(v.tensor_scalar(KK[:, k, :], K[:, k, :], pv("k_k", k), None, ALU.mult))
            settle()
            dve.sem_inc(sem("kk_raw"), 1)
            dve.wait_ge(ev_act, EV0["up"] + 8)
            for k in range(FT):
                step(v.tensor_scalar(t11[:, k, :], Ai[:, k, :], 1.0, pv("k_a", k), ALU.subtract, ALU.mult))
            settle()
            step(v.scalar_tensor_tensor(K[:, :, :], t11[:, :, :], 1.0, K[:, :, :], ALU.add, ALU.mult))
            settle()
            dve.wait_ge(sem("kkn"), 1)
            step(v.tensor_scalar(rn[:, :, :], rn[:, :, :], 1e-12, None, ALU.max))
            settle()
            step(v.reciprocal(rn[:, :, :], rn[:, :, :]))
            settle()
            v.tensor_tensor(KK[:, :, :], KK[:, :, :], rn[:, :, :], ALU.mult).then_inc(sem("kkn_used"), 1)
            dve.wait_ge(sem("kkn_used"), 1)
            for k in range(FT):
                step(v.scalar_tensor_tensor(t11[:, k, :], R[:, k, :], pv("r_k", k), K[:, k, :], ALU.mult, ALU.mult))
            settle()
            dve.sem_inc(sem("rk"), 1)
            for k in range(FT):
                step(v.tensor_tensor_scan(CSm[:, k, :], cc("chunk"), Sg[:, k, :], 0.0, ALU.mult, ALU.add))
            settle()
            dve.sem_inc(sem("cs_ready"), 1)
            dve.wait_ge(sem("pair_sum"), 2)
            v.tensor_tensor(t11[:, :, :].rearrange("p (b k) t -> p b (k t)", b=4), ps[:, 4:8, :],
                            V[:, :, :].rearrange("p (b k) t -> p b (k t)", b=4), ALU.mult).then_inc(sem("bonus"), 1)
            ch = lambda x: x[:, :, :].rearrange("p k (c n) -> p (k c) n", n=C)
            arv = lambda x, n: x[:, :, :, n, :].rearrange("p k c n -> p (k c) n")
            dve.wait_ge(ev_act, EV0["up"] + 12)
            dve.wait_ge(sem("e_ready"), 1)
            v.tensor_tensor(arv(AR, 1), ch(R), ch(E1), ALU.mult).then_inc(sem("rk_done0"), 1)
            dve.wait_ge(sem("e_ready"), 2)
            step(v.tensor_tensor(arv(BK, 1), ch(K), ch(E2), ALU.mult))
            step(v.tensor_copy(PC[:, :, :], E1[:, :, :].rearrange("p k (c n) -> p k c n", n=C)[:, :, :, C - 1]))
            settle()
            dve.wait_ge(sem("rk_done0"), 1)
            dve.sem_inc(sem("rk_done"), 1)
            dve.sem_inc(sem("bk_ready"), 1)
            dve.sem_inc(sem("ar_ready"), 1)
            dve.wait_ge(sem("e_ready"), 3)
            step(v.scalar_tensor_tensor(arv(AR, 0), ch(KK), -1.0, ch(E3), ALU.mult, ALU.mult))
            settle()
            dve.sem_inc(sem("ar_ready"), 1)

            for half in range(2):
                inv_pe, inv_dve = sem("inv_pe"), sem("inv_dve")
                for n in range(8):
                    dve.wait_ge(sem("g_done"), 8 * half + n + 1)
                    if n == 0 and half == 0:
                        dve.wait_ge(sem("bk_ready"), 2)
                        dve.wait_ge(sem("ar_ready"), 2)
                        dve.wait_ge(sem("e_ready"), 3)
                    v.tensor_tensor(Gs[:, n, :, :], ps[:, n, :].rearrange("p (c n) -> p c n", c=NCH),
                                    cc("gmask").unsqueeze(1).broadcast_to([P, NCH, 2 * C]), ALU.mult)\
                        .then_inc(sem("g_masked"), 1)

                def bank2(b0):
                    return ps[:, b0:b0 + 2, :].rearrange("p b (k n) -> p (b k) n", n=C)

                def bank4(b0, i):
                    return ps[:, b0:b0 + 4, :].rearrange("p b (k a n) -> p (b k) a n", a=2, n=C)[:, :, i, :]

                def m(name):
                    return cc(name).unsqueeze(1).broadcast_to([P, NP_, C])

                dve.wait_ge(inv_pe, 9 * half + 1)
                if half == 0:
                    dve.wait_ge(sem("v_copied"), 4)
                    dve.wait_ge(sem("b_used"), 1)
                step(v.tensor_tensor(DPa[:, :, 0, :], bank2(0), m("dmask"), ALU.mult))
                step(v.tensor_tensor(La[:, :, :], bank2(2), m("ldmask"), ALU.mult))
                settle()
                dve.sem_inc(inv_dve, 1)
                step(v.tensor_tensor(Em[:, :, :], bank2(0), m("emask"), ALU.mult))
                step(v.tensor_tensor(Et[:, :, :], bank2(2), m("etmask"), ALU.mult))
                step(v.tensor_tensor(DPb[:, :, 1, :], DPa[:, :, 0, :], m("eye64"), ALU.add))
                dve.wait_ge(inv_pe, 9 * half + 2)
                step(v.tensor_copy(DPb[:, :, 0, :], bank2(4)))
                settle()
                dve.sem_inc(inv_dve, 1)
                dve.wait_ge(inv_pe, 9 * half + 3)
                step(v.tensor_copy(DPa[:, :, 0, :], bank4(0, 0)))
                step(v.tensor_tensor(DPa[:, :, 1, :], bank4(0, 1), DPb[:, :, 1, :], ALU.add))
                settle()
                dve.sem_inc(inv_dve, 1)
                dve.wait_ge(inv_pe, 9 * half + 4)
                step(v.tensor_tensor(DPb[:, :, 1, :], bank4(0, 1), DPa[:, :, 1, :], ALU.add))
                settle()
                dve.sem_inc(inv_dve, 1)
                dve.wait_ge(inv_pe, 9 * half + 5)
                step(v.tensor_tensor(DPa[:, :, 1, :], bank2(4), DPb[:, :, 1, :], ALU.add))
                settle()
                dve.sem_inc(inv_dve, 1)
                dve.wait_ge(inv_pe, 9 * half + 6)
                step(v.tensor_copy(DPb[:, :, 0, :], bank2(0)))
                settle()
                dve.sem_inc(inv_dve, 1)
                dve.wait_ge(inv_pe, 9 * half + 7)
                step(v.tensor_tensor(DPb[:, :, 1, :], bank2(4), m("eye64"), ALU.add))
                settle()
                dve.sem_inc(inv_dve, 1)
                dve.wait_ge(inv_pe, 9 * half + 8)
                step(v.tensor_tensor(DPa[:, :, 0, :], bank2(0), DPb[:, :, 1, :], ALU.add))
                settle()
                dve.sem_inc(inv_dve, 1)
                dve.wait_ge(inv_pe, 9 * half + 9)
                step(v.tensor_copy(Em[:, :, :], bank2(4)))
                settle()
                dve.sem_inc(inv_dve, 1)
                for c in range(NCH - 1):
                    n = half * (NCH - 1) + c
                    dve.wait_ge(sem("s_pe"), n + 1)
                    s_in = ps[:, 4, 0:GW].rearrange("p (k n) -> p k n", n=C)
                    pc = PC[:, half * 4:half * 4 + 4, c:c + 1].broadcast_to([P, FT // 2, C])
                    if c:
                        step(v.tensor_tensor(STt[:, :, :], s_in, ST[:, :, :], ALU.add))
                        settle()
                        dve.wait_ge(sem("y_pe"), half * NCH + c + 1)
                        v.tensor_tensor(ST[:, :, :], STt[:, :, :], pc, ALU.mult).then_inc(sem("st_ready"), 1)
                    else:
                        v.tensor_tensor(ST[:, :, :], s_in, pc, ALU.mult).then_inc(sem("st_ready"), 1)
                    dve.wait_ge(sem("st_ready"), n + 1)
            dve.wait_ge(sem("gn_pe"), 1)
            for j in range(4):
                step(v.scalar_tensor_tensor(YC[:, 2 * j:2 * j + 2, :].rearrange("p k (c n) -> p (k c) n", n=C),
                                            ps[:, j, :].rearrange("p (k n) -> p k n", n=C), -1.0 / HD,
                                            AR[:, 2 * j:2 * j + 2, :, 1, :].rearrange("p k c n -> p (k c) n"),
                                            ALU.mult, ALU.add))
            settle()
            dve.sem_inc(sem("yc"), 1)
            dve.wait_ge(sem("yr"), 1)
            step(v.reciprocal(YR[:, :, :], YR[:, :, :]))
            settle()
            step(v.tensor_tensor(YC[:, :, :], YC[:, :, :], YR[:, :, :], ALU.mult))
            settle()
            dve.sem_inc(sem("ynorm"), 1)
            dve.wait_ge(sem("yaff"), FT)
            step(v.tensor_tensor(YR[:, :, :], YQ[:, :, :], t11[:, :, :], ALU.add))
            settle()
            v.tensor_tensor(YC[:, :, :], YR[:, :, :], Gt[:, :, :], ALU.mult).then_inc(sem("yfin"), 1)

            def residual(name):
                for g in range(4):
                    dve.wait_ge(unit_used, U0[name] + 2 * g + 2)
                    v.tensor_tensor(h[:, 2 * g:2 * g + 2, :], h[:, 2 * g:2 * g + 2, :],
                                    ps[:, 2 * (g % 2):2 * (g % 2) + 2, 0:T], ALU.add).then_inc(ev_dve, 1)
                    ahead(U0[name] + 2 * g)
                    ahead(U0[name] + 2 * g + 1)

            def mlp_dve(n1, n2, base_):
                def turn(i, gg, steady):
                    dve.wait_ge(ev_act, i * 2 + (EV0[n1] + gg + 1))
                    v.tensor_tensor(s2[:, gg, :, :], rl[:, gg, :, :], rl[:, gg, :, :], ALU.mult).then_inc(sem("s2_ready"), 1)
                    dve.wait_ge(sem("hh_ready"), i * 2 + (base_ + gg + 1))
                    dve.wait_ge(sem("s2_ready"), i * 2 + (base_ + gg + 1))
                    dve.sem_inc(sem("sq_used"), 1)
                    v.tensor_tensor(hl[:, ds(i * 4 + 2 * gg, 2), :], s2[:, gg, :, :],
                                    hh[:, ds(i * 4 + 2 * gg, 2), :].bitcast(f32), ALU.subtract).then_inc(sem("hid_ready"), 1)
                    for j in range(2):
                        u = U0[n1] + 2 * gg + j + RING
                        rest(2 * gg + j, i * 4 + (u + 1))

                with dve.Fori(0, 8) as i:
                    for gg in range(2):
                        turn(i, gg, True)
                for g in range(4):
                    for j in range(8):
                        ahead(U0[n2] + 8 * g + j)
                    dve.wait_ge(unit_used, U0[n2] + 8 * g + 8)
                    v.tensor_tensor(h[:, 2 * g:2 * g + 2, :], h[:, 2 * g:2 * g + 2, :],
                                    ps[:, 2 * (g % 2):2 * (g % 2) + 2, 0:T], ALU.add).then_inc(ev_dve, 1)

            residual("o0")
            norm_dve(1, "mlp0")
            mlp_dve("a1", "a2", 0)
            norm_dve(2, "mix1")

            for j in range(8):
                ahead(U0["q"] + j)
            for j in range(12):
                ahead(U0["kv"] + j)
            dve.wait_ge(sem("gate_pe"), 1)
            v.tensor_copy(pec[:, :], ps[:, 5, 0:2 * CB]).then_inc(sem("pe_col"), 1)
            dve.wait_ge(sem("pe_col"), 1)
            dve.wait_ge(ev_act, EV0["kv"] + 6)
            for b in range(2):
                for j in range(HKV):
                    e, m = j % 2, j // 2
                    for half in range(2):
                        src = kv[HD * e:HD * e + HD, b, m, CS * half:CS * half + CS * NB].rearrange("p (n l) -> p l n", l=CS)
                        emb = pec[HD * e:HD * e + HD, b * CB + CS * half:b * CB + CS * half + CS].unsqueeze(2)\
                            .broadcast_to([HD, CS, NB])
                        step(v.tensor_tensor(Zc[HD * half:HD * half + HD, b, :, j * NB:(j + 1) * NB], src, emb, ALU.add))
                        settle()
            dve.sem_inc(sem("zc"), 1)
            dve.wait_ge(sem("qrs_r"), 1)
            step(v.reciprocal(qrs[:, :, :], qrs[:, :, :]))
            settle()
            step(v.scalar_tensor_tensor(Qn[:, :, :], Qn[:, :, :], pv("qn"), qrs[:, :, :], ALU.mult, ALU.mult))
            settle()
            v.tensor_scalar(Qn[:, :, :], Qn[:, :, :], HD ** -0.5, None, ALU.mult).then_inc(sem("q_ready"), 1)
            dve.wait_ge(sem("cmp_pe"), 1)
            step(v.tensor_copy(hid[:, :, :], ps[:, 4, 0:128].rearrange("p (b n) -> p b n", b=2)[:, :, 0:HKV * NB]))
            settle()
            step(v.tensor_tensor(gu[:, :, :], hid[:, :, :], hid[:, :, :], ALU.mult))
            settle()
            step(v.tensor_scalar(gu[:, :, :], gu[:, :, :], GELU_B, 1.0, ALU.mult, ALU.add))
            settle()
            v.tensor_tensor(gu[:, :, :], gu[:, :, :], hid[:, :, :], ALU.mult).then_inc(sem("gelu_in"), 1)
            v.memset(hpad[:, :, :, :], 0.0).then_inc(sem("hpad_0"), 1)
            v.memset(vblk[:, :, :], 0.0).then_inc(sem("vblk_0"), 1)
            v.memset(Sc[:, :, :, :], 0.0).then_inc(sem("sc_0"), 1)
            dve.wait_ge(sem("gelu_sig"), 1)
            step(v.tensor_tensor(hid[:, :, :], hid[:, :, :], gu[:, :, :], ALU.mult))
            dve.wait_ge(sem("hpad_0"), 1)
            settle()
            step(v.tensor_copy(hpad[:, :, :, 0:NB], hid[:, 1, :].rearrange("p (j n) -> p j n", n=NB).unsqueeze(2)
                               .broadcast_to([P, HKV, 4, NB])))
            settle()
            dve.sem_inc(sem("hid_k"), 1)
            dve.wait_ge(sem("krs_r"), 1)
            step(v.reciprocal(krs[:, :, :, :], krs[:, :, :, :]))
            settle()
            for b in range(2):
                for j in range(HKV):
                    e, m = j % 2, j // 2
                    src = slice(HD * e, HD * e + HD)
                    for half in range(2):
                        g = par[src, pcol[f"kn{b + 1}"]:pcol[f"kn{b + 1}"] + 1]
                        step(v.scalar_tensor_tensor(kd[HD * half:HD * half + HD, b, j, :], kv[src, 2 + b, m, :], g,
                                                    krs[src, b, m, :], ALU.mult, ALU.mult))
                        settle()
            dve.sem_inc(sem("kd_ready"), 1)
            dve.wait_ge(sem("kcrs"), 1)
            step(v.reciprocal(gu[:, 1, :], gu[:, 1, :]))
            settle()
            v.scalar_tensor_tensor(kcm[:, :], ps[:, 5, 0:HKV * NB], pv("kn0"), gu[:, 1, :], ALU.mult, ALU.mult)\
                .then_inc(sem("kcm_r"), 1)
            dve.wait_ge(sem("sc_0"), 1)
            adc = cc("adc").rearrange("p (q h n) -> p q h n", q=TT, n=16)
            for q in range(TT):
                dve.wait_ge(sem("sc_pe"), q + 1)
                for e in range(2):
                    o = Sc[:, q, :, 0:16].rearrange("p (k a) n -> p k a n", a=2)[:, :, e, 0:NB]
                    a_ = adc[:, q, :, :].rearrange("p (k a) n -> p k a n", a=2)[:, :, e, 0:NB]
                    i_ = ps[:, [6, 0][q] + e, 0:FT * 16].rearrange("p (k n) -> p k n", n=16)[:, :, 0:NB]
                    step(v.tensor_tensor(o, i_, a_, ALU.add))
            settle()
            step(v.tensor_reduce(csm[:, 0, :, :], Sc[:, :, :, 0:NB], AXX, ALU.max))
            settle()
            step(v.tensor_scalar(csm[:, 0, :, :], csm[:, 0, :, :], FLOOR, None, ALU.max))
            settle()
            cb = lambda n: csm[:, n, :, :].unsqueeze(3).broadcast_to([P, TT, H, NB])
            v.tensor_tensor(Sc[:, :, :, 0:NB], Sc[:, :, :, 0:NB], cb(0), ALU.subtract).then_inc(sem("csub"), 1)
            dve.wait_ge(sem("cexp"), 1)
            step(v.tensor_reduce(csm[:, 1, :, :], Sc[:, :, :, 0:NB], AXX, ALU.add))
            settle()
            step(v.tensor_scalar(csm[:, 1, :, :], csm[:, 1, :, :], 1e-30, None, ALU.max))
            settle()
            step(v.reciprocal(csm[:, 2, :, :], csm[:, 1, :, :]))
            settle()
            gv = gat[:, :, :].rearrange("p q (h b) -> p q h b", b=3)
            dve.wait_ge(sem("gates_r"), 1)
            step(v.tensor_tensor(csm[:, 3, :, :], csm[:, 2, :, :], gv[:, :, :, 0], ALU.mult))
            settle()
            step(v.tensor_tensor(Sc[:, :, :, 0:NB], Sc[:, :, :, 0:NB], cb(3), ALU.mult))
            step(v.memset(Sc[:, :, :, NB:16], 0.0))
            settle()
            dve.sem_inc(sem("pc_ready"), 1)

            items = [(j, q, b) for j in range(HKV) for q in range(TT) for b in range(2)]
            dist = cc("dist")

            def soft(n):
                j, q, b = items[n]
                w = (q + 1) * P
                d = dist[:, 0:P] if q == 0 else dist[:, P:P + T]
                dve.wait_ge(sem("s_pe2"), n + 1)
                if n >= 2:
                    dve.wait_ge(sem("t_pe"), n - 1)
                for i in range(4):
                    step(v.scalar_tensor_tensor(SB[:, n % 2, i, 0:w], d, -SLOPES[4 * j + i],
                                                ps[:, 2 * (n % 2) + i % 2, (i // 2) * T:(i // 2) * T + w], ALU.mult, ALU.add))
                settle()
                dve.sem_inc(sem("s_read"), 1)
                step(v.tensor_reduce(nmx[:, n % 2, :], SB[:, n % 2, :, 0:w], AXX, ALU.max))
                settle()
                v.tensor_scalar(nmx[:, n % 2, :], nmx[:, n % 2, :], -1.0, None, ALU.mult).then_inc(sem("mx_ready"), 1)

            def combine(g):
                j, q = g // 2, g % 2
                hs = slice(4 * j, 4 * j + 4)
                dve.wait_ge(sem("p_ready"), 2 * g + 2)
                step(v.tensor_scalar(cof[:, q, :, hs], den[:, q, :, hs], 1e-30, None, ALU.max))
                settle()
                step(v.reciprocal(cof[:, q, :, hs], cof[:, q, :, hs]))
                settle()
                step(v.tensor_tensor(cof[:, q, :, hs], cof[:, q, :, hs],
                                     gv[:, q, hs, 1:3].rearrange("p h b -> p b h"), ALU.mult))
                settle()
                dve.wait_ge(sem("pv_pe"), 2 * g + 2)
                for b in range(2):
                    step(v.tensor_tensor(o1[:, b, :].rearrange("p (i n) -> p i n", n=HD),
                                         ps[:, 6 + g % 2, b * GW:(b + 1) * GW].rearrange("p (i n) -> p i n", n=HD),
                                         cof[:, q, b, hs].unsqueeze(2).broadcast_to([P, 4, HD]), ALU.mult))
                settle()
                dve.sem_inc(sem("o_done"), 1)
                step(v.tensor_tensor(Ot[:, q, j * GW:(j + 1) * GW], o1[:, 0, :], o1[:, 1, :], ALU.add))

            for n in range(len(items)):
                soft(n)
                if n >= 3 and n % 2 == 1:
                    combine((n - 3) // 2)
            combine(7)
            dve.wait_ge(sem("oc_pe"), 1)
            settle()
            v.tensor_tensor(Ot[:, :, :].rearrange("p q (b n) -> p (q b) n", b=2), ps[:, 0:4, :],
                            Ot[:, :, :].rearrange("p q (b n) -> p (q b) n", b=2), ALU.add).then_inc(sem("ot_ready"), 1)
            dve.wait_ge(sem("xh_ready"), 7)
            v.tensor_tensor(xl[1][:, :, :].rearrange("p (b k) t -> p b (k t)", b=4), ps[:, 4:8, :],
                            xh[1][:, :, :].bitcast(f32).rearrange("p (b k) t -> p b (k t)", b=4), ALU.subtract)\
                .then_inc(sem("xl_ready"), 1)
            residual("o1")
            norm_dve(3, "mlp1")
            mlp_dve("b1", "b2", 16)

        @block.gpsimd
        def _(pool):
            g = nc.gpsimd

            def lower(dst, src, hi, need, half=None):
                pool.wait_ge(sem("xh_ready"), need)
                g.tensor_tensor(dst[:, :, :], src[:, :, :], hi[:, :, :].bitcast(f32), ALU.subtract)\
                    .then_inc(sem("xl_ready"), 1)

            lower(xl[0], mix[1], xh[0], 1)
            lower(xl[1], mix[1], xh[1], 2)
            lower(xl[0], mix[1], xh[0], 3)
            pool.wait_ge(sem("kkn_used"), 1)
            g.tensor_tensor(Ai[:, :, :], KK[:, :, :], Ai[:, :, :], ALU.mult).then_inc(sem("b_ready"), 1)
            pool.wait_ge(sem("cs_ready"), 1)
            g.tensor_tensor(Sg[:, :, :], CSm[:, :, :], Sg[:, :, :], ALU.subtract).then_inc(sem("ex_ready"), 1)
            pool.wait_ge(sem("e_ready"), 2)
            pool.wait_ge(sem("b_ready"), 1)
            g.tensor_tensor(BK[:, :, :, 0, :].rearrange("p k c n -> p (k c) n"),
                            Ai[:, :, :].rearrange("p k (c n) -> p (k c) n", n=C),
                            E2[:, :, :].rearrange("p k (c n) -> p (k c) n", n=C), ALU.mult).then_inc(sem("bk_ready"), 1)
            pool.wait_ge(sem("bk_ready"), 2)
            pool.sem_inc(sem("b_used"), 1)
            pool.wait_ge(sem("rk_done"), 1)
            g.memset(UV[0:HD, :, :], 0.0).then_inc(sem("u_zero"), 1)
            lower(xl[0], YC, xh[0], 4)
            lower(xl[0], xn, xh[0], 5)
            lower(xl[0], xn, xh[0], 6)
            lower(xl[0], xn, xh[0], 8)

    return nc


_INS = ["x", "mix_norm", "mlp_norm", "mlp_w1", "mlp_w2", "rwkv_mu", "rwkv_w_in", "rwkv_w0", "rwkv_w1", "rwkv_w2",
        "rwkv_a0", "rwkv_a1", "rwkv_a2", "rwkv_g1", "rwkv_g2", "rwkv_k_k", "rwkv_k_a", "rwkv_r_k", "rwkv_ln_w",
        "rwkv_ln_b", "rwkv_w_out", "nsa_w_in", "nsa_cmp_pe", "nsa_cmp_w1", "nsa_cmp_w2", "nsa_q_norm", "nsa_k_norm",
        "nsa_w_out"]


def kernel(**inputs):
    import concourse.bacc as bacc
    from concourse.bass_utils import run_bass_kernel_spmd

    nc = bacc.Bacc("TRN2", target_bir_lowering=False, num_devices=1)
    arrays, aps = {}, {}
    for name in _INS:
        a = np.ascontiguousarray(inputs[name])
        arrays[f"in_{name}"] = a
        aps[name] = nc.dram_tensor(f"in_{name}", a.shape, mybir.dt.from_np(a.dtype), kind="ExternalInput").ap()
    consts, at = constants()
    assert at == CONST_AT and consts.shape[1] == CONST_N
    arrays["in_consts"] = consts
    aps["consts"] = nc.dram_tensor("in_consts", consts.shape, mybir.dt.float32, kind="ExternalInput").ap()
    out = nc.dram_tensor("out_0", (1, T, D), mybir.dt.float32, kind="ExternalOutput").ap()
    rwkv_nsa_trunk(nc, aps, out)
    r = run_bass_kernel_spmd(nc, [arrays], core_ids=[0])
    return r.results[0]["out_0"]
```

```python
import math
from contextlib import ExitStack

import concourse.bass as bass
import numpy as np
from concourse import mybir

P = 128
D = 1024
T = 256
FT = D // P
TT = T // P
HID = 4 * D
HT = HID // P
HD = 64
H = D // HD
C = 64
NCH = T // C
SUB = 16
LD, LI, LG = 64, 64, 160
HKV = 4
GRP = H // HKV
CB, CS = 32, 16
NB = T // CS - 1
NQ, NKV = D, HKV * HD
NG = 3 * H
EPS, GN_EPS = 1e-6, 64e-5
DECAY = math.exp(-0.5)
GELU_A, GELU_B = 2 * math.sqrt(2 / math.pi), 0.044715
FAR = 1e30
FLOOR = -1e25
SLOPES = [2.0 ** (-8.0 * (h + 1) / H) for h in range(H)]

UE = 1024
RING = 4
GW = 256


def constants():
    i = np.arange(P)
    s = (i % C)[:, None]
    t = np.arange(C)[None, :]
    same = (s // SUB) == (t // SUB)
    same32 = (s // (2 * SUB)) == (t // (2 * SUB))
    tt = np.arange(C)[None, :]
    cols = {
        "ident": np.eye(P),
        "mean": np.full((P, P), 1.0 / D),
        "pair": (i[:, None] // HD) == (i[None, :] // HD),
        "gmask": np.concatenate([s < tt, s <= tt], 1),
        "lmask16": (s > t) & same,
        "lmask32": (s > t) & ~same & same32,
        "lmask64": (s > t) & ~same32,
        "eye64": s == t,
        "hsel": np.arange(2 * H - 2)[None, :] == (H - 2 + i // HD)[:, None],
        "chunk": np.broadcast_to(np.arange(T)[None, :] % C != 0, (P, T)),
    }
    dist = []
    for q in range(TT):
        d = (q * P + i)[:, None] - np.arange((q + 1) * P)[None, :]
        dist.append(np.where(d >= 0, d, FAR))
    cols["dist"] = np.concatenate(dist, 1)
    end = np.arange(16) * CS + CB - 1
    adc = np.empty((P, TT, H, 16))
    for q in range(TT):
        d = (q * P + i)[:, None] - end[None, :]
        d = np.where((d >= 0) & (np.arange(16) < NB)[None, :], d, FAR)
        for h in range(H):
            adc[:, q, h] = -SLOPES[h] * d
    cols["adc"] = adc.reshape(P, -1)
    at, off = {}, 0
    for n, v in cols.items():
        at[n] = (off, v.shape[1])
        off += v.shape[1]
    return np.concatenate([np.asarray(v, np.float32) for v in cols.values()], 1), at


CONST_AT = {}
CONST_N = 0
_o = 0
for _n, _w in (("ident", P), ("mean", P), ("pair", P), ("gmask", 2 * C), ("lmask16", C), ("lmask32", C),
               ("lmask64", C), ("eye64", C), ("hsel", 2 * H - 2), ("chunk", T),
               ("dist", P * TT * (TT + 1) // 2), ("adc", TT * H * 16)):
    CONST_AT[_n] = (_o, _w)
    _o += _w
CONST_N = _o


def rwkv_nsa_trunk(nc, t, out):
    f32, r32 = mybir.dt.float32, mybir.dt.float32r
    ALU = mybir.AluOpType
    ACT = mybir.ActivationFunctionType
    AXX = mybir.AxisListType.X
    ds = bass.ds
    ctx = ExitStack()

    base = [(nc.sbuf_base + 63) // 64 * 64]

    def place(name, shape, off=None, dt=f32):
        size = 4 * int(np.prod(shape[1:]))
        if off is None:
            off = base[0]
            base[0] = (off + size + 63) // 64 * 64
        return nc.alloc_sbuf_tensor_at(name, shape, dt, offset=off)

    h = place("h", [P, FT, T])
    raw = place("raw", [P, RING, UE])
    whi = place("whi", [P, RING, UE], dt=r32)
    wlo = place("wlo", [P, RING, UE], dt=r32)
    cst = place("cst", [P, CONST_N])
    par = place("par", [P, 144])
    tiny = place("tiny", [P, 8])
    rs = place("rs", [P, T])
    ri = place("ri", [P, T])
    BLK = 4 * FT * T
    blk = base[0]
    off = lambda n, b=0: blk + n * BLK + b
    misc = blk + 16 * BLK
    A0, B0 = 12, 14
    xh = [place(f"xh{n}", [P, FT, T], off(12 + 2 * n), r32) for n in range(2)]
    xl = [place(f"xl{n}", [P, FT, T], off(13 + 2 * n), r32) for n in range(2)]

    xtok = place("xtok", [P, TT, D], off(1))
    prow = place("prow", [P, 2, P], off(2))
    sq = place("sq", [P, FT, T], off(0))
    xn = place("xn", [P, FT, T], off(11))
    dx = place("dx", [P, FT, T], off(1))
    mix = [place(f"mix{n}", [P, FT, T], off(2 + n)) for n in range(2)]
    R, K, V = (place(n, [P, FT, T], off(4 + i)) for i, n in enumerate("RKV"))
    lw = LD + LI + LG
    ldown = place("ldown", [P, FT, lw], off(7))
    lup_w = place("lup_w", [LD, D], off(7, 4 * FT * lw))
    lup_a = place("lup_a", [LI, D], off(7, 4 * FT * lw + 4 * D))
    lup_g0 = place("lup_g0", [P, D], off(7, 4 * FT * lw + 8 * D))
    lup_g1 = place("lup_g1", [LG - P, D], off(7, 4 * FT * lw + 12 * D))
    hw = place("hw", [LD, T], off(10, 2048))
    ha = place("ha", [LI, T], off(10, 2048 + 1024))
    hg0 = place("hg0", [P, T], off(10, 2048 + 2048))
    hg1 = place("hg1", [LG - P, T], off(10, 2048 + 3072))
    Sg = place("Sg", [P, FT, T], off(0))
    Ai = place("Ai", [P, FT, T], off(1))
    Gt = place("Gt", [P, FT, T], off(2))
    KK = place("KK", [P, FT, T], off(3))
    t11 = place("t11", [P, FT, T], off(11))
    CSm = place("CSm", [P, FT, T], off(14))
    sq2 = place("sq2", [P, FT, T], off(15))
    E1 = place("E1", [P, FT, T], off(15))
    E2 = CSm
    E3 = Sg
    kkr = place("kkr", [H, 2, T], misc + 4736)
    AR = place("AR", [P, FT, NCH, 2, C], off(7))
    BK = place("BK", [P, FT, NCH, 2, C], off(9))
    UV = place("UV", [P, NCH, D], off(4))
    BKT = place("BKT", [P, NCH, D], off(0))
    Gs = [place(f"Gs{n}", [P, FT, NCH, 2 * C], off([14, 12][n])) for n in range(2)]
    NP_ = 8
    NPAIR = FT * NCH // NP_ // 2
    DP = [place(f"DP{n}", [P, NP_, 2, C], off(12 + n)) for n in range(2)]
    LT = [place(f"LT{n}", [P, NP_, C], off(12 + n, 4096)) for n in range(2)]
    E32 = [place(f"E32{n}", [P, NP_, C], off(12 + n, 6144)) for n in range(2)]
    E64 = [place(f"E64{n}", [P, NP_, C], off(6, 4096 * n)) for n in range(2)]
    Lr = [place(f"Lr{n}", [P, NP_, C], off(6, 4096 * n + 2048)) for n in range(2)]
    Rinv = place("Rinv", [P, FT * NCH, C], off(3))
    PC = place("PC", [P, FT, NCH], misc)
    rst = place("rst", [H, 2 * C], misc + 128)
    XS = [place(f"XS{n}", [P, FT // 2, C], misc + 640 + 1024 * n) for n in range(2)]
    STt = [place(f"STt{n}", [P, FT // 2, C], misc + 2688 + 1024 * n) for n in range(2)]
    ST = [[place(f"ST{n}{b}", [P, FT // 2, C], misc + 4736 + 2048 * n + 1024 * b) for b in range(2)] for n in range(2)]
    spread = place("spread", [H, D], misc + 8832)
    YC = place("YC", [P, FT, C], off(6))
    YQ = place("YQ", [P, FT, C], off(6, 2048))
    YF = [place(f"YF{n}", [P, FT, C], off(6, 4096 + 2048 * n)) for n in range(2)]
    yh = place("yh", [P, FT, T], off(9), r32)
    yl = place("yl", [P, FT, T], off(10), r32)

    hh = place("hh", [P, HT, T], off(0), r32)
    hl = place("hl", [P, HT, T], off(4), r32)
    rl = place("rl", [P, 2, 2, T], off(8))
    s2 = place("s2", [P, 2, 2, T], off(8, 4096))
    cw1 = place("cw1", [P, 2, CB // 2, P], off(9))
    cw2 = place("cw2", [P, 2, 2, HD], off(14))
    gw = place("gw", [P, FT, NG], off(14, 1024))
    perow = place("perow", [2 * CB, 2, HD], off(14, 2560))
    pec = place("pec", [P, 2 * CB], off(14, 3072))
    Qn = place("Qn", [P, FT, T], off(1))
    kv = place("kv", [P, 4, 2, T], off(2))
    vt = place("vt", [P, 2, TT, NKV], off(3))
    gat = place("gat", [P, TT, NG], off(3, 4096))
    kcm = place("kcm", [P, HKV * NB], off(3, 4608))
    hid = place("hid", [P, 2, HKV * NB], off(3, 4864))
    gu = place("gu", [P, 2, HKV * NB], off(3, 5376))
    hpad = place("hpad", [P, HKV, 4, 32], off(3, 5888))
    kd = place("kd", [P, 2, HKV, T], off(4))
    Zc = place("Zc", [P, 2, CB // 2, HKV * NB], off(5))
    ksq = place("ksq", [P, 2, 2, T], off(6))
    krs = place("krs", [P, 2, 2, T], off(6, 4096))
    vblk = place("vblk", [P, HKV, 4 * HD], off(7))
    Sc = place("Sc", [P, TT, H, 32], off(8))
    PcT = place("PcT", [P, TT, HKV, P], off(8, 4096))
    csm = place("csm", [P, 4, TT, H], off(7, 4096))
    SB = place("SB", [P, 2, 4, T], off(0))
    PT = place("PT", [P, 2, 4, TT, P], off(5))
    qss = place("qss", [P, FT, T], off(0))
    qrs = place("qrs", [P, FT, T], off(15))
    nmx = place("nmx", [P, 2, 4], off(7, 5120))
    den = place("den", [P, TT, 2, H], off(7, 5376))
    cof = place("cof", [P, TT, 2, H], off(7, 5888))
    Ot = place("Ot", [P, TT, D], off(9))
    o1 = place("o1", [P, 2, GW], off(6, 0))
    otok = place("otok", [P, TT, D], off(9))

    ps = ctx.enter_context(nc.psum_tensor("ps", [P, 8, 512], f32))

    def cc(name, p0=0, p1=P):
        o, w = CONST_AT[name]
        return cst[p0:p1, o:o + w]

    names = ["mix0", "mix1", "mlp0", "mlp1", "mu0", "mu1", "mu2", "mu3", "mu4", "mu5", "w0", "a0",
             "k_k", "k_a", "r_k", "ln_w", "ln_b"]
    pcol = {n: FT * i for i, n in enumerate(names)}
    for i, n in enumerate(["qn", "kn0", "kn1", "kn2"]):
        pcol[n] = FT * len(names) + i
    NPAR = FT * len(names) + 4

    def pv(name, k=0):
        return par[:, pcol[name] + k:pcol[name] + k + 1]

    def kview(w):
        return w.rearrange("(k p) n -> p k n", p=P)

    w_in, w_o = kview(t["rwkv_w_in"][0]), kview(t["rwkv_w_out"][0])
    n_in, n_o = kview(t["nsa_w_in"][0]), kview(t["nsa_w_out"][0])
    m1 = [kview(t["mlp_w1"][i]) for i in range(2)]
    m2 = [kview(t["mlp_w2"][i]) for i in range(2)]
    UNITS = [("r", 8), ("k", 8), ("v", 8), ("o0", 8), ("a1", 32), ("a2", 32), ("q", 8), ("kv", 12),
             ("o1", 8), ("b1", 32), ("b2", 32)]
    U0, n = {}, 0
    for name, cnt in UNITS:
        U0[name] = n
        n += cnt
    NU = n
    GROUPS = [("x", 4, "act"), ("r", 4, "act"), ("k", 4, "act"), ("up", 12, "act"), ("v", 4, "act"),
              ("o0", 4, "dve"), ("a1", 16, "act"), ("a2", 4, "dve"), ("q", 4, "act"), ("kv", 6, "act"),
              ("o1", 4, "dve"), ("b1", 16, "act"), ("b2", 4, "dve")]
    G0, EV0, n, ev = {}, {}, 0, {"act": 0, "dve": 0}
    for name, cnt, who in GROUPS:
        G0[name], EV0[name] = n, ev[who]
        n += cnt
        ev[who] += cnt

    XH0 = {x: 2 * i for i, x in enumerate(["r", "k", "v", "a", "nsa", "o1", "b"])}
    XL0 = {"r": ("xl_dve", 0), "k": ("xl_pool", 0), "v": ("xl_pool", 2), "a": ("xl_dve", 2), "nsa": ("xl_dve", 4),
           "o1": ("xl_dve", 6), "b": ("xl_dve", 8)}

    sems = {}

    def sem(name):
        if name not in sems:
            sems[name] = ctx.enter_context(nc.semaphore(name))
        return sems[name]

    with ctx:
        raw_in = [sem(f"raw_in{s}") for s in range(RING)]
        hi_ready = sem("hi_ready")
        lo_ready = sem("lo_ready")
        unit_used = sem("unit_used")
        ev_act = sem("ev_act")
        ev_dve = sem("ev_dve")
        block = ctx.enter_context(nc.Block())

        @block.sync
        def _(sp):
            sp.dma_start(cst[:, 0:3 * P], t["consts"][:, 0:3 * P]).then_inc(sem("cst_in"), 16)
            sp.dma_start(xtok[:, :, :], t["x"][0].rearrange("(a p) n -> p a n", p=P)).then_inc(sem("x_in"), 16)
            pr = sem("par_in")
            for i, n in enumerate(["mix_norm", "mlp_norm"]):
                sp.dma_start(prow[16 * i:16 * i + 16, 0, :], t[n].rearrange("a (k p) -> (a k) p", p=P)).then_inc(pr, 16)
            sp.dma_start(prow[32:80, 0, :], t["rwkv_mu"][0].rearrange("a (k p) -> (a k) p", p=P)).then_inc(pr, 16)
            for i, n in enumerate(["rwkv_w0", "rwkv_a0", "rwkv_k_k", "rwkv_k_a"]):
                sp.dma_start(prow[80 + 8 * i:88 + 8 * i, 0, :], t[n][0].rearrange("(k p) -> k p", p=P)).then_inc(pr, 16)
            sp.dma_start(prow[112:120, 0, :], t["rwkv_r_k"][0].rearrange("(k a) n -> k (a n)", a=2)).then_inc(pr, 16)
            sp.dma_start(prow[120:128, 0, :], t["rwkv_ln_w"][0].rearrange("(k p) -> k p", p=P)).then_inc(pr, 16)
            sp.dma_start(prow[0:8, 1, :], t["rwkv_ln_b"][0].rearrange("(k p) -> k p", p=P)).then_inc(pr, 16)
            for a in range(2):
                sp.dma_start(prow[8:9, 1, a * HD:(a + 1) * HD], t["nsa_q_norm"]).then_inc(pr, 16)
                sp.dma_start(prow[9:12, 1, a * HD:(a + 1) * HD], t["nsa_k_norm"][0]).then_inc(pr, 16)
            sp.dma_start(spread[:, :], t["spread"]).then_inc(sem("spread_in"), 16)

            def rows(v, n):
                return v.rearrange("(k p) -> k p", p=P) if n else v

            def load(u, src):
                s = u % RING if isinstance(u, int) else None
                dst = raw[:, s, :].rearrange("p (k n) -> p k n", n=GW)
                if u >= RING:
                    sp.wait_ge(lo_ready, u - RING + 1)
                sp.dma_start(dst, src).then_inc(raw_in[s], 16)

            def pairs(name, view, col0, lo, hi):
                for j in range(lo, hi):
                    c0 = col0 + (j // 2) * GW
                    load(U0[name] + j, view[:, 4 * (j % 2):4 * (j % 2) + 4, c0:c0 + GW])

            lo = sem("lora_in")
            pairs("r", w_in, 0, 0, 4)
            sp.dma_start(cst[:, 3 * P:], t["consts"][:, 3 * P:]).then_inc(sem("cst_rest"), 16)
            sp.dma_start(ldown[:, :, 0:LD], kview(t["rwkv_w1"][0])).then_inc(lo, 16)
            sp.dma_start(ldown[:, :, LD:LD + LI], kview(t["rwkv_a1"][0])).then_inc(lo, 16)
            sp.dma_start(ldown[:, :, LD + LI:lw], kview(t["rwkv_g1"][0])).then_inc(lo, 16)
            sp.dma_start(lup_w[:, :], t["rwkv_w2"][0]).then_inc(lo, 16)
            sp.dma_start(lup_a[:, :], t["rwkv_a2"][0]).then_inc(lo, 16)
            sp.dma_start(lup_g0[:, :], t["rwkv_g2"][0][0:P, :]).then_inc(lo, 16)
            sp.dma_start(lup_g1[:, :], t["rwkv_g2"][0][P:LG, :]).then_inc(lo, 16)
            pairs("r", w_in, 0, 4, 8)
            pairs("k", w_in, D, 0, 8)
            pairs("v", w_in, 2 * D, 0, 8)
            pairs("o0", w_o, 0, 0, 8)

            def mlp_loads(n1, n2, v1, v2):
                pairs(n1, v1, 0, 0, 4)
                if n1 == "a1":
                    sp.wait_ge(ev_dve, EV0["o0"] + 4)
                    cs = sem("cmp_in")
                    for a in range(2):
                        src = t["nsa_cmp_w1"][0].rearrange("b (a l d) m -> a d b l m", a=2, l=CB // 2)[a]
                        for b in range(2):
                            sp.dma_start(cw1[64 * a:64 * a + 64, b, :, :], src[:, b, :, :]).then_inc(cs, 16)
                        sp.dma_start(cw2[:, :, a, :], t["nsa_cmp_w2"][0].rearrange("b m d -> m b d")).then_inc(cs, 16)
                        sp.dma_start(perow[:, a, :], t["nsa_cmp_pe"][0].rearrange("b l d -> (b l) d")).then_inc(cs, 16)
                    sp.dma_start(gw[:, :, :], n_in[:, :, NQ + 6 * NKV:]).then_inc(cs, 16)
                with sp.Fori(1, 8) as i:
                    for j in range(4):
                        sp.wait_ge(lo_ready, i * 4 + (U0[n1] + j - RING + 1))
                        sp.dma_start(raw[:, j, :].rearrange("p (k n) -> p k n", n=GW),
                                     v1[:, 4 * (j % 2):4 * (j % 2) + 4, ds(i * (2 * GW) + (j // 2) * GW, GW)])\
                          .then_inc(raw_in[j], 16)
                with sp.Fori(0, 4) as i:
                    for j in range(8):
                        sp.wait_ge(lo_ready, i * 8 + (U0[n2] + j - RING + 1))
                        sp.dma_start(raw[:, j % RING, :].rearrange("p (k n) -> p k n", n=GW),
                                     v2[:, 4 * j:4 * j + 4, ds(i * GW, GW)]).then_inc(raw_in[j % RING], 16)

            mlp_loads("a1", "a2", m1[0], m2[0])
            pairs("q", n_in, 0, 0, 8)
            pairs("kv", n_in, NQ, 0, 12)
            pairs("o1", n_o, 0, 0, 8)
            mlp_loads("b1", "b2", m1[1], m2[1])
            for q in range(TT):
                sp.wait_ge(sem("out_ready"), q + 1)
                sp.dma_start(out[0, q * P:(q + 1) * P, :], otok[:, q, :]).then_inc(sem("stored"), 16)
            sp.wait_ge(sem("stored"), 16 * TT)

        @block.tensor
        def _(pe):
            mm = nc.tensor.matmul

            def group_free(name, g):
                if EV0[name] + g - 1 > 0:
                    pe.wait_ge(ev_act if who[name] == "act" else ev_dve, EV0[name] + g - 1)

            who = {n: w for n, _, w in GROUPS}

            def unit_mm(slot, bank0, kbase, ktiles, hi, lo):
                for k in range(4):
                    kk = kbase + k
                    for m in range(2):
                        o = ps[:, bank0 + m, 0:T]
                        c0 = k * GW + m * P
                        wh, wl = whi[:, slot, c0:c0 + P], wlo[:, slot, c0:c0 + P]
                        mm(o, wh, hi[:, kk, :], start=(kk == 0), stop=False)
                        mm(o, wh, lo[:, kk, :], start=False, stop=False)
                        last = mm(o, wl, hi[:, kk, :], start=False, stop=(kk == ktiles - 1))
                return last

            def parts(x, half):
                pe.wait_ge(sem("xh_ready"), XH0[x] + half + 1)
                where, base_ = XL0[x]
                pe.wait_ge(sem(where), base_ + half + 1)

            def linear8(name, hi, lo, x=None, between=None):
                for g in range(4):
                    group_free(name, g)
                    for j in range(2):
                        u = U0[name] + 2 * g + j
                        if g == 0 and x:
                            parts(x, j)
                        pe.wait_ge(lo_ready, u + 1)
                        last = unit_mm(u % RING, 2 * (g % 2), 4 * j, FT, hi, lo)
                        last.then_inc(unit_used, 1)
                    if between:
                        between(g)

            pe.wait_ge(sem("cst_in"), 16)
            pe.wait_ge(sem("x_in"), 16)
            for g in range(4):
                if g >= 2:
                    pe.wait_ge(ev_act, g - 1)
                for m in range(2):
                    for q in range(TT):
                        last = nc.tensor.transpose(ps[:, 2 * (g % 2) + m, q * P:(q + 1) * P],
                                                   xtok[:, q, (2 * g + m) * P:(2 * g + m + 1) * P], cc("ident"))
                last.then_inc(sem("x_pe0"), 1)
            pe.wait_ge(sem("par_in"), 16 * 14)
            nc.tensor.transpose(ps[:, 5, 0:P], prow[:, 0, :], cc("ident"))
            nc.tensor.transpose(ps[:, 5, P:P + 12], prow[0:12, 1, :], cst[0:12, 0:12]).then_inc(sem("par_t"), 1)

            def norm_pe(i):
                for k in range(FT):
                    if k % 2 == 0:
                        pe.wait_ge(sem("sq_ready"), 4 * i + 1 + k // 2)
                    last = mm(ps[:, 4, 0:T], cc("mean"), sq[:, k, :], start=(k == 0), stop=(k == FT - 1))
                last.then_inc(sem("ms_ready"), 1)

            norm_pe(0)

            def hsel(k):
                return cc("hsel")[:, H - 2 - 2 * k:2 * H - 2 - 2 * k]

            def hspread(k):
                return spread[:, k * P:(k + 1) * P]

            def lora_down(n, src, c0, width, bank):
                for k in range(FT):
                    last = mm(ps[0:width, bank, 0:T], ldown[:, k, c0:c0 + width], src[:, k, :],
                              start=(k == 0), stop=(k == FT - 1))
                return last

            linear8("r", xh[0], xl[0], "r")
            pe.wait_ge(sem("lora_in"), 16 * 7)
            pe.wait_ge(sem("mix_ready"), 6)
            lora_down("w", mix[1], 0, LD, 5).then_inc(sem("lora_h"), 1)
            pe.wait_ge(sem("mix_ready"), 8)
            lora_down("a", mix[0], LD, LI, 6).then_inc(sem("lora_h"), 1)
            pe.wait_ge(sem("mix_ready"), 10)
            lora_down("g", mix[1], LD + LI, P, 7)
            lora_down("g", mix[1], LD + LI + P, LG - P, 4).then_inc(sem("lora_h"), 1)
            linear8("k", xh[1], xl[1], "k")
            ups = [(1, [(lup_w, hw)]), (2, [(lup_a, ha)]), (3, [(lup_g0, hg0), (lup_g1, hg1)])]
            for n, (need, lora) in enumerate(ups):
                pe.wait_ge(sem("lora_act"), need)
                if n == 2:
                    pe.wait_ge(sem("kksq"), 1)
                    pe.wait_ge(sem("cst_rest"), 16)
                    for k in range(FT):
                        last = mm(ps[0:H, 4, 0:T], hsel(k), sq2[:, k, :], start=(k == 0), stop=(k == FT - 1))
                    last.then_inc(sem("kk_sum"), 1)
                for g in range(4):
                    pe.wait_ge(ev_act, EV0["up"] + 4 * n + g - 1)
                    for m in range(2):
                        c0 = (2 * g + m) * P
                        for i, (w, x) in enumerate(lora):
                            last = mm(ps[:, 2 * (g % 2) + m, 0:T], w[:, c0:c0 + P], x[:, :],
                                      start=(i == 0), stop=(i == len(lora) - 1))
                    last.then_inc(sem("up_pe"), 1)

            def between_v(g):
                if g == 0:
                    pe.wait_ge(sem("spread_in"), 16)
                    pe.wait_ge(sem("kk_inv"), 1)
                    for k in range(FT):
                        last = mm(ps[:, 4 + k // 2, (k % 2) * T:(k % 2 + 1) * T], hspread(k), kkr[:, 1, :],
                                  start=True, stop=True)
                    last.then_inc(sem("kk_spread"), 1)
                if g == 1:
                    pe.wait_ge(sem("rk"), 1)
                    pe.wait_ge(sem("kkn_used"), 1)
                    for j in range(4):
                        last = mm(ps[:, 4 + j, :], cc("pair"), t11[:, 2 * j:2 * j + 2, :], start=True, stop=True)
                    last.then_inc(sem("rk_sum"), 1)

            linear8("v", xh[0], xl[0], "v", between_v)

            def b_k(c):
                b = 4 + 2 * (c % 2)
                for k in range(FT):
                    last = nc.tensor.transpose(ps[:, b + k // 4, (k % 4) * P:(k % 4 + 1) * P],
                                               BK[:, k, c, :, :], cc("ident"))
                last.then_inc(sem("bkT"), 1)

            pe.wait_ge(sem("bk_ready"), 2)
            pe.wait_ge(sem("rk_copied"), 1)
            b_k(0)
            b_k(1)
            pe.wait_ge(ev_act, EV0["v"] + 4)
            for q in range(TT):
                for k in range(FT):
                    last = nc.tensor.transpose(ps[:, 2 * q + k // 4, (k % 4) * P:(k % 4 + 1) * P],
                                               V[:, k, q * P:(q + 1) * P], cc("ident"))
                last.then_inc(sem("vT"), 1)
            pe.wait_ge(sem("bkt_act"), 1)
            b_k(2)
            pe.wait_ge(sem("bkt_dve"), 1)
            b_k(3)

            pe.wait_ge(sem("ar_ready"), 2)

            def at(e):
                return slice(HD * e, HD * e + HD)

            def g_products(half):
                for n in range(8):
                    k, e = half * FT // 2 + n // 2, n % 2
                    if half == 0 and n % 2 == 0:
                        who_, cnt_ = [("v_copied", 2), ("v_copied", 4), ("bkt_act", 2), ("bkt_dve", 2)][n // 2]
                        pe.wait_ge(sem(who_), cnt_)
                    for c in range(NCH):
                        last = mm(ps[:, n, c * P:(c + 1) * P], BK[at(e), k, c, :, :], AR[at(e), k, c, :, :],
                                  start=True, stop=True)
                    last.then_inc(sem("g_done"), 1)

            g_products(0)

            def batch(slot, bank, width, lhs, rhs):
                def one(p, e):
                    return mm(ps[at(e), bank + p // 4, (p % 4) * width:(p % 4 + 1) * width], lhs(p, e), rhs(p, e),
                              start=True, stop=True)
                for a in range(2):
                    for i in range(NP_ // 2):
                        one(i, a)
                        last = one(i + NP_ // 2, 1 - a)
                last.then_inc(sem(f"inv_pe{slot}"), 1)

            for pair in range(NPAIR):
                for n in range(9):
                    for s in range(2):
                        p0 = (2 * pair + s) * NP_
                        lt = lambda p, e: LT[s][at(e), p, :]
                        pw = lambda p, e: DP[s][at(e), p, 0, :]
                        pr = lambda p, e: DP[s][at(e), p, 1, :]
                        both = lambda p, e: DP[s][at(e), p, :, :]
                        if n == 0 and pair == 0:
                            pe.wait_ge(sem("g_masked"), 4 * s + 4)
                        else:
                            pe.wait_ge(sem(f"inv_dve{s}"), 13 * pair + [0, 2, 4, 6, 8, 9, 10, 11, 12][n])
                            pe.wait_ge(sem(f"inv_act{s}"), 5 * pair + [0, 1, 2, 3, 3, 3, 4, 4, 5][n])
                        if n in (5, 7):
                            pe.wait_ge(sem(f"inv_pool{s}"), 2 * pair + {5: 1, 7: 2}[n])
                        b = 4 * s + 2 * (n % 2)
                        ar = lambda p, e: AR[at(e), (p0 + p) // NCH, p % NCH, 0, :]
                        bk = lambda p, e: BK[at(e), (p0 + p) // NCH, p % NCH, 0, :]
                        e32 = lambda p, e: E32[s][at(e), p, :]
                        e64 = lambda p, e: E64[s][at(e), p, :]
                        if n == 0:
                            batch(s, b, C, ar, bk)
                        elif n == 1:
                            batch(s, b, C, lt, pw)
                        elif n in (2, 3):
                            batch(s, b, 2 * C, lt, both)
                        elif n in (4, 6):
                            batch(s, b, C, lt, pr if n == 4 else pw)
                        elif n in (5, 7):
                            batch(s, b, C, e32 if n == 5 else e64, pr)
                        else:
                            batch(s, b, C, lt, pw)

            for s in range(2):
                pe.wait_ge(sem(f"inv_dve{s}"), 13 * NPAIR)
            g_products(1)
            pe.wait_ge(sem("g_masked"), 16)
            pe.wait_ge(sem("u_zero"), 1)

            def hk(half):
                for k_ in range(FT // 2):
                    for e in range(2):
                        k = half * FT // 2 + k_
                        yield k_, k, e, 2 * k_ + e, slice((2 * k + e) * HD, (2 * k + e + 1) * HD)

            def gn_mean(c):
                for n in range(2):
                    pe.wait_ge(sem(f"y_copied{n}"), c + 1)
                if c:
                    pe.wait_ge(sem("y_scaled"), c)
                mm(ps[:, 6, :], cc("pair"), AR[:, :, c, 1, :], start=True, stop=True).then_inc(sem("mean_pe"), 1)

            def gn_var(c):
                pe.wait_ge(sem("y_sq"), c + 1)
                for k in range(FT):
                    last = mm(ps[0:H, 7, 0:C], hsel(k), YQ[:, k, :], start=(k == 0), stop=(k == FT - 1))
                last.then_inc(sem("var_pe"), 1)

            def gn_spread(c):
                pe.wait_ge(sem("y_rstd"), c + 1)
                for k in range(FT):
                    last = mm(ps[:, 6, k * C:(k + 1) * C], hspread(k), rst[:, 0:C], start=True, stop=True)
                last.then_inc(sem("rstd_pe"), 1)

            for c in range(NCH):
                for half in range(2):
                    if c:
                        pe.wait_ge(sem(f"st_ready{half}"), c)
                        pe.wait_ge(sem(f"x_sb{half}"), c)
                    for k_, k, e, hd, cols in hk(half):
                        o = ps[at(e), 3 * half, k_ * C:(k_ + 1) * C]
                        last = mm(o, Gs[half][:, hd, c, 0:C], UV[:, c, cols], start=True, stop=(c == 0))
                        if c:
                            last = mm(o, AR[at(e), k, c, 0, :], ST[half][(c - 1) % 2][at(e), k_, :], start=False, stop=True)
                    last.then_inc(sem(f"xs_pe{half}"), 1)
                if c:
                    gn_mean(c - 1)
                for half in range(2):
                    pe.wait_ge(sem(f"x_sb{half}"), c + 1)
                    if c:
                        pe.wait_ge(sem(f"y_copied{half}"), c)
                    for k_, k, e, hd, cols in hk(half):
                        last = mm(ps[0:HD, 3 * half + 1 + e, k_ * C:(k_ + 1) * C], Rinv[at(e), k * NCH + c, :],
                                  XS[half][at(e), k_, :], start=True, stop=True)
                    last.then_inc(sem(f"u_pe{half}"), 1)
                if c:
                    gn_var(c - 1)
                for half in range(2):
                    pe.wait_ge(sem(f"u_even{half}"), c + 1)
                    pe.wait_ge(sem(f"u_odd{half}"), c + 1)
                    if c < NCH - 1:
                        if c:
                            pe.wait_ge(sem(f"st_ready{half}"), c)
                        for k_, k, e, hd, cols in hk(half):
                            last = mm(ps[at(e), 3 * half, k_ * C:(k_ + 1) * C], BKT[:, c, cols], UV[:, c, cols],
                                      start=True, stop=True)
                        last.then_inc(sem(f"s_pe{half}"), 1)
                for half in range(2):
                    for k_, k, e, hd, cols in hk(half):
                        o = ps[at(e), 3 * half + 1, k_ * C:(k_ + 1) * C]
                        last = mm(o, UV[:, c, cols], Gs[half][:, hd, c, C:2 * C], start=True, stop=(c == 0))
                        if c:
                            last = mm(o, ST[half][(c - 1) % 2][at(e), k_, :], AR[at(e), k, c, 1, :], start=False, stop=True)
                    last.then_inc(sem(f"y_pe{half}"), 1)
                if c:
                    gn_spread(c - 1)
            gn_mean(NCH - 1)
            gn_var(NCH - 1)
            gn_spread(NCH - 1)
            pe.wait_ge(sem("yh_ready"), NCH)
            pe.wait_ge(sem("yl_ready"), NCH)
            linear8("o0", yh, yl)

            def mlp_pe(n1, n2, hi, lo, x):
                for g in range(2):
                    group_free(n1, g)
                    for j in range(2):
                        if g == 0:
                            parts(x, j)
                        pe.wait_ge(lo_ready, U0[n1] + 2 * g + j + 1)
                        unit_mm(2 * g + j, 2 * g, 4 * j, FT, hi, lo).then_inc(unit_used, 1)
                with pe.Fori(1, 8) as i:
                    for g in range(2):
                        pe.wait_ge(ev_act, i * 2 + (EV0[n1] + g - 1))
                        for j in range(2):
                            pe.wait_ge(lo_ready, i * 4 + (U0[n1] + 2 * g + j + 1))
                            unit_mm(2 * g + j, 2 * g, 4 * j, FT, hi, lo).then_inc(unit_used, 1)
                pe.wait_ge(sem("hid_ready"), 16 if n1 == "a1" else 32)
                with pe.Fori(0, 2) as i:
                    for g in range(2):
                        pe.wait_ge(ev_dve, i * 2 + (EV0[n2] + g - 1))
                        for j in range(8):
                            pe.wait_ge(lo_ready, i * 16 + (U0[n2] + 8 * g + j + 1))
                            unit_mm(j % RING, 2 * g, 4 * j, HT, hh, hl).then_inc(unit_used, 1)

            norm_pe(1)
            mlp_pe("a1", "a2", xh[0], xl[0], "a")

            norm_pe(2)
            linear8("q", xh[0], xl[0], "nsa")
            for g, tok in enumerate([0, 0, 0, 1, 0, 1]):
                pe.wait_ge(ev_act, EV0["kv"] + g - 1)
                for j in range(2):
                    u = U0["kv"] + 2 * g + j
                    pe.wait_ge(lo_ready, u + 1)
                    if not tok:
                        last = unit_mm(u % RING, 2 * (g % 2), 4 * j, FT, xh[0], xl[0])
                    else:
                        for k in range(4):
                            kk_ = 4 * j + k
                            for q in range(TT):
                                o = ps[:, 2 * (g % 2) + q, 0:GW]
                                tq = slice(q * P, (q + 1) * P)
                                wh = whi[:, u % RING, k * GW:(k + 1) * GW]
                                wl = wlo[:, u % RING, k * GW:(k + 1) * GW]
                                mm(o, xh[0][:, kk_, tq], wh, start=(kk_ == 0), stop=False)
                                mm(o, xh[0][:, kk_, tq], wl, start=False, stop=False)
                                last = mm(o, xl[0][:, kk_, tq], wh, start=False, stop=(kk_ == FT - 1))
                    last.then_inc(unit_used, 1)
            pe.wait_ge(sem("cmp_in"), 16 * 9)
            for q in range(TT):
                for k in range(FT):
                    mm(ps[:, 4, q * 64:q * 64 + NG], xn[:, k, q * P:(q + 1) * P], gw[:, k, :],
                       start=(k == 0), stop=(k == FT - 1))
            nc.tensor.transpose(ps[:, 5, 0:2 * CB], perow[:, :, :], cst[0:2 * CB, 0:2 * CB]).then_inc(sem("gate_pe"), 1)
            pe.wait_ge(sem("qsq"), 1)
            pe.wait_ge(ev_act, EV0["kv"] + 6)
            for j, bank in enumerate([6, 7, 0, 1]):
                last = mm(ps[:, bank, :], cc("pair"), qss[:, 2 * j:2 * j + 2, :], start=True, stop=True)
            last.then_inc(sem("qn_pe"), 1)
            pe.wait_ge(sem("ksq_r"), 1)
            for a in range(2):
                last = mm(ps[:, 2 + a, :], cc("pair"), ksq[:, a, :, :], start=True, stop=True)
            last.then_inc(sem("kn_pe"), 1)
            pe.wait_ge(sem("zc"), 1)
            pe.wait_ge(sem("gates_r"), 1)
            for b in range(2):
                for l in range(CB // 2):
                    last = mm(ps[:, 4, b * 64:b * 64 + HKV * NB], cw1[:, b, l, :], Zc[:, b, l, :],
                              start=(l == 0), stop=(l == CB // 2 - 1))
            last.then_inc(sem("cmp_pe"), 1)
            pe.wait_ge(sem("hid_k"), 1)
            mm(ps[:, 5, 0:HKV * NB], cw2[:, 0, :, :], hid[:, 0, :], start=True, stop=True)
            for j in range(HKV):
                last = mm(ps[:, 5, 128 + j * HD:128 + (j + 1) * HD], hpad[:, j, :, :], cw2[:, 1, 0, :],
                          start=True, stop=True)
            last.then_inc(sem("cmp2_pe"), 1)
            pe.wait_ge(sem("kcsq"), 1)
            mm(ps[:, 4, 0:HKV * NB], cc("pair"), gu[:, 0, :], start=True, stop=True).then_inc(sem("kc_pe"), 1)
            pe.wait_ge(sem("kcm_r"), 1)
            pe.wait_ge(sem("q_ready"), 1)
            for q in range(TT):
                b0 = [6, 0][q]
                for k in range(FT):
                    for e in range(2):
                        qe = slice(HD * e, HD * e + HD)
                        j = (2 * k + e) // GRP
                        last = mm(ps[:, b0 + e, k * 16:k * 16 + NB], Qn[qe, k, q * P:(q + 1) * P],
                                  kcm[qe, j * NB:(j + 1) * NB], start=True, stop=True)
                last.then_inc(sem("sc_pe"), 1)
            pe.wait_ge(sem("pc_ready"), 1)
            for q in range(TT):
                for j in range(HKV):
                    last = nc.tensor.transpose(ps[:, 4 + q, j * P:(j + 1) * P], Sc[:, q, 4 * j:4 * j + 4, :], cc("ident"))
            last.then_inc(sem("pct_pe"), 1)

            items = [(j, q, b) for j in range(HKV) for q in range(TT) for b in range(2)]
            pe.wait_ge(sem("kd_ready"), 1)
            pe.wait_ge(sem("pct_r"), 1)

            def scores(n):
                j, q, b = items[n]
                if n >= 2:
                    pe.wait_ge(sem("s_read"), n - 1)
                w = (q + 1) * P
                for i in range(2):
                    for e in range(2):
                        k = 2 * j + i
                        qe = slice(HD * e, HD * e + HD)
                        last = mm(ps[:, 2 * (n % 2) + e, i * T:i * T + w], Qn[qe, k, q * P:(q + 1) * P],
                                  kd[qe, b, j, 0:w], start=True, stop=True)
                last.then_inc(sem("s_pe2"), 1)

            def transposes(n):
                j, q, b = items[n]
                pe.wait_ge(sem("p_ready"), n + 1)
                if n >= 1:
                    pe.wait_ge(sem("pt_read"), n)
                for s in range(q + 1):
                    for i in range(4):
                        last = nc.tensor.transpose(ps[:, 4 + s, i * P:(i + 1) * P],
                                                   SB[:, n % 2, i, s * P:(s + 1) * P], cc("ident"))
                last.then_inc(sem("t_pe"), 1)

            def weighted(n):
                j, q, b = items[n]
                pe.wait_ge(sem("pt_read"), n + 1)
                g = n // 2
                if b == 0 and g >= 2:
                    pe.wait_ge(sem("o_done"), g - 1)
                for i in range(4):
                    for s in range(q + 1):
                        last = mm(ps[:, 6 + g % 2, b * GW + i * HD:b * GW + (i + 1) * HD],
                                  PT[:, n % 2, i, s, :], vt[:, b, s, j * HD:(j + 1) * HD],
                                  start=(s == 0), stop=(s == q))
                last.then_inc(sem("pv_pe"), 1)

            scores(0)
            for n in range(len(items)):
                if n + 1 < len(items):
                    scores(n + 1)
                transposes(n)
                if n >= 1:
                    weighted(n - 1)
            weighted(len(items) - 1)
            pe.wait_ge(sem("s_read"), len(items))
            for q in range(TT):
                for j in range(HKV):
                    last = mm(ps[:, 2 * q + j // 2, (j % 2) * GW:(j % 2 + 1) * GW], PcT[:, q, j, :], vblk[:, j, :],
                              start=True, stop=True)
            last.then_inc(sem("oc_pe"), 1)
            pe.wait_ge(sem("ot_ready"), 1)
            pe.wait_ge(sem("pt_read"), len(items))
            for k in range(FT):
                for q in range(TT):
                    last = nc.tensor.transpose(ps[:, 4 + k // 2, (k % 2) * T + q * P:(k % 2) * T + (q + 1) * P],
                                               Ot[:, q, k * P:(k + 1) * P], cc("ident"))
            last.then_inc(sem("oT_pe"), 1)
            linear8("o1", xh[1], xl[1], "o1")

            norm_pe(3)
            mlp_pe("b1", "b2", xh[0], xl[0], "b")
            for q in range(TT):
                for k in range(FT):
                    if q == 0 and k % 2 == 0:
                        pe.wait_ge(ev_dve, EV0["b2"] + k // 2 + 1)
                    last = nc.tensor.transpose(ps[:, 4 + 2 * q + k // 4, (k % 4) * P:(k % 4 + 1) * P],
                                               h[:, k, q * P:(q + 1) * P], cc("ident"))
                last.then_inc(sem("fin_pe"), 1)

        @block.scalar
        def _(act):
            A = nc.scalar.activation
            aown = sem("act_step")
            cnt = [0]

            def step(ins):
                cnt[0] += 1
                ins.then_inc(aown, 1)

            def settle():
                act.wait_ge(aown, cnt[0])

            def split(u):
                s = u % RING
                act.wait_ge(raw_in[s], 16 * (u // RING + 1))
                if u >= RING:
                    act.wait_ge(unit_used, u - RING + 1)
                A(whi[:, s, :], raw[:, s, :], ACT.Copy).then_inc(hi_ready, 1)

            def ahead(u):
                if u + RING < NU:
                    split(u + RING)

            def evac8(name, dst):
                for g in range(4):
                    act.wait_ge(unit_used, U0[name] + 2 * g + 2)
                    A(dst[:, 2 * g:2 * g + 2, :], ps[:, 2 * (g % 2):2 * (g % 2) + 2, 0:T], ACT.Copy).then_inc(ev_act, 1)
                    ahead(U0[name] + 2 * g)
                    ahead(U0[name] + 2 * g + 1)

            for g in range(4):
                act.wait_ge(sem("x_pe0"), g + 1)
                A(h[:, 2 * g:2 * g + 2, :], ps[:, 2 * (g % 2):2 * (g % 2) + 2, 0:T], ACT.Copy).then_inc(ev_act, 1)

            def norm_act(i):
                if i == 0:
                    act.wait_ge(sem("eps_set"), 2)
                A(tiny[:, 2:3], tiny[:, 0:1], ACT.Sqrt).then_inc(sem("table"), 1)
                for m in range(4):
                    if i == 0:
                        act.wait_ge(ev_act, m + 1)
                    else:
                        act.wait_ge(ev_dve, 4 * (i - 1) + m + 1)
                    A(sq[:, 2 * m:2 * m + 2, :], h[:, 2 * m:2 * m + 2, :], ACT.Square).then_inc(sem("sq_ready"), 1)
                act.wait_ge(sem("ms_ready"), i + 1)
                act.wait_ge(sem("eps_set"), 2)
                if i:
                    act.wait_ge(sem("xn_done"), i)
                A(rs[:, :], ps[:, 4, 0:T], ACT.Sqrt, bias=tiny[:, 0:1]).then_inc(sem("rs_ready"), 1)

            norm_act(0)
            for u in range(RING):
                split(u)

            def upper(dst, src, ready, count):
                for half in range(2):
                    act.wait_ge(sem(ready), count + half + 1)
                    A(dst[:, 4 * half:4 * half + 4, :], src[:, 4 * half:4 * half + 4, :], ACT.Copy).then_inc(sem("xh_ready"), 1)

            upper(xh[0], mix[1], "mix_ready", 0)
            upper(xh[1], mix[0], "mix_ready", 2)
            evac8("r", R)
            act.wait_ge(sem("lora_h"), 1)
            A(hw[:, :], ps[0:LD, 5, 0:T], ACT.Tanh).then_inc(sem("lora_act"), 1)
            act.wait_ge(sem("lora_h"), 2)
            A(ha[:, :], ps[0:LI, 6, 0:T], ACT.Copy).then_inc(sem("lora_act"), 1)
            act.wait_ge(sem("lora_h"), 3)
            step(A(hg0[:, :], ps[:, 7, 0:T], ACT.Sigmoid))
            settle()
            A(hg1[:, :], ps[0:LG - P, 4, 0:T], ACT.Sigmoid).then_inc(sem("lora_act"), 1)
            upper(xh[0], mix[0], "mix_ready", 10)
            evac8("k", K)
            for n, (dst, bias) in enumerate([(Sg, "w0"), (Ai, "a0"), (Gt, None)]):
                if n == 1:
                    act.wait_ge(sem("kk_raw"), 1)
                    A(sq2[:, :, :], KK[:, :, :], ACT.Square).then_inc(sem("kksq"), 1)
                if n == 2:
                    act.wait_ge(sem("xl_pool"), 4)
                for g in range(4):
                    act.wait_ge(sem("up_pe"), 4 * n + g + 1)
                    if bias is None:
                        A(dst[:, 2 * g:2 * g + 2, :], ps[:, 2 * (g % 2):2 * (g % 2) + 2, 0:T], ACT.Copy).then_inc(ev_act, 1)
                        if g == 0:
                            act.wait_ge(sem("kk_sum"), 1)
                            A(kkr[:, 0, :], ps[0:H, 4, 0:T], ACT.Sqrt).then_inc(sem("kk_root"), 1)
                            act.wait_ge(sem("cs_ready"), 1)
                            A(E1[:, :, :], CSm[:, :, :], ACT.Exp, scale=-DECAY).then_inc(sem("e1_ready"), 1)
                        continue
                    step(A(dst[:, 2 * g, :], ps[:, 2 * (g % 2), 0:T], ACT.Sigmoid, bias=pv(bias, 2 * g)))
                    settle()
                    A(dst[:, 2 * g + 1, :], ps[:, 2 * (g % 2) + 1, 0:T], ACT.Sigmoid, bias=pv(bias, 2 * g + 1))\
                        .then_inc(ev_act, 1)
            act.wait_ge(sem("ex_ready"), 1)
            A(E2[:, :, :], CSm[:, :, :], ACT.Exp, scale=DECAY).then_inc(sem("e2_ready"), 1)
            A(E3[:, :, :], Sg[:, :, :], ACT.Exp, scale=-DECAY).then_inc(sem("e3_ready"), 1)
            for g in range(4):
                act.wait_ge(unit_used, U0["v"] + 2 * g + 2)
                A(V[:, 2 * g:2 * g + 2, :], ps[:, 2 * (g % 2):2 * (g % 2) + 2, 0:T], ACT.Copy).then_inc(ev_act, 1)
                ahead(U0["v"] + 2 * g)
                ahead(U0["v"] + 2 * g + 1)
                if g == 2:
                    act.wait_ge(sem("rk_sum"), 1)
                    A(t11[:, :, :].rearrange("p (b k) t -> p b (k t)", b=4), ps[:, 4:8, :], ACT.Copy).then_inc(sem("rk_copied"), 1)
            def bkt_copy(c):
                act.wait_ge(sem("bkT"), c + 1)
                A(BKT[:, c, :].rearrange("p (b n) -> p b n", b=2), ps[:, 4:6, :], ACT.Copy).then_inc(sem("bkt_act"), 1)

            act.wait_ge(sem("ar_ready"), 2)
            act.wait_ge(sem("bk_ready"), 2)
            bkt_copy(0)
            act.wait_ge(sem("rk_done"), 1)
            for q in range(TT):
                act.wait_ge(sem("vT"), q + 1)
                for c in range(2):
                    A(UV[HD:P, 2 * q + c, :].rearrange("p (b n) -> p b n", b=2), ps[HD * c:HD * c + HD, 2 * q:2 * q + 2, :],
                      ACT.Copy).then_inc(sem("v_copied"), 1)
            bkt_copy(2)
            for pair in range(NPAIR):
                for n in (0, 1, 2, 5, 7):
                    for s in range(2):
                        act.wait_ge(sem(f"inv_pe{s}"), 9 * pair + n + 1)
                        b = 4 * s + 2 * (n % 2)
                        if n == 0:
                            if pair:
                                act.wait_ge(sem(f"inv_pool{s}"), 2 * pair)
                            act.wait_ge(sem(f"inv_dve{s}"), 13 * pair + 1)
                            if pair == 0:
                                act.wait_ge(sem("bonus"), 1)
                            dst = Lr[s][:, :, :]
                        else:
                            if n == 1:
                                act.wait_ge(sem(f"inv_dve{s}"), 13 * pair + 3)
                            dst = DP[s][:, :, 0, :]
                        if n == 2:
                            src = ps[:, b:b + 2, :].rearrange("p b (k a n) -> p (b k) a n", a=2, n=C)[:, :, 0, :]
                            A(dst, src, ACT.Copy).then_inc(sem(f"inv_act{s}"), 1)
                        else:
                            A(dst.rearrange("p (b k) n -> p b k n", b=2),
                              ps[:, b:b + 2, 0:GW].rearrange("p b (k n) -> p b k n", n=C), ACT.Copy)\
                                .then_inc(sem(f"inv_act{s}"), 1)

            def quarter(src):
                return src.rearrange("p (k n) -> p k n", n=C)

            def gn_square(c):
                act.wait_ge(sem("yc"), c + 1)
                A(YQ[:, :, :], YC[:, :, :], ACT.Square).then_inc(sem("y_sq"), 1)

            def gn_sqrt(c):
                act.wait_ge(sem("var_pe"), c + 1)
                A(rst[:, C:2 * C], ps[0:H, 7, 0:C], ACT.Sqrt, bias=tiny[0:H, 1:2], scale=1.0 / HD).then_inc(sem("y_std"), 1)

            def gn_upper(c):
                act.wait_ge(sem("y_gated"), 2 * c + 2)
                A(yh[:, :, c * C:(c + 1) * C], YF[c % 2][:, :, :], ACT.Copy).then_inc(sem("yh_ready"), 1)

            for c in range(NCH):
                for half in range(2):
                    act.wait_ge(sem(f"xs_pe{half}"), c + 1)
                    A(XS[half][:, :, :], quarter(ps[:, 3 * half, 0:GW]), ACT.Copy).then_inc(sem(f"x_sb{half}"), 1)
                if c:
                    gn_square(c - 1)
                for half in range(2):
                    act.wait_ge(sem(f"u_pe{half}"), c + 1)
                    o = UV[0:HD, c, half * 512:half * 512 + 512].rearrange("p (k a n) -> p k a n", a=2, n=HD)[:, :, 0, :]
                    A(o, quarter(ps[0:HD, 3 * half + 1, 0:GW]), ACT.Copy).then_inc(sem(f"u_even{half}"), 1)
                if c:
                    gn_sqrt(c - 1)
                for half in range(2):
                    act.wait_ge(sem(f"y_pe{half}"), c + 1)
                    A(AR[:, half * 4:half * 4 + 4, c, 1, :], quarter(ps[:, 3 * half + 1, 0:GW]), ACT.Copy)\
                        .then_inc(sem(f"y_copied{half}"), 1)
                if c >= 2:
                    gn_upper(c - 2)
            gn_square(NCH - 1)
            gn_upper(NCH - 2)
            gn_sqrt(NCH - 1)
            gn_upper(NCH - 1)
            for j in range(8):
                ahead(U0["o0"] + j)

            def x_parts(n):
                for m in range(2):
                    act.wait_ge(sem("xn_ready"), 2 * n + m + 1)
                    A(xh[0][:, 4 * m:4 * m + 4, :], xn[:, 4 * m:4 * m + 4, :], ACT.Copy).then_inc(sem("xh_ready"), 1)

            def mlp_act(n1, n2, base_):
                def turn(i, gg, steady):
                    act.wait_ge(unit_used, i * 4 + (U0[n1] + 2 * gg + 2))
                    if steady:
                        act.wait_ge(sem("sq_used"), i * 2 + (base_ + gg - 1))
                    A(rl[:, gg, :, :], ps[:, 2 * gg:2 * gg + 2, 0:T], ACT.Relu).then_inc(ev_act, 1)
                    for j in range(2):
                        u = U0[n1] + 2 * gg + j + RING
                        act.wait_ge(raw_in[2 * gg + j], i * 16 + 16 * (u // RING + 1))
                        act.wait_ge(unit_used, i * 4 + (u - RING + 1))
                        A(whi[:, 2 * gg + j, :], raw[:, 2 * gg + j, :], ACT.Copy).then_inc(hi_ready, 1)
                    act.wait_ge(ev_act, i * 2 + (EV0[n1] + gg + 1))
                    A(hh[:, ds(i * 4 + 2 * gg, 2), :], rl[:, gg, :, :], ACT.Square).then_inc(sem("hh_ready"), 1)

                for gg in range(2):
                    turn(0, gg, False)
                with act.Fori(1, 8) as i:
                    for gg in range(2):
                        turn(i, gg, True)
                with act.Fori(0, 3) as i:
                    for j in range(8):
                        u = U0[n2] + j + RING
                        act.wait_ge(raw_in[j % RING], i * 32 + 16 * (u // RING + 1))
                        act.wait_ge(unit_used, i * 8 + (u - RING + 1))
                        A(whi[:, j % RING, :], raw[:, j % RING, :], ACT.Copy).then_inc(hi_ready, 1)
                for j in range(24, 32):
                    ahead(U0[n2] + j)

            norm_act(1)
            x_parts(0)
            mlp_act("a1", "a2", 0)
            norm_act(2)
            x_parts(1)
            evac8("q", Qn)
            act.wait_ge(ev_act, EV0["q"] + 4)
            A(qss[:, :, :], Qn[:, :, :], ACT.Square).then_inc(sem("qsq"), 1)
            dst = [kv[:, 0, :, :], kv[:, 1, :, :], kv[:, 2, :, :], vt[:, 0, :, :], kv[:, 3, :, :], vt[:, 1, :, :]]
            for g in range(6):
                act.wait_ge(unit_used, U0["kv"] + 2 * g + 2)
                A(dst[g], ps[:, 2 * (g % 2):2 * (g % 2) + 2, 0:T], ACT.Copy).then_inc(ev_act, 1)
                ahead(U0["kv"] + 2 * g)
                ahead(U0["kv"] + 2 * g + 1)
            act.wait_ge(ev_act, EV0["kv"] + 6)
            A(ksq[:, :, :, :], kv[:, 2:4, :, :], ACT.Square).then_inc(sem("ksq_r"), 1)
            act.wait_ge(sem("gate_pe"), 1)
            A(gat[:, :, :], ps[:, 4, 0:128].rearrange("p (q n) -> p q n", q=TT)[:, :, 0:NG], ACT.Sigmoid)\
                .then_inc(sem("gates_r"), 1)
            act.wait_ge(sem("pe_col"), 1)
            act.wait_ge(sem("qn_pe"), 1)
            step(A(qrs[:, 0:4, :].rearrange("p (b k) t -> p b (k t)", b=2), ps[:, 6:8, :], ACT.Sqrt, bias=tiny[:, 0:1], scale=1.0 / HD))
            A(qrs[:, 4:8, :].rearrange("p (b k) t -> p b (k t)", b=2), ps[:, 0:2, :], ACT.Sqrt, bias=tiny[:, 0:1], scale=1.0 / HD)\
                .then_inc(sem("qrs_r"), 1)
            act.wait_ge(sem("kn_pe"), 1)
            A(krs[:, :, :, :].rearrange("p b k t -> p b (k t)"), ps[:, 2:4, :], ACT.Sqrt, bias=tiny[:, 0:1], scale=1.0 / HD)\
                .then_inc(sem("krs_r"), 1)
            act.wait_ge(sem("gelu_in"), 1)
            A(gu[:, :, :], gu[:, :, :], ACT.Sigmoid, scale=GELU_A).then_inc(sem("gelu_sig"), 1)
            act.wait_ge(sem("cmp2_pe"), 1)
            act.wait_ge(sem("hid_k"), 1)
            A(gu[:, 0, :], ps[:, 5, 0:HKV * NB], ACT.Square).then_inc(sem("kcsq"), 1)
            for a in range(4):
                o = vblk[32 * a:32 * a + 32, :, a * HD:(a + 1) * HD]
                if a == 0:
                    act.wait_ge(sem("vblk_0"), 1)
                i_ = ps[32 * a:32 * a + 32, 5, 128:128 + HKV * HD].rearrange("p (j n) -> p j n", n=HD)
                A(o, i_, ACT.Copy).then_inc(sem("vblk_r"), 1)
            act.wait_ge(sem("kc_pe"), 1)
            A(gu[:, 1, :], ps[:, 4, 0:HKV * NB], ACT.Sqrt, bias=tiny[:, 0:1], scale=1.0 / HD).then_inc(sem("kcrs"), 1)
            act.wait_ge(sem("csub"), 1)
            A(Sc[:, :, :, 0:16], Sc[:, :, :, 0:16], ACT.Exp).then_inc(sem("cexp"), 1)
            act.wait_ge(sem("pct_pe"), 1)
            A(PcT[:, :, :, :].rearrange("p q j n -> p q (j n)"), ps[:, 4:6, :], ACT.Copy).then_inc(sem("pct_r"), 1)
            items = [(j, q, b) for j in range(HKV) for q in range(TT) for b in range(2)]

            def exps(n):
                j, q, b = items[n]
                w = (q + 1) * P
                act.wait_ge(sem("mx_ready"), n + 1)
                for i in range(4):
                    hd = 4 * j + i
                    o = A(SB[:, n % 2, i, 0:w], SB[:, n % 2, i, 0:w], ACT.Exp, bias=nmx[:, n % 2, i:i + 1],
                          accum_out=den[:, q, b, hd:hd + 1])
                    step(o)
                settle()
                act.sem_inc(sem("p_ready"), 1)

            def pt_copy(n):
                j, q, b = items[n]
                act.wait_ge(sem("t_pe"), n + 1)
                if n >= 2:
                    act.wait_ge(sem("pv_pe"), n - 1)
                A(PT[:, n % 2, :, 0:q + 1, :].rearrange("p i s t -> p s i t"),
                  ps[:, 4:5 + q, :].rearrange("p s (i t) -> p s i t", t=P), ACT.Copy).then_inc(sem("pt_read"), 1)

            for n in range(len(items)):
                exps(n)
                if n >= 1:
                    pt_copy(n - 1)
            pt_copy(len(items) - 1)
            act.wait_ge(sem("oT_pe"), 1)
            for half in range(2):
                A(xh[1][:, 4 * half:4 * half + 4, :].rearrange("p (b k) t -> p b (k t)", b=2),
                  ps[:, 4 + 2 * half:6 + 2 * half, :], ACT.Copy).then_inc(sem("xh_ready"), 1)
            for j in range(8):
                ahead(U0["o1"] + j)
            norm_act(3)
            x_parts(2)
            mlp_act("b1", "b2", 16)
            for q in range(TT):
                act.wait_ge(sem("fin_pe"), q + 1)
                A(otok[:, q, :].rearrange("p (b n) -> p b n", b=2), ps[:, 4 + 2 * q:6 + 2 * q, :], ACT.Copy)\
                    .then_inc(sem("out_ready"), 1)

        @block.vector
        def _(dve):
            v = nc.vector
            down = sem("dve_step")
            cnt = [0]

            def step(ins):
                cnt[0] += 1
                ins.then_inc(down, 1)

            def settle():
                dve.wait_ge(down, cnt[0])

            def rest(slot, hi_count):
                dve.wait_ge(hi_ready, hi_count)
                v.tensor_tensor(wlo[:, slot, :], raw[:, slot, :], whi[:, slot, :].bitcast(f32), ALU.subtract)\
                    .then_inc(lo_ready, 1)

            def ahead(u):
                if u + RING < NU:
                    rest((u + RING) % RING, u + RING + 1)

            v.memset(tiny[:, 0:1], EPS).then_inc(sem("eps_set"), 1)
            v.memset(tiny[:, 1:2], GN_EPS).then_inc(sem("eps_set"), 1)
            dve.wait_ge(sem("par_t"), 1)
            v.tensor_copy(par[:, 0:NPAR], ps[:, 5, 0:NPAR]).then_inc(sem("par_r"), 1)
            dve.wait_ge(sem("par_r"), 1)

            def lower(dst, src, hi, x):
                for half in range(2):
                    part = slice(4 * half, 4 * half + 4)
                    dve.wait_ge(sem("xh_ready"), XH0[x] + half + 1)
                    v.tensor_tensor(dst[:, part, :], src[:, part, :], hi[:, part, :].bitcast(f32), ALU.subtract)\
                        .then_inc(sem("xl_dve"), 1)

            def norm_dve(i, g):
                if i == 0:
                    dve.wait_ge(ev_act, 4)
                dve.wait_ge(sem("rs_ready"), i + 1)
                step(v.reciprocal(ri[:, :], rs[:, :]))
                settle()
                for k in range(FT):
                    step(v.scalar_tensor_tensor(xn[:, k, :], h[:, k, :], pv(g, k), ri[:, :], ALU.mult, ALU.mult))
                    if k % 4 == 3:
                        settle()
                        if i:
                            dve.sem_inc(sem("xn_ready"), 1)
                dve.sem_inc(sem("xn_done"), 1)
                if i:
                    lower(xl[0], xn, xh[0], ["a", "nsa", "b"][i - 1])

            norm_dve(0, "mix0")
            step(v.tensor_tensor(dx[:, :, 1:T], xn[:, :, 0:T - 1], xn[:, :, 1:T], ALU.subtract))
            step(v.tensor_scalar(dx[:, :, 0:1], xn[:, :, 0:1], -1.0, None, ALU.mult))
            settle()

            def mixing(mu, dst):
                for k in range(FT):
                    step(v.scalar_tensor_tensor(dst[:, k, :], dx[:, k, :], pv(f"mu{mu}", k), xn[:, k, :], ALU.mult, ALU.add))
                    if k % 4 == 3:
                        settle()
                        dve.sem_inc(sem("mix_ready"), 1)

            def ahead2(name, j):
                ahead(U0[name] + j)
                ahead(U0[name] + j + 1)

            mixing(0, mix[1])
            lower(xl[0], mix[1], xh[0], "r")
            for u in range(RING):
                rest(u, u + 1)
            mixing(2, mix[0])
            mixing(1, mix[1])
            ahead2("r", 0)
            dve.wait_ge(sem("xh_ready"), XH0["k"] + 2)
            dve.wait_ge(sem("xl_pool"), 2)
            mixing(4, mix[0])
            ahead2("r", 2)
            ahead2("r", 4)
            ahead2("r", 6)
            dve.wait_ge(sem("lora_h"), 1)
            mixing(5, mix[1])
            dve.wait_ge(sem("lora_h"), 2)
            mixing(3, mix[0])
            for j in range(8):
                ahead(U0["k"] + j)

            def wide(name):
                return par[:, pcol[name]:pcol[name] + FT].unsqueeze(2).broadcast_to([P, FT, T])

            dve.wait_ge(sem("lora_h"), 3)
            dve.wait_ge(ev_act, EV0["k"] + 4)
            v.tensor_tensor(KK[:, :, :], K[:, :, :], wide("k_k"), ALU.mult).then_inc(sem("kk_raw"), 1)
            dve.wait_ge(ev_act, EV0["up"] + 4)
            dve.wait_ge(sem("cst_rest"), 16)
            for k in range(FT):
                step(v.tensor_tensor_scan(CSm[:, k, :], cc("chunk"), Sg[:, k, :], 0.0, ALU.mult, ALU.add))
            settle()
            dve.sem_inc(sem("cs_ready"), 1)
            dve.wait_ge(ev_act, EV0["up"] + 8)
            dve.wait_ge(sem("kk_raw"), 1)
            for k in range(FT):
                step(v.tensor_scalar(t11[:, k, :], Ai[:, k, :], 1.0, pv("k_a", k), ALU.subtract, ALU.mult))
            settle()
            step(v.scalar_tensor_tensor(K[:, :, :], t11[:, :, :], 1.0, K[:, :, :], ALU.add, ALU.mult))
            settle()
            dve.wait_ge(sem("kk_root"), 1)
            step(v.tensor_scalar(kkr[:, 1, :], kkr[:, 0, :], 1e-12, None, ALU.max))
            settle()
            v.reciprocal(kkr[:, 1, :], kkr[:, 1, :]).then_inc(sem("kk_inv"), 1)
            for k in range(FT):
                step(v.scalar_tensor_tensor(t11[:, k, :], R[:, k, :], pv("r_k", k), K[:, k, :], ALU.mult, ALU.mult))
            settle()
            dve.sem_inc(sem("rk"), 1)
            ch = lambda x: x[:, :, :].rearrange("p k (c n) -> p (k c) n", n=C)
            arv = lambda x, n: x[:, :, :, n, :].rearrange("p k c n -> p (k c) n")
            dve.wait_ge(ev_act, EV0["up"] + 12)
            dve.wait_ge(sem("e1_ready"), 1)
            step(v.tensor_tensor(arv(AR, 1), ch(R), ch(E1), ALU.mult))
            step(v.tensor_copy(PC[:, :, :], E1[:, :, :].rearrange("p k (c n) -> p k c n", n=C)[:, :, :, C - 1]))
            dve.wait_ge(sem("kk_spread"), 1)
            v.tensor_tensor(KK[:, :, :].rearrange("p (b k) t -> p b (k t)", b=4), KK[:, :, :].rearrange("p (b k) t -> p b (k t)", b=4),
                            ps[:, 4:8, :], ALU.mult).then_inc(sem("kkn_used"), 1)
            ahead2("v", 0)
            dve.wait_ge(sem("e2_ready"), 1)
            step(v.tensor_tensor(arv(BK, 1), ch(K), ch(E2), ALU.mult))
            settle()
            dve.sem_inc(sem("rk_done"), 1)
            dve.sem_inc(sem("bk_ready"), 1)
            dve.sem_inc(sem("ar_ready"), 1)
            dve.wait_ge(sem("e3_ready"), 1)
            dve.wait_ge(sem("kkn_used"), 1)
            step(v.scalar_tensor_tensor(arv(AR, 0), ch(KK), -1.0, ch(E3), ALU.mult, ALU.mult))
            settle()
            dve.sem_inc(sem("ar_ready"), 1)
            ahead2("v", 2)
            ahead2("v", 4)
            ahead2("v", 6)
            dve.wait_ge(sem("bk_ready"), 2)
            for n, c in enumerate([1, 3]):
                dve.wait_ge(sem("bkT"), c + 1)
                v.tensor_copy(BKT[:, c, :].rearrange("p (b n) -> p b n", b=2), ps[:, 6:8, :]).then_inc(sem("bkt_dve"), 1)

            def mask_g(half):
                for n in range(8):
                    dve.wait_ge(sem("g_done"), 8 * half + n + 1)
                    if n == 0 and half == 0:
                        dve.wait_ge(sem("bk_ready"), 2)
                        dve.wait_ge(sem("ar_ready"), 2)
                    v.tensor_tensor(Gs[half][:, n, :, :], ps[:, n, :].rearrange("p (c n) -> p c n", c=NCH),
                                    cc("gmask").unsqueeze(1).broadcast_to([P, NCH, 2 * C]), ALU.mult)\
                        .then_inc(sem("g_masked"), 1)

            mask_g(0)
            for pair in range(NPAIR):
                for n in (0, 1, 2, 3, 4, 6, 8):
                    for s in range(2):
                        done = sem(f"inv_dve{s}")
                        dve.wait_ge(sem(f"inv_pe{s}"), 9 * pair + n + 1)
                        b = 4 * s + 2 * (n % 2)
                        if n in (2, 3):
                            wide = ps[:, b:b + 2, :].rearrange("p b (k a n) -> p (b k) a n", a=2, n=C)
                            power, more = wide[:, :, 0, :], wide[:, :, 1, :]
                        else:
                            power = more = ps[:, b:b + 2, 0:GW].rearrange("p b (k n) -> p b k n", n=C)

                        def sp(x):
                            return x if n in (2, 3) else x.rearrange("p (b k) n -> p b k n", b=2)

                        def m(name):
                            return cc(name).unsqueeze(1).broadcast_to([P, NP_, C])

                        prod = DP[s][:, :, 1, :]
                        if n in (1, 2):
                            dve.wait_ge(sem(f"inv_act{s}"), 5 * pair + n + 1)
                        if n == 0:
                            if pair == 0 and s == 0:
                                dve.wait_ge(sem("bonus"), 1)
                            mask = cc("lmask16").unsqueeze(1).unsqueeze(1).broadcast_to([P, 2, NP_ // 2, C])
                            v.tensor_tensor(sp(LT[s][:, :, :]), power, mask, ALU.mult).then_inc(done, 1)
                            dve.wait_ge(done, 13 * pair + 1)
                            v.transpose(DP[s][:, :, 0, :], LT[s][:, :, :]).then_inc(done, 1)
                            dve.wait_ge(done, 13 * pair + 2)
                            v.tensor_tensor(prod, DP[s][:, :, 0, :], m("eye64"), ALU.add).then_inc(done, 1)
                        elif n == 1:
                            v.transpose(LT[s][:, :, :], DP[s][:, :, 0, :]).then_inc(done, 1)
                        elif n in (2, 3):
                            v.transpose(LT[s][:, :, :], DP[s][:, :, 0, :] if n == 2 else power).then_inc(done, 1)
                            v.tensor_tensor(prod, prod, more, ALU.add).then_inc(done, 1)
                        elif n in (4, 6):
                            v.tensor_tensor(sp(prod), sp(prod), more, ALU.add).then_inc(done, 1)
                            dve.wait_ge(done, 13 * pair + {4: 9, 6: 11}[n])
                            v.transpose(LT[s][:, :, :], prod).then_inc(done, 1)
                        else:
                            p0 = (2 * pair + s) * NP_
                            v.tensor_tensor(sp(Rinv[:, p0:p0 + NP_, :]), sp(prod), more, ALU.add).then_inc(done, 1)
            mask_g(1)

            def gn_center(c):
                dve.wait_ge(sem("mean_pe"), c + 1)
                v.scalar_tensor_tensor(YC[:, :, :], ps[:, 6, :].rearrange("p (k n) -> p k n", n=C), -1.0 / HD,
                                       AR[:, :, c, 1, :], ALU.mult, ALU.add).then_inc(sem("yc"), 1)

            def gn_rstd(c):
                dve.wait_ge(sem("y_std"), c + 1)
                v.reciprocal(rst[:, 0:C], rst[:, C:2 * C]).then_inc(sem("y_rstd"), 1)

            def gn_scale(c):
                dve.wait_ge(sem("rstd_pe"), c + 1)
                if c >= 2:
                    dve.wait_ge(sem("yh_ready"), c - 1)
                    dve.wait_ge(sem("yl_ready"), c - 1)
                v.tensor_tensor(YF[c % 2][:, :, :], YC[:, :, :], ps[:, 6, :].rearrange("p (k n) -> p k n", n=C), ALU.mult)\
                    .then_inc(sem("y_scaled"), 1)

            for c in range(NCH):
                if c >= 2:
                    gn_scale(c - 2)
                if c:
                    gn_center(c - 1)
                for half in range(2):
                    dve.wait_ge(sem(f"u_pe{half}"), c + 1)
                    o = UV[0:HD, c, half * 512:half * 512 + 512].rearrange("p (k a n) -> p k a n", a=2, n=HD)[:, :, 1, :]
                    v.tensor_copy(o, ps[0:HD, 3 * half + 2, 0:GW].rearrange("p (k n) -> p k n", n=C))\
                        .then_inc(sem(f"u_odd{half}"), 1)
                if c < NCH - 1:
                    for half in range(2):
                        dve.wait_ge(sem(f"s_pe{half}"), c + 1)
                        s_in = ps[:, 3 * half, 0:GW].rearrange("p (k n) -> p k n", n=C)
                        pc = PC[:, half * 4:half * 4 + 4, c:c + 1].broadcast_to([P, FT // 2, C])
                        if c:
                            step(v.tensor_tensor(STt[half][:, :, :], s_in, ST[half][(c - 1) % 2][:, :, :], ALU.add))
                            settle()
                            s_in = STt[half][:, :, :]
                        if c >= 2:
                            dve.wait_ge(sem(f"y_pe{half}"), c)
                        v.tensor_tensor(ST[half][c % 2][:, :, :], s_in, pc, ALU.mult).then_inc(sem(f"st_ready{half}"), 1)
                        dve.wait_ge(sem(f"st_ready{half}"), c + 1)
                if c:
                    gn_rstd(c - 1)
            gn_scale(NCH - 2)
            gn_center(NCH - 1)
            gn_rstd(NCH - 1)
            gn_scale(NCH - 1)

            def residual(name):
                for g in range(4):
                    dve.wait_ge(unit_used, U0[name] + 2 * g + 2)
                    v.tensor_tensor(h[:, 2 * g:2 * g + 2, :], h[:, 2 * g:2 * g + 2, :],
                                    ps[:, 2 * (g % 2):2 * (g % 2) + 2, 0:T], ALU.add).then_inc(ev_dve, 1)
                    ahead(U0[name] + 2 * g)
                    ahead(U0[name] + 2 * g + 1)

            def mlp_dve(n1, n2, base_):
                def turn(i, gg, steady):
                    dve.wait_ge(ev_act, i * 2 + (EV0[n1] + gg + 1))
                    v.tensor_tensor(s2[:, gg, :, :], rl[:, gg, :, :], rl[:, gg, :, :], ALU.mult).then_inc(sem("s2_ready"), 1)
                    dve.wait_ge(sem("hh_ready"), i * 2 + (base_ + gg + 1))
                    dve.wait_ge(sem("s2_ready"), i * 2 + (base_ + gg + 1))
                    dve.sem_inc(sem("sq_used"), 1)
                    v.tensor_tensor(hl[:, ds(i * 4 + 2 * gg, 2), :], s2[:, gg, :, :],
                                    hh[:, ds(i * 4 + 2 * gg, 2), :].bitcast(f32), ALU.subtract).then_inc(sem("hid_ready"), 1)
                    for j in range(2):
                        u = U0[n1] + 2 * gg + j + RING
                        rest(2 * gg + j, i * 4 + (u + 1))

                with dve.Fori(0, 8) as i:
                    for gg in range(2):
                        turn(i, gg, True)
                for g in range(4):
                    for j in range(8):
                        ahead(U0[n2] + 8 * g + j)
                    dve.wait_ge(unit_used, U0[n2] + 8 * g + 8)
                    v.tensor_tensor(h[:, 2 * g:2 * g + 2, :], h[:, 2 * g:2 * g + 2, :],
                                    ps[:, 2 * (g % 2):2 * (g % 2) + 2, 0:T], ALU.add).then_inc(ev_dve, 1)

            residual("o0")
            norm_dve(1, "mlp0")
            mlp_dve("a1", "a2", 0)
            norm_dve(2, "mix1")

            for j in range(8):
                ahead(U0["q"] + j)
            for j in range(12):
                ahead(U0["kv"] + j)
            dve.wait_ge(sem("gate_pe"), 1)
            v.tensor_copy(pec[:, :], ps[:, 5, 0:2 * CB]).then_inc(sem("pe_col"), 1)
            dve.wait_ge(sem("pe_col"), 1)
            dve.wait_ge(ev_act, EV0["kv"] + 6)
            for b in range(2):
                for j in range(HKV):
                    e, m = j % 2, j // 2
                    for half in range(2):
                        src = kv[HD * e:HD * e + HD, b, m, CS * half:CS * half + CS * NB].rearrange("p (n l) -> p l n", l=CS)
                        emb = pec[HD * e:HD * e + HD, b * CB + CS * half:b * CB + CS * half + CS].unsqueeze(2)\
                            .broadcast_to([HD, CS, NB])
                        step(v.tensor_tensor(Zc[HD * half:HD * half + HD, b, :, j * NB:(j + 1) * NB], src, emb, ALU.add))
                        settle()
            dve.sem_inc(sem("zc"), 1)
            dve.wait_ge(sem("qrs_r"), 1)
            step(v.reciprocal(qrs[:, :, :], qrs[:, :, :]))
            settle()
            step(v.scalar_tensor_tensor(Qn[:, :, :], Qn[:, :, :], pv("qn"), qrs[:, :, :], ALU.mult, ALU.mult))
            settle()
            v.tensor_scalar(Qn[:, :, :], Qn[:, :, :], HD ** -0.5, None, ALU.mult).then_inc(sem("q_ready"), 1)
            dve.wait_ge(sem("cmp_pe"), 1)
            step(v.tensor_copy(hid[:, :, :], ps[:, 4, 0:128].rearrange("p (b n) -> p b n", b=2)[:, :, 0:HKV * NB]))
            settle()
            step(v.tensor_tensor(gu[:, :, :], hid[:, :, :], hid[:, :, :], ALU.mult))
            settle()
            step(v.tensor_scalar(gu[:, :, :], gu[:, :, :], GELU_B, 1.0, ALU.mult, ALU.add))
            settle()
            v.tensor_tensor(gu[:, :, :], gu[:, :, :], hid[:, :, :], ALU.mult).then_inc(sem("gelu_in"), 1)
            v.memset(hpad[:, :, :, :], 0.0).then_inc(sem("hpad_0"), 1)
            v.memset(vblk[:, :, :], 0.0).then_inc(sem("vblk_0"), 1)
            v.memset(Sc[:, :, :, :], 0.0).then_inc(sem("sc_0"), 1)
            dve.wait_ge(sem("gelu_sig"), 1)
            step(v.tensor_tensor(hid[:, :, :], hid[:, :, :], gu[:, :, :], ALU.mult))
            dve.wait_ge(sem("hpad_0"), 1)
            settle()
            step(v.tensor_copy(hpad[:, :, :, 0:NB], hid[:, 1, :].rearrange("p (j n) -> p j n", n=NB).unsqueeze(2)
                               .broadcast_to([P, HKV, 4, NB])))
            settle()
            dve.sem_inc(sem("hid_k"), 1)
            dve.wait_ge(sem("krs_r"), 1)
            step(v.reciprocal(krs[:, :, :, :], krs[:, :, :, :]))
            settle()
            for b in range(2):
                for j in range(HKV):
                    e, m = j % 2, j // 2
                    src = slice(HD * e, HD * e + HD)
                    for half in range(2):
                        g = par[src, pcol[f"kn{b + 1}"]:pcol[f"kn{b + 1}"] + 1]
                        step(v.scalar_tensor_tensor(kd[HD * half:HD * half + HD, b, j, :], kv[src, 2 + b, m, :], g,
                                                    krs[src, b, m, :], ALU.mult, ALU.mult))
                        settle()
            dve.sem_inc(sem("kd_ready"), 1)
            dve.wait_ge(sem("kcrs"), 1)
            step(v.reciprocal(gu[:, 1, :], gu[:, 1, :]))
            settle()
            v.scalar_tensor_tensor(kcm[:, :], ps[:, 5, 0:HKV * NB], pv("kn0"), gu[:, 1, :], ALU.mult, ALU.mult)\
                .then_inc(sem("kcm_r"), 1)
            dve.wait_ge(sem("sc_0"), 1)
            adc = cc("adc").rearrange("p (q h n) -> p q h n", q=TT, n=16)
            for q in range(TT):
                dve.wait_ge(sem("sc_pe"), q + 1)
                for e in range(2):
                    o = Sc[:, q, :, 0:16].rearrange("p (k a) n -> p k a n", a=2)[:, :, e, 0:NB]
                    a_ = adc[:, q, :, :].rearrange("p (k a) n -> p k a n", a=2)[:, :, e, 0:NB]
                    i_ = ps[:, [6, 0][q] + e, 0:FT * 16].rearrange("p (k n) -> p k n", n=16)[:, :, 0:NB]
                    step(v.tensor_tensor(o, i_, a_, ALU.add))
            settle()
            step(v.tensor_reduce(csm[:, 0, :, :], Sc[:, :, :, 0:NB], AXX, ALU.max))
            settle()
            step(v.tensor_scalar(csm[:, 0, :, :], csm[:, 0, :, :], FLOOR, None, ALU.max))
            settle()
            cb = lambda n: csm[:, n, :, :].unsqueeze(3).broadcast_to([P, TT, H, NB])
            v.tensor_tensor(Sc[:, :, :, 0:NB], Sc[:, :, :, 0:NB], cb(0), ALU.subtract).then_inc(sem("csub"), 1)
            dve.wait_ge(sem("cexp"), 1)
            step(v.tensor_reduce(csm[:, 1, :, :], Sc[:, :, :, 0:NB], AXX, ALU.add))
            settle()
            step(v.tensor_scalar(csm[:, 1, :, :], csm[:, 1, :, :], 1e-30, None, ALU.max))
            settle()
            step(v.reciprocal(csm[:, 2, :, :], csm[:, 1, :, :]))
            settle()
            gv = gat[:, :, :].rearrange("p q (h b) -> p q h b", b=3)
            dve.wait_ge(sem("gates_r"), 1)
            step(v.tensor_tensor(csm[:, 3, :, :], csm[:, 2, :, :], gv[:, :, :, 0], ALU.mult))
            settle()
            step(v.tensor_tensor(Sc[:, :, :, 0:NB], Sc[:, :, :, 0:NB], cb(3), ALU.mult))
            step(v.memset(Sc[:, :, :, NB:16], 0.0))
            settle()
            dve.sem_inc(sem("pc_ready"), 1)

            items = [(j, q, b) for j in range(HKV) for q in range(TT) for b in range(2)]
            dist = cc("dist")

            def soft(n):
                j, q, b = items[n]
                w = (q + 1) * P
                d = dist[:, 0:P] if q == 0 else dist[:, P:P + T]
                dve.wait_ge(sem("s_pe2"), n + 1)
                if n >= 2:
                    dve.wait_ge(sem("t_pe"), n - 1)
                for i in range(4):
                    step(v.scalar_tensor_tensor(SB[:, n % 2, i, 0:w], d, -SLOPES[4 * j + i],
                                                ps[:, 2 * (n % 2) + i % 2, (i // 2) * T:(i // 2) * T + w], ALU.mult, ALU.add))
                settle()
                dve.sem_inc(sem("s_read"), 1)
                step(v.tensor_reduce(nmx[:, n % 2, :], SB[:, n % 2, :, 0:w], AXX, ALU.max))
                settle()
                v.tensor_scalar(nmx[:, n % 2, :], nmx[:, n % 2, :], -1.0, None, ALU.mult).then_inc(sem("mx_ready"), 1)

            def combine(g):
                j, q = g // 2, g % 2
                hs = slice(4 * j, 4 * j + 4)
                dve.wait_ge(sem("p_ready"), 2 * g + 2)
                step(v.tensor_scalar(cof[:, q, :, hs], den[:, q, :, hs], 1e-30, None, ALU.max))
                settle()
                step(v.reciprocal(cof[:, q, :, hs], cof[:, q, :, hs]))
                settle()
                step(v.tensor_tensor(cof[:, q, :, hs], cof[:, q, :, hs],
                                     gv[:, q, hs, 1:3].rearrange("p h b -> p b h"), ALU.mult))
                settle()
                dve.wait_ge(sem("pv_pe"), 2 * g + 2)
                for b in range(2):
                    step(v.tensor_tensor(o1[:, b, :].rearrange("p (i n) -> p i n", n=HD),
                                         ps[:, 6 + g % 2, b * GW:(b + 1) * GW].rearrange("p (i n) -> p i n", n=HD),
                                         cof[:, q, b, hs].unsqueeze(2).broadcast_to([P, 4, HD]), ALU.mult))
                settle()
                dve.sem_inc(sem("o_done"), 1)
                step(v.tensor_tensor(Ot[:, q, j * GW:(j + 1) * GW], o1[:, 0, :], o1[:, 1, :], ALU.add))

            for n in range(len(items)):
                soft(n)
                if n >= 3 and n % 2 == 1:
                    combine((n - 3) // 2)
            combine(7)
            dve.wait_ge(sem("oc_pe"), 1)
            settle()
            v.tensor_tensor(Ot[:, :, :].rearrange("p q (b n) -> p (q b) n", b=2), ps[:, 0:4, :],
                            Ot[:, :, :].rearrange("p q (b n) -> p (q b) n", b=2), ALU.add).then_inc(sem("ot_ready"), 1)
            for half in range(2):
                part = slice(4 * half, 4 * half + 4)
                dve.wait_ge(sem("xh_ready"), XH0["o1"] + half + 1)
                v.tensor_tensor(xl[1][:, part, :].rearrange("p (b k) t -> p b (k t)", b=2), ps[:, 4 + 2 * half:6 + 2 * half, :],
                                xh[1][:, part, :].bitcast(f32).rearrange("p (b k) t -> p b (k t)", b=2), ALU.subtract)\
                    .then_inc(sem("xl_dve"), 1)
            residual("o1")
            norm_dve(3, "mlp1")
            mlp_dve("b1", "b2", 16)

        @block.gpsimd
        def _(pool):
            g = nc.gpsimd

            def lower(dst, src, hi, x):
                for half in range(2):
                    part = slice(4 * half, 4 * half + 4)
                    pool.wait_ge(sem("xh_ready"), XH0[x] + half + 1)
                    g.tensor_tensor(dst[:, part, :], src[:, part, :], hi[:, part, :].bitcast(f32), ALU.subtract)\
                        .then_inc(sem("xl_pool"), 1)

            lower(xl[1], mix[0], xh[1], "k")
            lower(xl[0], mix[0], xh[0], "v")
            pool.wait_ge(sem("cs_ready"), 1)
            g.tensor_tensor(Sg[:, :, :], CSm[:, :, :], Sg[:, :, :], ALU.subtract).then_inc(sem("ex_ready"), 1)
            pool.wait_ge(sem("kkn_used"), 1)
            g.tensor_tensor(Ai[:, :, :], KK[:, :, :], Ai[:, :, :], ALU.mult).then_inc(sem("b_ready"), 1)
            pool.wait_ge(sem("e2_ready"), 1)
            pool.wait_ge(sem("b_ready"), 1)
            g.tensor_tensor(BK[:, :, :, 0, :].rearrange("p k c n -> p (k c) n"),
                            Ai[:, :, :].rearrange("p k (c n) -> p (k c) n", n=C),
                            E2[:, :, :].rearrange("p k (c n) -> p (k c) n", n=C), ALU.mult).then_inc(sem("bk_ready"), 1)
            pool.wait_ge(sem("bk_ready"), 2)
            pool.wait_ge(sem("rk_done"), 1)
            g.memset(UV[0:HD, :, :], 0.0).then_inc(sem("u_zero"), 1)
            pool.wait_ge(sem("rk_copied"), 1)
            pool.wait_ge(ev_act, EV0["v"] + 4)
            g.tensor_tensor(t11[:, :, :], t11[:, :, :], V[:, :, :], ALU.mult).then_inc(sem("bonus"), 1)
            pool.wait_ge(sem("bonus"), 1)
            for pair in range(NPAIR):
                for s in range(2):
                    pool.wait_ge(sem(f"inv_act{s}"), 5 * pair + 1)
                    if pair:
                        pool.wait_ge(sem(f"inv_pe{s}"), 9 * pair)
                    for dst, name in ((E32[s], "lmask32"), (E64[s], "lmask64")):
                        g.tensor_tensor(dst[:, :, :], Lr[s][:, :, :], cc(name).unsqueeze(1).broadcast_to([P, NP_, C]), ALU.mult)\
                            .then_inc(sem(f"inv_pool{s}"), 1)
            def wide(name):
                return par[:, pcol[name]:pcol[name] + FT].unsqueeze(2).broadcast_to([P, FT, T])

            fold = sem("gate_folded")
            g.tensor_tensor(t11[:, :, :], t11[:, :, :], wide("ln_b"), ALU.add).then_inc(fold, 1)
            pool.wait_ge(fold, 1)
            g.tensor_tensor(t11[:, :, :], t11[:, :, :], Gt[:, :, :], ALU.mult).then_inc(fold, 1)
            pool.wait_ge(fold, 2)
            g.tensor_tensor(Gt[:, :, :], Gt[:, :, :], wide("ln_w"), ALU.mult).then_inc(fold, 1)
            pool.wait_ge(fold, 3)
            for c in range(NCH):
                pool.wait_ge(sem("y_scaled"), c + 1)
                tok = slice(c * C, (c + 1) * C)
                y = YF[c % 2][:, :, :]
                g.tensor_tensor(y, y, Gt[:, :, tok], ALU.mult).then_inc(sem("y_gated"), 1)
                pool.wait_ge(sem("y_gated"), 2 * c + 1)
                g.tensor_tensor(y, y, t11[:, :, tok], ALU.add).then_inc(sem("y_gated"), 1)
                pool.wait_ge(sem("yh_ready"), c + 1)
                g.tensor_tensor(yl[:, :, tok], y, yh[:, :, tok].bitcast(f32), ALU.subtract).then_inc(sem("yl_ready"), 1)

    return nc


_INS = ["x", "mix_norm", "mlp_norm", "mlp_w1", "mlp_w2", "rwkv_mu", "rwkv_w_in", "rwkv_w0", "rwkv_w1", "rwkv_w2",
        "rwkv_a0", "rwkv_a1", "rwkv_a2", "rwkv_g1", "rwkv_g2", "rwkv_k_k", "rwkv_k_a", "rwkv_r_k", "rwkv_ln_w",
        "rwkv_ln_b", "rwkv_w_out", "nsa_w_in", "nsa_cmp_pe", "nsa_cmp_w1", "nsa_cmp_w2", "nsa_q_norm", "nsa_k_norm",
        "nsa_w_out"]


def kernel(**inputs):
    import concourse.bacc as bacc
    from concourse.bass_utils import run_bass_kernel_spmd

    nc = bacc.Bacc("TRN2", target_bir_lowering=False, num_devices=1)
    arrays, aps = {}, {}
    for name in _INS:
        a = np.ascontiguousarray(inputs[name])
        arrays[f"in_{name}"] = a
        aps[name] = nc.dram_tensor(f"in_{name}", a.shape, mybir.dt.from_np(a.dtype), kind="ExternalInput").ap()
    consts, at = constants()
    assert at == CONST_AT and consts.shape[1] == CONST_N
    arrays["in_consts"] = consts
    aps["consts"] = nc.dram_tensor("in_consts", consts.shape, mybir.dt.float32, kind="ExternalInput").ap()
    spread = (np.arange(D)[None, :] // HD == np.arange(H)[:, None]).astype(np.float32)
    arrays["in_spread"] = spread
    aps["spread"] = nc.dram_tensor("in_spread", spread.shape, mybir.dt.float32, kind="ExternalInput").ap()
    out = nc.dram_tensor("out_0", (1, T, D), mybir.dt.float32, kind="ExternalOutput").ap()
    rwkv_nsa_trunk(nc, aps, out)
    r = run_bass_kernel_spmd(nc, [arrays], core_ids=[0])
    return r.results[0]["out_0"]
```

```python
import math
from contextlib import ExitStack

import concourse.bass as bass
import numpy as np
from concourse import mybir

P = 128
D = 1024
T = 256
FT = D // P
TT = T // P
HID = 4 * D
HT = HID // P
HD = 64
H = D // HD
C = 64
NCH = T // C
SUB = 16
LD, LI, LG = 64, 64, 160
HKV = 4
GRP = H // HKV
CB, CS = 32, 16
NB = T // CS - 1
NQ, NKV = D, HKV * HD
NG = 3 * H
EPS, GN_EPS = 1e-6, 64e-5
DECAY = math.exp(-0.5)
GELU_A, GELU_B = 2 * math.sqrt(2 / math.pi), 0.044715
FAR = 1e30
FLOOR = -1e25
SLOPES = [2.0 ** (-8.0 * (h + 1) / H) for h in range(H)]

UE = 1024
RING = 4
GW = 256


def constants():
    i = np.arange(P)
    s = (i % C)[:, None]
    t = np.arange(C)[None, :]
    same = (s // SUB) == (t // SUB)
    same32 = (s // (2 * SUB)) == (t // (2 * SUB))
    tt = np.arange(C)[None, :]
    cols = {
        "ident": np.eye(P),
        "mean": np.full((P, P), 1.0 / D),
        "pair": (i[:, None] // HD) == (i[None, :] // HD),
        "center": np.eye(P) - ((i[:, None] // HD) == (i[None, :] // HD)) / HD,
        "gmask": np.concatenate([s < tt, s <= tt], 1),
        "lmask16": (s > t) & same,
        "lmask32": (s > t) & ~same & same32,
        "lmask64": (s > t) & ~same32,
        "eye64": s == t,
        "hsel": np.arange(2 * H - 2)[None, :] == (H - 2 + i // HD)[:, None],
        "chunk": np.broadcast_to(np.arange(T)[None, :] % C != 0, (P, T)),
    }
    dist = []
    for q in range(TT):
        d = (q * P + i)[:, None] - np.arange((q + 1) * P)[None, :]
        dist.append(np.where(d >= 0, d, FAR))
    cols["dist"] = np.concatenate(dist, 1)
    end = np.arange(16) * CS + CB - 1
    adc = np.empty((P, TT, H, 16))
    for q in range(TT):
        d = (q * P + i)[:, None] - end[None, :]
        d = np.where((d >= 0) & (np.arange(16) < NB)[None, :], d, FAR)
        for h in range(H):
            adc[:, q, h] = -SLOPES[h] * d
    cols["adc"] = adc.reshape(P, -1)
    at, off = {}, 0
    for n, v in cols.items():
        at[n] = (off, v.shape[1])
        off += v.shape[1]
    return np.concatenate([np.asarray(v, np.float32) for v in cols.values()], 1), at


CONST_AT = {}
CONST_N = 0
_o = 0
for _n, _w in (("ident", P), ("mean", P), ("pair", P), ("center", P), ("gmask", 2 * C), ("lmask16", C), ("lmask32", C),
               ("lmask64", C), ("eye64", C), ("hsel", 2 * H - 2), ("chunk", T),
               ("dist", P * TT * (TT + 1) // 2), ("adc", TT * H * 16)):
    CONST_AT[_n] = (_o, _w)
    _o += _w
CONST_N = _o


def rwkv_nsa_trunk(nc, t, out):
    f32, r32 = mybir.dt.float32, mybir.dt.float32r
    ALU = mybir.AluOpType
    ACT = mybir.ActivationFunctionType
    AXX = mybir.AxisListType.X
    ds = bass.ds
    ctx = ExitStack()

    base = [(nc.sbuf_base + 63) // 64 * 64]

    def place(name, shape, off=None, dt=f32):
        size = 4 * int(np.prod(shape[1:]))
        if off is None:
            off = base[0]
            base[0] = (off + size + 63) // 64 * 64
        return nc.alloc_sbuf_tensor_at(name, shape, dt, offset=off)

    h = place("h", [P, FT, T])
    raw = place("raw", [P, RING, UE])
    whi = place("whi", [P, RING, UE], dt=r32)
    wlo = place("wlo", [P, RING, UE], dt=r32)
    cst = place("cst", [P, CONST_N])
    par = place("par", [P, 144])
    tiny = place("tiny", [P, 8])
    roots = base[0]
    rs = place("rs", [P, T])
    ri = place("ri", [P, T])
    BLK = 4 * FT * T
    blk = base[0]
    off = lambda n, b=0: blk + n * BLK + b
    misc = blk + 16 * BLK
    A0, B0 = 12, 14
    xh = [place(f"xh{n}", [P, FT, T], off(12 + 2 * n), r32) for n in range(2)]
    xl = [place(f"xl{n}", [P, FT, T], off(13 + 2 * n), r32) for n in range(2)]

    xtok = place("xtok", [P, TT, D], off(1))
    prow = place("prow", [P, 2, P], off(2))
    sq = place("sq", [P, FT, T], off(0))
    xn = place("xn", [P, FT, T], off(11))
    dx = place("dx", [P, FT, T], off(1))
    mix = [place(f"mix{n}", [P, FT, T], off(2 + n)) for n in range(2)]
    R, K, V = (place(n, [P, FT, T], off(4 + i)) for i, n in enumerate("RKV"))
    lw = LD + LI + LG
    ldown = place("ldown", [P, FT, lw], off(7))
    lup_w = place("lup_w", [LD, D], off(7, 4 * FT * lw))
    lup_a = place("lup_a", [LI, D], off(7, 4 * FT * lw + 4 * D))
    lup_g0 = place("lup_g0", [P, D], off(7, 4 * FT * lw + 8 * D))
    lup_g1 = place("lup_g1", [LG - P, D], off(7, 4 * FT * lw + 12 * D))
    hw = place("hw", [LD, T], off(10, 2048))
    ha = place("ha", [LI, T], off(10, 2048 + 1024))
    hg0 = place("hg0", [P, T], off(10, 2048 + 2048))
    hg1 = place("hg1", [LG - P, T], off(10, 2048 + 3072))
    Sg = place("Sg", [P, FT, T], off(0))
    Ai = place("Ai", [P, FT, T], off(1))
    Gt = place("Gt", [P, FT, T], off(2))
    KK = place("KK", [P, FT, T], off(3))
    t11 = place("t11", [P, FT, T], off(11))
    CSm = place("CSm", [P, FT, T], off(14))
    sq2 = place("sq2", [P, FT, T], off(15))
    E1 = place("E1", [P, FT, T], off(15))
    E2 = CSm
    E3 = Sg
    kkr = place("kkr", [H, 2, T], misc + 4224)
    AR = place("AR", [P, FT, NCH, 2, C], off(7))
    BK = place("BK", [P, FT, NCH, 2, C], off(9))
    UV = place("UV", [P, NCH, D], off(4))
    BKT = place("BKT", [P, NCH, D], off(0))
    Gs = [place(f"Gs{n}", [P, FT, NCH, 2 * C], off([14, 12][n])) for n in range(2)]
    NP_ = 8
    NPAIR = FT * NCH // NP_ // 2
    DP = [place(f"DP{n}", [P, NP_, 2, C], off(12 + n)) for n in range(2)]
    LT = [place(f"LT{n}", [P, NP_, 2 * C], off(12 + n, 4096)) for n in range(2)]
    E32 = [place(f"E32{n}", [P, NP_, 2 * C], off(14 + n)) for n in range(2)]
    E64 = [place(f"E64{n}", [P, NP_, 2 * C], off(14 + n, 4096)) for n in range(2)]
    Lr = [place(f"Lr{n}", [P, NP_, C], off(6, 2048 * n)) for n in range(2)]
    Rinv = place("Rinv", [P, FT * NCH, C], off(3))
    PC = place("PC", [P, FT, NCH], misc)
    rst = place("rst", [H, 2 * C], off(1, 6144))
    XS = [place(f"XS{n}", [P, FT // 2, 2, C], misc + 128 + 2048 * n) for n in range(2)]
    STt = [place(f"STt{n}", [P, FT // 2, C], roots + 1024 * n) for n in range(2)]
    ST = [[place(f"ST{n}{b}", [P, FT // 2, C], misc + 4224 + 2048 * n + 1024 * b) for b in range(2)] for n in range(2)]
    spread = place("spread", [H, D + FT + P], misc + 8320)
    rsb = place("rsb", [H, FT, C], off(1, 4096))
    YQ = place("YQ", [P, FT, C], off(6))
    YC = place("YC", [P, FT, C], off(6, 2048))
    YF = [place(f"YF{n}", [P, FT, C], off(6, 4096 + 2048 * n)) for n in range(2)]
    yh = place("yh", [P, FT, T], off(9), r32)
    yl = place("yl", [P, FT, T], off(10), r32)

    hh = place("hh", [P, HT, T], off(0), r32)
    hl = place("hl", [P, HT, T], off(4), r32)
    rl = place("rl", [P, 2, 2, T], off(8))
    s2 = place("s2", [P, 2, 2, T], off(8, 4096))
    cw1 = place("cw1", [P, 2, CB // 2, P], off(9))
    cw2 = place("cw2", [P, 2, 2, HD], off(14))
    gw = place("gw", [P, FT, NG], off(14, 1024))
    perow = place("perow", [2 * CB, 2, HD], off(14, 2560))
    pec = place("pec", [P, 2 * CB], off(14, 3072))
    Qn = place("Qn", [P, FT, T], off(1))
    kv = place("kv", [P, 4, 2, T], off(2))
    vt = place("vt", [P, 2, TT, NKV], off(3))
    gat = place("gat", [P, TT, NG], off(3, 4096))
    kcm = place("kcm", [P, HKV, 2, 16], off(7, 6144))
    hid = place("hid", [P, 2, HKV * NB], off(3, 4864))
    gu = place("gu", [P, 2, HKV * NB], off(3, 5376))
    hpad = place("hpad", [P, HKV, 4, 32], off(3, 5888))
    kd = place("kd", [P, 2, HKV, T], off(4))
    Zc = place("Zc", [P, 2, CB // 2, HKV * NB], off(5))
    ksq = place("ksq", [P, 2, 2, T], off(6))
    ht = place("ht", [HKV * NB, 2, P], off(6, 4096))
    gcol = place("gcol", [NG, T], off(6, 6144))
    gt = place("gt", [HKV * NB, 2, P], off(6, 5120))
    qkr = place("qkr", [H, 4, T], misc + 4224)
    vblk = place("vblk", [P, HKV, 4 * HD], off(7))
    Sc = place("Sc", [P, TT, H, 32], off(8))
    PcT = place("PcT", [P, TT, HKV, P], off(8, 4096))
    csm = place("csm", [P, 4, TT, H], off(7, 4096))
    SB = [place(f"SB{n}", [P, 4, T], o) for n, o in enumerate([off(0), off(0, 4096), off(11), off(11, 4096)])]
    PT = place("PT", [P, 2, 4, TT, P], off(5))
    qss = place("qss", [P, FT, T], off(0))
    nmx = place("nmx", [P, 4, 4], off(7, 5120))
    den = place("den", [P, TT, 2, H], off(7, 5376))
    cof = place("cof", [P, TT, 2, H], off(7, 5888))
    Of = place("Of", [P, 2, 2, P], off(6))
    otok = place("otok", [P, TT, D], off(9))

    ps = ctx.enter_context(nc.psum_tensor("ps", [P, 8, 512], f32))

    def cc(name, p0=0, p1=P):
        o, w = CONST_AT[name]
        return cst[p0:p1, o:o + w]

    names = ["mix0", "mix1", "mlp0", "mlp1", "mu0", "mu1", "mu2", "mu3", "mu4", "mu5", "w0", "a0",
             "k_k", "k_a", "r_k", "ln_w", "ln_b"]
    pcol = {n: FT * i for i, n in enumerate(names)}
    for i, n in enumerate(["qn", "kn0", "kn1", "kn2"]):
        pcol[n] = FT * len(names) + i
    NPAR = FT * len(names) + 4

    def pv(name, k=0):
        return par[:, pcol[name] + k:pcol[name] + k + 1]

    def kview(w):
        return w.rearrange("(k p) n -> p k n", p=P)

    w_in, w_o = kview(t["rwkv_w_in"][0]), kview(t["rwkv_w_out"][0])
    n_in, n_o = kview(t["nsa_w_in"][0]), kview(t["nsa_w_out"][0])
    m1 = [kview(t["mlp_w1"][i]) for i in range(2)]
    m2 = [kview(t["mlp_w2"][i]) for i in range(2)]
    UNITS = [("r", 8), ("k", 8), ("v", 8), ("o0", 8), ("a1", 32), ("a2", 32), ("kc", 4), ("q", 8), ("kv", 8),
             ("o1", 8), ("b1", 32), ("b2", 32)]
    U0, n = {}, 0
    for name, cnt in UNITS:
        U0[name] = n
        n += cnt
    NU = n
    GROUPS = [("x", 4, "act"), ("r", 4, "act"), ("k", 4, "act"), ("up", 12, "act"), ("v", 4, "act"),
              ("o0", 4, "dve"), ("a1", 16, "act"), ("a2", 4, "dve"), ("kc", 2, "act"), ("q", 4, "act"), ("kv", 4, "act"),
              ("o1", 4, "dve"), ("b1", 16, "act"), ("b2", 4, "dve")]
    G0, EV0, n, ev = {}, {}, 0, {"act": 0, "dve": 0}
    for name, cnt, who in GROUPS:
        G0[name], EV0[name] = n, ev[who]
        n += cnt
        ev[who] += cnt

    XH0 = {x: 4 * i for i, x in enumerate(["r", "k", "v", "a", "nsa", "b"])}
    XL0 = {"r": ("xl_pool", 0, 4), "k": ("xl_pool", 4, 2), "v": ("xl_pool", 6, 2), "a": ("xl_dve", 0, 4),
           "nsa": ("xl_dve", 4, 4), "b": ("xl_dve", 8, 4)}

    sems = {}

    def sem(name):
        if name not in sems:
            sems[name] = ctx.enter_context(nc.semaphore(name))
        return sems[name]

    with ctx:
        raw_in = [sem(f"raw_in{s}") for s in range(RING)]
        hi_ready = sem("hi_ready")
        lo_ready = sem("lo_ready")
        unit_used = sem("unit_used")
        ev_act = sem("ev_act")
        ev_dve = sem("ev_dve")
        block = ctx.enter_context(nc.Block())

        @block.sync
        def _(sp):
            sp.dma_start(cst[:, 0:3 * P], t["consts"][:, 0:3 * P]).then_inc(sem("cst_in"), 16)
            sp.dma_start(xtok[:, :, :], t["x"][0].rearrange("(a p) n -> p a n", p=P)).then_inc(sem("x_in"), 16)
            pr = sem("par_in")
            for i, n in enumerate(["mix_norm", "mlp_norm"]):
                sp.dma_start(prow[16 * i:16 * i + 16, 0, :], t[n].rearrange("a (k p) -> (a k) p", p=P)).then_inc(pr, 16)
            sp.dma_start(prow[32:80, 0, :], t["rwkv_mu"][0].rearrange("a (k p) -> (a k) p", p=P)).then_inc(pr, 16)
            for i, n in enumerate(["rwkv_w0", "rwkv_a0", "rwkv_k_k", "rwkv_k_a"]):
                sp.dma_start(prow[80 + 8 * i:88 + 8 * i, 0, :], t[n][0].rearrange("(k p) -> k p", p=P)).then_inc(pr, 16)
            sp.dma_start(prow[112:120, 0, :], t["rwkv_r_k"][0].rearrange("(k a) n -> k (a n)", a=2)).then_inc(pr, 16)
            sp.dma_start(prow[120:128, 0, :], t["rwkv_ln_w"][0].rearrange("(k p) -> k p", p=P)).then_inc(pr, 16)
            sp.dma_start(prow[0:8, 1, :], t["rwkv_ln_b"][0].rearrange("(k p) -> k p", p=P)).then_inc(pr, 16)
            for a in range(2):
                sp.dma_start(prow[8:9, 1, a * HD:(a + 1) * HD], t["nsa_q_norm"]).then_inc(pr, 16)
                sp.dma_start(prow[9:12, 1, a * HD:(a + 1) * HD], t["nsa_k_norm"][0]).then_inc(pr, 16)
            sp.dma_start(spread[:, :], t["spread"]).then_inc(sem("spread_in"), 16)

            def load(u, src):
                s = u % RING if isinstance(u, int) else None
                dst = raw[:, s, :].rearrange("p (k n) -> p k n", n=GW)
                if u >= RING:
                    sp.wait_ge(lo_ready, u - RING + 1)
                sp.dma_start(dst, src).then_inc(raw_in[s], 16)

            def pairs(name, view, col0, lo, hi):
                for j in range(lo, hi):
                    c0 = col0 + (j // 2) * GW
                    load(U0[name] + j, view[:, 4 * (j % 2):4 * (j % 2) + 4, c0:c0 + GW])

            lo = sem("lora_in")
            pairs("r", w_in, 0, 0, 4)
            sp.dma_start(cst[:, 3 * P:], t["consts"][:, 3 * P:]).then_inc(sem("cst_rest"), 16)
            sp.dma_start(ldown[:, :, 0:LD], kview(t["rwkv_w1"][0])).then_inc(lo, 16)
            sp.dma_start(ldown[:, :, LD:LD + LI], kview(t["rwkv_a1"][0])).then_inc(lo, 16)
            sp.dma_start(ldown[:, :, LD + LI:lw], kview(t["rwkv_g1"][0])).then_inc(lo, 16)
            sp.dma_start(lup_w[:, :], t["rwkv_w2"][0]).then_inc(lo, 16)
            sp.dma_start(lup_a[:, :], t["rwkv_a2"][0]).then_inc(lo, 16)
            sp.dma_start(lup_g0[:, :], t["rwkv_g2"][0][0:P, :]).then_inc(lo, 16)
            sp.dma_start(lup_g1[:, :], t["rwkv_g2"][0][P:LG, :]).then_inc(lo, 16)
            pairs("r", w_in, 0, 4, 8)
            pairs("k", w_in, D, 0, 8)
            pairs("v", w_in, 2 * D, 0, 8)
            pairs("o0", w_o, 0, 0, 8)

            def mlp_loads(n1, n2, v1, v2):
                pairs(n1, v1, 0, 0, 4)
                if n1 == "a1":
                    sp.wait_ge(ev_dve, EV0["o0"] + 4)
                    cs = sem("cmp_in")
                    for a in range(2):
                        src = t["nsa_cmp_w1"][0].rearrange("b (a l d) m -> a d b l m", a=2, l=CB // 2)[a]
                        for b in range(2):
                            sp.dma_start(cw1[64 * a:64 * a + 64, b, :, :], src[:, b, :, :]).then_inc(cs, 16)
                        sp.dma_start(cw2[:, :, a, :], t["nsa_cmp_w2"][0].rearrange("b m d -> m b d")).then_inc(cs, 16)
                        sp.dma_start(perow[:, a, :], t["nsa_cmp_pe"][0].rearrange("b l d -> (b l) d")).then_inc(cs, 16)
                    sp.dma_start(gw[:, :, :], n_in[:, :, NQ + 6 * NKV:]).then_inc(cs, 16)
                with sp.Fori(1, 8) as i:
                    for j in range(4):
                        sp.wait_ge(lo_ready, i * 4 + (U0[n1] + j - RING + 1))
                        sp.dma_start(raw[:, j, :].rearrange("p (k n) -> p k n", n=GW),
                                     v1[:, 4 * (j % 2):4 * (j % 2) + 4, ds(i * (2 * GW) + (j // 2) * GW, GW)])\
                          .then_inc(raw_in[j], 16)
                with sp.Fori(0, 4) as i:
                    for j in range(8):
                        sp.wait_ge(lo_ready, i * 8 + (U0[n2] + j - RING + 1))
                        sp.dma_start(raw[:, j % RING, :].rearrange("p (k n) -> p k n", n=GW),
                                     v2[:, 4 * j:4 * j + 4, ds(i * GW, GW)]).then_inc(raw_in[j % RING], 16)

            mlp_loads("a1", "a2", m1[0], m2[0])
            pairs("kc", n_in, NQ, 0, 4)
            pairs("q", n_in, 0, 0, 8)
            for j in range(8):
                c0 = NQ + [2, 4, 3, 5][j // 2] * NKV
                load(U0["kv"] + j, n_in[:, 4 * (j % 2):4 * (j % 2) + 4, c0:c0 + GW])
            pairs("o1", n_o, 0, 0, 8)
            mlp_loads("b1", "b2", m1[1], m2[1])
            for q in range(TT):
                sp.wait_ge(sem("out_ready"), q + 1)
                sp.dma_start(out[0, q * P:(q + 1) * P, :], otok[:, q, :]).then_inc(sem("stored"), 16)
            sp.wait_ge(sem("stored"), 16 * TT)

        @block.tensor
        def _(pe):
            mm = nc.tensor.matmul

            def group_free(name, g):
                if EV0[name] + g - 1 > 0:
                    pe.wait_ge(ev_act if who[name] == "act" else ev_dve, EV0[name] + g - 1)

            who = {n: w for n, _, w in GROUPS}

            def parts(x, n):
                if x == "o1":
                    pe.wait_ge(sem("att_upper"), HKV * (n // 2) + HKV)
                    pe.wait_ge(sem("att_lower"), HKV * (n // 2) + HKV)
                    return
                pe.wait_ge(sem("xh_ready"), XH0[x] + n + 1)
                where, base_, pieces = XL0[x]
                pe.wait_ge(sem(where), base_ + n * pieces // 4 + 1)

            def unit_mm(slot, bank0, kbase, ktiles, hi, lo, x=None):
                for k in range(4):
                    kk = kbase + k
                    if x and k % 2 == 0:
                        parts(x, kk // 2)
                    for m in range(2):
                        o = ps[:, bank0 + m, 0:T]
                        c0 = k * GW + m * P
                        wh, wl = whi[:, slot, c0:c0 + P], wlo[:, slot, c0:c0 + P]
                        mm(o, wh, hi[:, kk, :], start=(kk == 0), stop=False)
                        mm(o, wh, lo[:, kk, :], start=False, stop=False)
                        last = mm(o, wl, hi[:, kk, :], start=False, stop=(kk == ktiles - 1))
                return last

            def linear8(name, hi, lo, x=None, between=None, groups=4):
                for g in range(groups):
                    group_free(name, g)
                    for j in range(2):
                        u = U0[name] + 2 * g + j
                        pe.wait_ge(lo_ready, u + 1)
                        last = unit_mm(u % RING, 2 * (g % 2), 4 * j, FT, hi, lo, x if g == 0 else None)
                        last.then_inc(unit_used, 1)
                    if between:
                        between(g)

            pe.wait_ge(sem("cst_in"), 16)
            pe.wait_ge(sem("x_in"), 16)
            for g in range(4):
                if g >= 2:
                    pe.wait_ge(ev_act, g - 1)
                for m in range(2):
                    for q in range(TT):
                        last = nc.tensor.transpose(ps[:, 2 * (g % 2) + m, q * P:(q + 1) * P],
                                                   xtok[:, q, (2 * g + m) * P:(2 * g + m + 1) * P], cc("ident"))
                last.then_inc(sem("x_pe0"), 1)
            pe.wait_ge(sem("par_in"), 16 * 14)
            nc.tensor.transpose(ps[:, 5, 0:P], prow[:, 0, :], cc("ident"))
            nc.tensor.transpose(ps[:, 5, P:P + 12], prow[0:12, 1, :], cst[0:12, 0:12]).then_inc(sem("par_t"), 1)

            def norm_pe(i):
                for k in range(FT):
                    if k % 2 == 0:
                        pe.wait_ge(sem("sq_ready"), 4 * i + 1 + k // 2)
                    last = mm(ps[:, 4, 0:T], cc("mean"), sq[:, k, :], start=(k == 0), stop=(k == FT - 1))
                last.then_inc(sem("ms_ready"), 1)

            norm_pe(0)

            def hsel(k):
                return cc("hsel")[:, H - 2 - 2 * k:2 * H - 2 - 2 * k]

            def hspread(k):
                return spread[:, k * P:(k + 1) * P]

            def lora_down(n, src, c0, width, bank):
                for k in range(FT):
                    last = mm(ps[0:width, bank, 0:T], ldown[:, k, c0:c0 + width], src[:, k, :],
                              start=(k == 0), stop=(k == FT - 1))
                return last

            linear8("r", xh[0], xl[0], "r")
            pe.wait_ge(sem("lora_in"), 16 * 7)
            pe.wait_ge(sem("mix_ready"), 12)
            lora_down("w", mix[1], 0, LD, 5).then_inc(sem("lora_h"), 1)
            pe.wait_ge(sem("mix_ready"), 16)
            lora_down("a", mix[0], LD, LI, 6).then_inc(sem("lora_h"), 1)
            linear8("k", xh[1], xl[1], "k")
            pe.wait_ge(sem("mix_ready"), 20)
            lora_down("g", mix[1], LD + LI, P, 7)
            lora_down("g", mix[1], LD + LI + P, LG - P, 4).then_inc(sem("lora_h"), 1)
            ups = [(1, [(lup_w, hw)]), (2, [(lup_a, ha)]), (3, [(lup_g0, hg0), (lup_g1, hg1)])]
            for n, (need, lora) in enumerate(ups):
                pe.wait_ge(sem("lora_act"), need)
                if n == 2:
                    pe.wait_ge(sem("kksq"), 1)
                    pe.wait_ge(sem("cst_rest"), 16)
                    for k in range(FT):
                        last = mm(ps[0:H, 4, 0:T], hsel(k), sq2[:, k, :], start=(k == 0), stop=(k == FT - 1))
                    last.then_inc(sem("kk_sum"), 1)
                for g in range(4):
                    pe.wait_ge(ev_act, EV0["up"] + 4 * n + g - 1)
                    for m in range(2):
                        c0 = (2 * g + m) * P
                        for i, (w, x) in enumerate(lora):
                            last = mm(ps[:, 2 * (g % 2) + m, 0:T], w[:, c0:c0 + P], x[:, :],
                                      start=(i == 0), stop=(i == len(lora) - 1))
                    last.then_inc(sem("up_pe"), 1)

            def between_v(g):
                if g == 0:
                    pe.wait_ge(sem("spread_in"), 16)
                    pe.wait_ge(sem("kk_inv"), 1)
                    for k in range(FT):
                        last = mm(ps[:, 4 + k // 2, (k % 2) * T:(k % 2 + 1) * T], hspread(k), kkr[:, 1, :],
                                  start=True, stop=True)
                    last.then_inc(sem("kk_spread"), 1)
                if g == 1:
                    pe.wait_ge(sem("rk"), 1)
                    pe.wait_ge(sem("kkn_used"), 1)
                    for j in range(4):
                        last = mm(ps[:, 4 + j, :], cc("pair"), t11[:, 2 * j:2 * j + 2, :], start=True, stop=True)
                    last.then_inc(sem("rk_sum"), 1)

            linear8("v", xh[0], xl[0], "v", between_v)

            def b_k(c):
                b = 4 + 2 * (c % 2)
                for k in range(FT):
                    last = nc.tensor.transpose(ps[:, b + k // 4, (k % 4) * P:(k % 4 + 1) * P],
                                               BK[:, k, c, :, :], cc("ident"))
                last.then_inc(sem("bkT"), 1)

            pe.wait_ge(sem("bk_ready"), 2)
            pe.wait_ge(sem("rk_copied"), 1)
            b_k(0)
            b_k(1)
            pe.wait_ge(ev_act, EV0["v"] + 4)
            for q in range(TT):
                for k in range(FT):
                    last = nc.tensor.transpose(ps[:, 2 * q + k // 4, (k % 4) * P:(k % 4 + 1) * P],
                                               V[:, k, q * P:(q + 1) * P], cc("ident"))
                last.then_inc(sem("vT"), 1)
            pe.wait_ge(sem("bkt_act"), 1)
            b_k(2)

            pe.wait_ge(sem("ar_ready"), 2)

            def at(e):
                return slice(HD * e, HD * e + HD)

            def g_products(half):
                for n in range(8):
                    k, e = half * FT // 2 + n // 2, n % 2
                    if half:
                        pe.wait_ge(sem("g_masked"), n + 1)
                    for c in range(NCH):
                        last = mm(ps[:, n, c * P:(c + 1) * P], BK[at(e), k, c, :, :], AR[at(e), k, c, :, :],
                                  start=True, stop=True)
                    last.then_inc(sem("g_done"), 1)

            def lower_products(s, pair, bank):
                p0 = (2 * pair + s) * NP_

                def one(p, e):
                    k, c = (p0 + p) // NCH, p % NCH
                    return mm(ps[at(e), bank + p // 4, (p % 4) * C:(p % 4 + 1) * C], AR[at(e), k, c, 0, :],
                              BK[at(e), k, c, 0, :], start=True, stop=True)
                for a in range(2):
                    for i in range(NP_ // 2):
                        one(i, a)
                        last = one(i + NP_ // 2, 1 - a)
                return last

            def times_both(s, bank, lhs):
                for p in range(NP_):
                    last = mm(ps[:, bank + p // 4, (p % 4) * P:(p % 4 + 1) * P], lhs[:, p, :], DP[s][:, p, :, :],
                              start=True, stop=True)
                return last

            for pair in range(NPAIR):
                for n in range(9):
                    for s in range(2):
                        if n == 0 and pair == 0:
                            if s == 0:
                                pe.wait_ge(sem("v_copied"), 2)
                            else:
                                pe.wait_ge(sem("bkt_act"), 2)
                                pe.wait_ge(sem("bkt_dve"), 3)
                        else:
                            pe.wait_ge(sem(f"inv_dve{s}"), 20 * pair + [-1, 5, 7, 10, 13, 14, 16, 17, 19][n])
                            pe.wait_ge(sem(f"inv_act{s}"), 5 * pair + [0, 1, 2, 3, 3, 3, 4, 4, 5][n])
                        if n in (5, 7):
                            pe.wait_ge(sem(f"inv_pool{s}"), 4 * pair + {5: 2, 7: 4}[n])
                        b = 4 * s + 2 * ((n + pair) % 2)
                        if n == 0:
                            last = lower_products(s, pair, b)
                        else:
                            last = times_both(s, b, {5: E32, 7: E64}.get(n, LT)[s])
                        last.then_inc(sem(f"inv_pe{s}"), 1)

            for s in range(2):
                pe.wait_ge(sem(f"inv_dve{s}"), 20 * NPAIR)
            g_products(0)
            g_products(1)
            pe.wait_ge(sem("u_zero"), 1)

            def hk(half):
                for k_ in range(FT // 2):
                    for e in range(2):
                        k = half * FT // 2 + k_
                        yield k_, k, e, 2 * k_ + e, slice((2 * k + e) * HD, (2 * k + e + 1) * HD)

            def gn_mean(c):
                for n in range(2):
                    pe.wait_ge(sem(f"y_copied{n}"), c + 1)
                if c:
                    pe.wait_ge(sem("y_scaled"), c)
                mm(ps[:, 6, :], cc("center"), AR[:, :, c, 1, :], start=True, stop=True).then_inc(sem("mean_pe"), 1)

            def gn_var(c):
                pe.wait_ge(sem("y_sq"), c + 1)
                for k in range(FT):
                    last = mm(ps[0:H, 7, 0:C], hsel(k), YQ[:, k, :], start=(k == 0), stop=(k == FT - 1))
                last.then_inc(sem("var_pe"), 1)

            def gn_spread(c):
                pe.wait_ge(sem("y_rstd"), c + 1)
                mm(ps[:, 7, :], spread[:, D + FT:], rsb[:, :, :], start=True, stop=True).then_inc(sem("rstd_pe"), 1)

            for c in range(NCH):
                for half in range(2):
                    if c:
                        pe.wait_ge(sem(f"st_ready{half}"), c)
                    else:
                        pe.wait_ge(sem("g_masked"), 16 if half else 9)
                    for k_, k, e, hd, cols in hk(half):
                        o = ps[at(e), 3 * half, k_ * C:(k_ + 1) * C]
                        last = mm(o, Gs[half][:, hd, c, 0:C], UV[:, c, cols], start=True, stop=(c == 0))
                        if c:
                            last = mm(o, AR[at(e), k, c, 0, :], ST[half][(c - 1) % 2][at(e), k_, :], start=False, stop=True)
                    last.then_inc(sem(f"xs_pe{half}"), 1)
                if c:
                    gn_mean(c - 1)
                for half in range(2):
                    pe.wait_ge(sem(f"x_even{half}"), c + 1)
                    pe.wait_ge(sem(f"x_odd{half}"), c + 1)
                    for k_ in range(FT // 2):
                        last = mm(ps[0:HD, 3 * half + 1, k_ * P:(k_ + 1) * P], Rinv[:, (half * FT // 2 + k_) * NCH + c, :],
                                  XS[half][:, k_, :, :], start=True, stop=True)
                    last.then_inc(sem(f"u_pe{half}"), 1)
                if c:
                    gn_var(c - 1)
                for half in range(2):
                    pe.wait_ge(sem(f"u_sb{half}"), c + 1)
                    if c < NCH - 1:
                        if c:
                            pe.wait_ge(sem(f"st_ready{half}"), c)
                        for k_, k, e, hd, cols in hk(half):
                            last = mm(ps[at(e), 3 * half, k_ * C:(k_ + 1) * C], BKT[:, c, cols], UV[:, c, cols],
                                      start=True, stop=True)
                        last.then_inc(sem(f"s_pe{half}"), 1)
                for half in range(2):
                    if c:
                        pe.wait_ge(sem(f"y_copied{half}"), c)
                    for k_, k, e, hd, cols in hk(half):
                        o = ps[at(e), 3 * half + 2, k_ * C:(k_ + 1) * C]
                        last = mm(o, UV[:, c, cols], Gs[half][:, hd, c, C:2 * C], start=True, stop=(c == 0))
                        if c:
                            last = mm(o, ST[half][(c - 1) % 2][at(e), k_, :], AR[at(e), k, c, 1, :], start=False, stop=True)
                    last.then_inc(sem(f"y_pe{half}"), 1)
                if c:
                    gn_spread(c - 1)
            gn_mean(NCH - 1)
            gn_var(NCH - 1)
            gn_spread(NCH - 1)
            pe.wait_ge(sem("yh_ready"), NCH)
            pe.wait_ge(sem("yl_ready"), NCH - 1)
            pe.wait_ge(sem("yl_last"), 1)
            linear8("o0", yh, yl)

            def mlp_pe(n1, n2, hi, lo, x):
                for g in range(2):
                    group_free(n1, g)
                    for j in range(2):
                        pe.wait_ge(lo_ready, U0[n1] + 2 * g + j + 1)
                        unit_mm(2 * g + j, 2 * g, 4 * j, FT, hi, lo, x if g == 0 else None).then_inc(unit_used, 1)
                with pe.Fori(1, 8) as i:
                    for g in range(2):
                        pe.wait_ge(ev_act, i * 2 + (EV0[n1] + g - 1))
                        for j in range(2):
                            pe.wait_ge(lo_ready, i * 4 + (U0[n1] + 2 * g + j + 1))
                            unit_mm(2 * g + j, 2 * g, 4 * j, FT, hi, lo).then_inc(unit_used, 1)
                done = 0 if n1 == "a1" else 16
                with pe.Fori(0, 2) as i:
                    for g in range(2):
                        pe.wait_ge(ev_dve, i * 2 + (EV0[n2] + g - 1))
                        for j in range(8):
                            if g == 0:
                                pe.wait_ge(sem("hid_ready"), done + 2 * j + 2)
                            pe.wait_ge(lo_ready, i * 16 + (U0[n2] + 8 * g + j + 1))
                            unit_mm(j % RING, 2 * g, 4 * j, HT, hh, hl).then_inc(unit_used, 1)

            norm_pe(1)
            mlp_pe("a1", "a2", xh[0], xl[0], "a")

            norm_pe(2)
            linear8("kc", xh[0], xl[0], "nsa", groups=2)

            def between_q(g):
                if g == 0:
                    pe.wait_ge(sem("cmp_in"), 16 * 9)
                    for k in range(FT):
                        mm(ps[0:NG, 4, 0:T], gw[:, k, :], xn[:, k, :], start=(k == 0), stop=(k == FT - 1))
                    nc.tensor.transpose(ps[:, 5, 0:2 * CB], perow[:, :, :], cst[0:2 * CB, 0:2 * CB])\
                        .then_inc(sem("gate_pe"), 1)
                if g == 1:
                    pe.wait_ge(sem("gates_r"), 1)
                    pe.wait_ge(sem("pe_col"), 1)
                    for q in range(TT):
                        last = nc.tensor.transpose(ps[:, 5, q * 64:q * 64 + NG], gcol[:, q * P:(q + 1) * P], cst[0:NG, 0:NG])
                    last.then_inc(sem("rows_T"), 1)
                if g == 2:
                    pe.wait_ge(sem("zc"), 1)
                    pe.wait_ge(sem("gates_r"), 1)
                    for b in range(2):
                        for l in range(CB // 2):
                            last = mm(ps[0:HKV * NB, 4, b * P:(b + 1) * P], Zc[:, b, l, :], cw1[:, b, l, :],
                                      start=(l == 0), stop=(l == CB // 2 - 1))
                    last.then_inc(sem("cmp_pe"), 1)
                if g == 3:
                    pe.wait_ge(sem("hid_rows"), 1)
                    pe.wait_ge(sem("gates_r"), 2)
                    for b in range(2):
                        last = nc.tensor.transpose(ps[:, 5, b * 64:b * 64 + HKV * NB], ht[:, b, :], cst[0:HKV * NB, 0:HKV * NB])
                    last.then_inc(sem("rows_T"), 1)

            linear8("q", xh[0], xl[0], between=between_q)

            def q_spread(half):
                for i in range(4):
                    last = mm(ps[:, 6 + i // 2, (i % 2) * T:(i % 2 + 1) * T], hspread(4 * half + i), qkr[:, 1, :],
                              start=True, stop=True)
                last.then_inc(sem("q_spread"), 1)

            def between_kv(g):
                if g == 0:
                    pe.wait_ge(sem("hid_k"), 1)
                    mm(ps[:, 5, 0:HKV * NB], cw2[:, 0, :, :], hid[:, 0, :], start=True, stop=True)
                    for j in range(HKV):
                        last = mm(ps[:, 5, 128 + j * HD:128 + (j + 1) * HD], hpad[:, j, :, :], cw2[:, 1, 0, :],
                                  start=True, stop=True)
                    last.then_inc(sem("cmp2_pe"), 1)
                    pe.wait_ge(sem("qsq"), 1)
                    for k in range(FT):
                        last = mm(ps[0:H, 6, 0:T], hsel(k), qss[:, k, :], start=(k == 0), stop=(k == FT - 1))
                    last.then_inc(sem("q_sum"), 1)
                if g == 1:
                    pe.wait_ge(sem("kcsq"), 1)
                    mm(ps[:, 4, 0:HKV * NB], cc("pair"), gu[:, 0, :], start=True, stop=True).then_inc(sem("kc_pe"), 1)
                    pe.wait_ge(sem("q_inv"), 1)
                    q_spread(0)
                if g == 2:
                    pe.wait_ge(sem("q_scaled"), 1)
                    q_spread(1)
                    pe.wait_ge(sem("ksq_r"), 1)
                    pe.wait_ge(sem("kcrs"), 1)
                    for k in range(4):
                        last = mm(ps[0:H, 4, 0:T], hsel(k), ksq[:, k // 2, k % 2, :], start=(k == 0), stop=(k == 3))
                    last.then_inc(sem("k_sum"), 1)
                if g == 3:
                    pe.wait_ge(sem("k_inv"), 1)
                    pe.wait_ge(sem("vblk_r"), 4)
                    pe.wait_ge(sem("kcm_r"), 2)
                    for k in range(4):
                        last = mm(ps[:, 4 + k // 2, (k % 2) * T:(k % 2 + 1) * T], hspread(k), qkr[:, 3, :],
                                  start=True, stop=True)
                    last.then_inc(sem("k_spread"), 1)
                    pe.wait_ge(sem("q_scaled"), 2)
                    for q in range(TT):
                        for k in range(FT):
                            o = q * T + k * 32
                            last = mm(ps[:, 6, o:o + 32], Qn[:, k, q * P:(q + 1) * P], kcm[:, k // 2, :, :],
                                      start=True, stop=True)
                    last.then_inc(sem("sc_pe"), 1)

            for g, tok in enumerate([0, 0, 1, 1]):
                group_free("kv", g)
                for j in range(2):
                    u = U0["kv"] + 2 * g + j
                    pe.wait_ge(lo_ready, u + 1)
                    if not tok:
                        last = unit_mm(u % RING, 2 * (g % 2), 4 * j, FT, xh[0], xl[0])
                    else:
                        for k in range(4):
                            kk_ = 4 * j + k
                            for q in range(TT):
                                o = ps[:, 2 * (g % 2) + q, 0:GW]
                                tq = slice(q * P, (q + 1) * P)
                                wh = whi[:, u % RING, k * GW:(k + 1) * GW]
                                wl = wlo[:, u % RING, k * GW:(k + 1) * GW]
                                mm(o, xh[0][:, kk_, tq], wh, start=(kk_ == 0), stop=False)
                                mm(o, xh[0][:, kk_, tq], wl, start=False, stop=False)
                                last = mm(o, xl[0][:, kk_, tq], wh, start=False, stop=(kk_ == FT - 1))
                    last.then_inc(unit_used, 1)
                between_kv(g)

            items = [(j, q, b) for j in range(HKV) for q in range(TT) for b in range(2)]
            pe.wait_ge(ev_act, EV0["kv"] + 4)

            def scores(n):
                j, q, b = items[n]
                if n >= 2:
                    pe.wait_ge(sem("s_read"), n - 1)
                if n < 2:
                    pe.wait_ge(sem("kd_ready"), 2 * n + 2)
                    pe.wait_ge(sem("kd_copied"), 2 * n + 2)
                w = (q + 1) * P
                for i in range(2):
                    for e in range(2):
                        k = 2 * j + i
                        qe = slice(HD * e, HD * e + HD)
                        last = mm(ps[:, 2 * (n % 2) + e, i * T:i * T + w], Qn[qe, k, q * P:(q + 1) * P],
                                  kd[qe, b, j, 0:w], start=True, stop=True)
                last.then_inc(sem("s_pe2"), 1)

            def transposes(n):
                j, q, b = items[n]
                pe.wait_ge(sem("p_scaled"), n + 1)
                if n >= 1:
                    pe.wait_ge(sem("pt_read"), n)
                for s in range(q + 1):
                    for i in range(4):
                        last = nc.tensor.transpose(ps[:, 4 + s, i * P:(i + 1) * P],
                                                   SB[n % 4][:, i, s * P:(s + 1) * P], cc("ident"))
                last.then_inc(sem("t_pe"), 1)

            def weighted(n):
                j, q, b = items[n]
                g = n // 2
                o = ps[0:HD, 6 + g % 2, :]
                if b == 0:
                    if g >= 2:
                        pe.wait_ge(sem("o_read"), g - 1)
                    for i in range(4):
                        mm(o[:, i * P:(i + 1) * P], vblk[:, j, i * HD:(i + 1) * HD], PcT[:, q, j, :], start=(i == 0), stop=False)
                pe.wait_ge(sem("pt_read"), n + 1)
                for s in range(q + 1):
                    last = mm(o, vt[:, b, s, j * HD:(j + 1) * HD], PT[:, n % 2, :, s, :],
                              start=False, stop=(b == 1 and s == q))
                last.then_inc(sem("pv_pe"), 1)

            scores(0)
            scores(1)
            pe.wait_ge(sem("pc_ready"), 1)
            for q in range(TT):
                for j in range(HKV):
                    last = nc.tensor.transpose(ps[:, 4 + q, j * P:(j + 1) * P], Sc[:, q, 4 * j:4 * j + 4, :], cc("ident"))
            last.then_inc(sem("pct_pe"), 1)
            scores(2)
            pe.wait_ge(sem("pct_r"), 1)
            for n in range(len(items)):
                if n + 3 < len(items):
                    scores(n + 3)
                transposes(n)
                if n >= 1:
                    weighted(n - 1)
            weighted(len(items) - 1)
            linear8("o1", xh[1], xl[1], "o1")

            norm_pe(3)
            mlp_pe("b1", "b2", xh[0], xl[0], "b")
            for q in range(TT):
                for k in range(FT):
                    if q == 0 and k % 2 == 0:
                        pe.wait_ge(ev_dve, EV0["b2"] + k // 2 + 1)
                    last = nc.tensor.transpose(ps[:, 4 + 2 * q + k // 4, (k % 4) * P:(k % 4 + 1) * P],
                                               h[:, k, q * P:(q + 1) * P], cc("ident"))
                last.then_inc(sem("fin_pe"), 1)

        @block.scalar
        def _(act):
            A = nc.scalar.activation
            aown = sem("act_step")
            cnt = [0]

            def step(ins):
                cnt[0] += 1
                ins.then_inc(aown, 1)

            def settle():
                act.wait_ge(aown, cnt[0])

            def split(u):
                s = u % RING
                act.wait_ge(raw_in[s], 16 * (u // RING + 1))
                if u >= RING:
                    act.wait_ge(unit_used, u - RING + 1)
                A(whi[:, s, :], raw[:, s, :], ACT.Copy).then_inc(hi_ready, 1)

            def ahead(u):
                if u + RING < NU:
                    split(u + RING)

            def evac8(name, dst, after_first=None):
                for g in range(4):
                    act.wait_ge(unit_used, U0[name] + 2 * g + 2)
                    A(dst[:, 2 * g:2 * g + 2, :], ps[:, 2 * (g % 2):2 * (g % 2) + 2, 0:T], ACT.Copy).then_inc(ev_act, 1)
                    ahead(U0[name] + 2 * g)
                    ahead(U0[name] + 2 * g + 1)
                    if g == 0 and after_first:
                        after_first()

            for g in range(4):
                act.wait_ge(sem("x_pe0"), g + 1)
                A(h[:, 2 * g:2 * g + 2, :], ps[:, 2 * (g % 2):2 * (g % 2) + 2, 0:T], ACT.Copy).then_inc(ev_act, 1)

            def norm_act(i):
                if i == 0:
                    act.wait_ge(sem("eps_set"), 3)
                step(A(tiny[:, 2:3], tiny[:, 0:1], ACT.Sqrt))
                for m in range(4):
                    if i == 0:
                        act.wait_ge(ev_act, m + 1)
                    else:
                        act.wait_ge(ev_dve, 4 * (i - 1) + m + 1)
                    A(sq[:, 2 * m:2 * m + 2, :], h[:, 2 * m:2 * m + 2, :], ACT.Square).then_inc(sem("sq_ready"), 1)
                if i == 0:
                    split(0)
                    split(1)
                act.wait_ge(sem("ms_ready"), i + 1)
                act.wait_ge(sem("eps_set"), 3)
                if i:
                    act.wait_ge(sem("xn_done"), i)
                A(rs[:, :], ps[:, 4, 0:T], ACT.Sqrt, bias=tiny[:, 0:1]).then_inc(sem("rs_ready"), 1)

            norm_act(0)
            for u in range(2, RING):
                split(u)

            def upper(dst, src, ready, count):
                for n in range(4):
                    act.wait_ge(sem(ready), count + n + 1)
                    A(dst[:, 2 * n:2 * n + 2, :], src[:, 2 * n:2 * n + 2, :], ACT.Copy).then_inc(sem("xh_ready"), 1)

            upper(xh[0], mix[1], "mix_ready", 0)
            evac8("r", R, lambda: upper(xh[1], mix[0], "mix_ready", 4))
            act.wait_ge(sem("lora_h"), 1)
            A(hw[:, :], ps[0:LD, 5, 0:T], ACT.Tanh).then_inc(sem("lora_act"), 1)
            act.wait_ge(sem("lora_h"), 2)
            A(ha[:, :], ps[0:LI, 6, 0:T], ACT.Copy).then_inc(sem("lora_act"), 1)
            upper(xh[0], mix[0], "mix_ready", 20)
            evac8("k", K)
            act.wait_ge(sem("lora_h"), 3)
            step(A(hg0[:, :], ps[:, 7, 0:T], ACT.Sigmoid))
            settle()
            A(hg1[:, :], ps[0:LG - P, 4, 0:T], ACT.Sigmoid).then_inc(sem("lora_act"), 1)
            for n, (dst, bias) in enumerate([(Sg, "w0"), (Ai, "a0"), (Gt, None)]):
                if n == 1:
                    act.wait_ge(sem("kk_raw"), 1)
                    A(sq2[:, :, :], KK[:, :, :], ACT.Square).then_inc(sem("kksq"), 1)
                if n == 2:
                    act.wait_ge(sem("xl_pool"), 8)
                for g in range(4):
                    act.wait_ge(sem("up_pe"), 4 * n + g + 1)
                    if bias is None:
                        A(dst[:, 2 * g:2 * g + 2, :], ps[:, 2 * (g % 2):2 * (g % 2) + 2, 0:T], ACT.Copy).then_inc(ev_act, 1)
                        continue
                    step(A(dst[:, 2 * g, :], ps[:, 2 * (g % 2), 0:T], ACT.Sigmoid, bias=pv(bias, 2 * g)))
                    settle()
                    A(dst[:, 2 * g + 1, :], ps[:, 2 * (g % 2) + 1, 0:T], ACT.Sigmoid, bias=pv(bias, 2 * g + 1))\
                        .then_inc(ev_act, 1)
            act.wait_ge(sem("kk_sum"), 1)
            A(kkr[:, 0, :], ps[0:H, 4, 0:T], ACT.Sqrt).then_inc(sem("kk_root"), 1)
            act.wait_ge(sem("cs_ready"), 1)
            A(E1[:, :, :], CSm[:, :, :], ACT.Exp, scale=-DECAY).then_inc(sem("e1_ready"), 1)
            act.wait_ge(sem("ex_ready"), 1)
            A(E2[:, :, :], CSm[:, :, :], ACT.Exp, scale=DECAY).then_inc(sem("e2_ready"), 1)
            A(E3[:, :, :], Sg[:, :, :], ACT.Exp, scale=-DECAY).then_inc(sem("e3_ready"), 1)
            for g in range(4):
                act.wait_ge(unit_used, U0["v"] + 2 * g + 2)
                A(V[:, 2 * g:2 * g + 2, :], ps[:, 2 * (g % 2):2 * (g % 2) + 2, 0:T], ACT.Copy).then_inc(ev_act, 1)
                ahead(U0["v"] + 2 * g)
                ahead(U0["v"] + 2 * g + 1)
                if g == 2:
                    act.wait_ge(sem("rk_sum"), 1)
                    A(t11[:, :, :].rearrange("p (b k) t -> p b (k t)", b=4), ps[:, 4:8, :], ACT.Copy).then_inc(sem("rk_copied"), 1)
            def bkt_copy(c):
                act.wait_ge(sem("bkT"), c + 1)
                A(BKT[:, c, :].rearrange("p (b n) -> p b n", b=2), ps[:, 4:6, :], ACT.Copy).then_inc(sem("bkt_act"), 1)

            act.wait_ge(sem("ar_ready"), 2)
            act.wait_ge(sem("bk_ready"), 2)
            bkt_copy(0)
            act.wait_ge(sem("rk_done"), 1)
            act.wait_ge(sem("vT"), 1)
            for c in range(2):
                A(UV[HD:P, c, :].rearrange("p (b n) -> p b n", b=2), ps[HD * c:HD * c + HD, 0:2, :],
                  ACT.Copy).then_inc(sem("v_copied"), 1)
            bkt_copy(2)
            for pair in range(NPAIR):
                for n in (0, 1, 2, 5, 7):
                    for s in range(2):
                        act.wait_ge(sem(f"inv_pe{s}"), 9 * pair + n + 1)
                        b = 4 * s + 2 * ((n + pair) % 2)
                        if n == 0:
                            if pair:
                                act.wait_ge(sem(f"inv_pool{s}"), 4 * pair)
                            else:
                                act.wait_ge(sem("bonus"), 1)
                            dst = Lr[s][:, :, :]
                        else:
                            dst = DP[s][:, :, 0, :]
                        if n:
                            src = ps[:, b:b + 2, :].rearrange("p b (k a n) -> p (b k) a n", a=2, n=C)[:, :, 1 if n in (5, 7) else 0, :]
                            A(dst, src, ACT.Copy).then_inc(sem(f"inv_act{s}"), 1)
                        else:
                            A(dst.rearrange("p (b k) n -> p b k n", b=2),
                              ps[:, b:b + 2, 0:GW].rearrange("p b (k n) -> p b k n", n=C), ACT.Copy)\
                                .then_inc(sem(f"inv_act{s}"), 1)

            def quarter(src):
                return src.rearrange("p (k n) -> p k n", n=C)

            def gn_square(c):
                act.wait_ge(sem("mean_pe"), c + 1)
                A(YQ[:, :, :], quarter(ps[:, 6, :]), ACT.Square).then_inc(sem("y_sq"), 1)
                if c:
                    act.wait_ge(sem("y_scaled"), c)
                A(YC[:, :, :], quarter(ps[:, 6, :]), ACT.Copy).then_inc(sem("yc"), 1)

            def gn_sqrt(c):
                act.wait_ge(sem("var_pe"), c + 1)
                A(rst[:, C:2 * C], ps[0:H, 7, 0:C], ACT.Sqrt, bias=tiny[0:H, 1:2], scale=1.0 / HD).then_inc(sem("y_std"), 1)

            def gn_upper(c):
                if c < NCH - 1:
                    act.wait_ge(sem("y_gated"), 2 * c + 2)
                else:
                    act.wait_ge(sem("y_last"), 2)
                A(yh[:, :, c * C:(c + 1) * C], YF[c % 2][:, :, :], ACT.Copy).then_inc(sem("yh_ready"), 1)

            for c in range(NCH):
                for half in range(2):
                    act.wait_ge(sem(f"xs_pe{half}"), c + 1)
                    if c == 0:
                        act.wait_ge(sem("u_zero"), 1)
                    A(XS[half][0:HD, :, 0, :], quarter(ps[0:HD, 3 * half, 0:GW]), ACT.Copy).then_inc(sem(f"x_even{half}"), 1)
                if c:
                    gn_square(c - 1)
                act.wait_ge(sem("u_pe0"), c + 1)
                A(UV[0:HD, c, 0:512], ps[0:HD, 1, :], ACT.Copy).then_inc(sem("u_sb0"), 1)
                if c:
                    gn_sqrt(c - 1)
                for half in range(2):
                    act.wait_ge(sem(f"y_pe{half}"), c + 1)
                    A(AR[:, half * 4:half * 4 + 4, c, 1, :], quarter(ps[:, 3 * half + 2, 0:GW]), ACT.Copy)\
                        .then_inc(sem(f"y_copied{half}"), 1)
                if c >= 2:
                    gn_upper(c - 2)
            gn_square(NCH - 1)
            gn_upper(NCH - 2)
            gn_sqrt(NCH - 1)
            gn_upper(NCH - 1)
            for j in range(8):
                ahead(U0["o0"] + j)

            def x_parts(n):
                for m in range(4):
                    act.wait_ge(sem("xn_ready"), 4 * n + m + 1)
                    A(xh[0][:, 2 * m:2 * m + 2, :], xn[:, 2 * m:2 * m + 2, :], ACT.Copy).then_inc(sem("xh_ready"), 1)

            def mlp_act(n1, n2, base_):
                def turn(i, gg, steady):
                    act.wait_ge(unit_used, i * 4 + (U0[n1] + 2 * gg + 2))
                    if steady:
                        act.wait_ge(sem("sq_used"), i * 2 + (base_ + gg - 1))
                    A(rl[:, gg, :, :], ps[:, 2 * gg:2 * gg + 2, 0:T], ACT.Relu).then_inc(ev_act, 1)
                    for j in range(2):
                        u = U0[n1] + 2 * gg + j + RING
                        act.wait_ge(raw_in[2 * gg + j], i * 16 + 16 * (u // RING + 1))
                        act.wait_ge(unit_used, i * 4 + (u - RING + 1))
                        A(whi[:, 2 * gg + j, :], raw[:, 2 * gg + j, :], ACT.Copy).then_inc(hi_ready, 1)
                    act.wait_ge(ev_act, i * 2 + (EV0[n1] + gg + 1))
                    A(hh[:, ds(i * 4 + 2 * gg, 2), :], rl[:, gg, :, :], ACT.Square).then_inc(sem("hh_ready"), 1)

                for gg in range(2):
                    turn(0, gg, False)
                with act.Fori(1, 8) as i:
                    for gg in range(2):
                        turn(i, gg, True)
                with act.Fori(0, 3) as i:
                    for j in range(8):
                        u = U0[n2] + j + RING
                        act.wait_ge(raw_in[j % RING], i * 32 + 16 * (u // RING + 1))
                        act.wait_ge(unit_used, i * 8 + (u - RING + 1))
                        A(whi[:, j % RING, :], raw[:, j % RING, :], ACT.Copy).then_inc(hi_ready, 1)
                for j in range(24, 32):
                    ahead(U0[n2] + j)

            norm_act(1)
            x_parts(0)
            mlp_act("a1", "a2", 0)
            norm_act(2)
            x_parts(1)
            def evac(name, g, dst):
                act.wait_ge(unit_used, U0[name] + 2 * g + 2)
                A(dst, ps[:, 2 * (g % 2):2 * (g % 2) + 2, 0:T], ACT.Copy).then_inc(ev_act, 1)
                ahead(U0[name] + 2 * g)
                ahead(U0[name] + 2 * g + 1)

            evac("kc", 0, kv[:, 0, :, :])
            evac("kc", 1, kv[:, 1, :, :])
            evac("q", 0, Qn[:, 0:2, :])
            act.wait_ge(sem("gate_pe"), 1)
            A(gcol[:, :], ps[0:NG, 4, 0:T], ACT.Sigmoid).then_inc(sem("gates_r"), 1)
            evac("q", 1, Qn[:, 2:4, :])
            act.wait_ge(sem("rows_T"), 1)
            A(gat[:, :, :], ps[:, 5, 0:128].rearrange("p (q n) -> p q n", q=TT)[:, :, 0:NG], ACT.Copy)\
                .then_inc(sem("gates_r"), 1)
            evac("q", 2, Qn[:, 4:6, :])
            act.wait_ge(sem("gelu_in"), 1)
            A(gt[:, :, :], gt[:, :, :], ACT.Sigmoid, scale=GELU_A).then_inc(sem("gelu_sig"), 1)
            evac("q", 3, Qn[:, 6:8, :])
            act.wait_ge(ev_act, EV0["q"] + 4)
            A(qss[:, :, :], Qn[:, :, :], ACT.Square).then_inc(sem("qsq"), 1)
            evac("kv", 0, kv[:, 2, :, :])
            act.wait_ge(sem("cmp2_pe"), 1)
            act.wait_ge(sem("hid_k"), 1)
            A(gu[:, 0, :], ps[:, 5, 0:HKV * NB], ACT.Square).then_inc(sem("kcsq"), 1)
            act.wait_ge(sem("zeroed"), 11)
            for a in range(4):
                o = vblk[32 * a:32 * a + 32, :, a * HD:(a + 1) * HD]
                i_ = ps[32 * a:32 * a + 32, 5, 128:128 + HKV * HD].rearrange("p (j n) -> p j n", n=HD)
                A(o, i_, ACT.Copy).then_inc(sem("vblk_r"), 1)
            act.wait_ge(sem("q_sum"), 1)
            A(qkr[:, 0, :], ps[0:H, 6, 0:T], ACT.Sqrt, bias=tiny[0:H, 3:4]).then_inc(sem("q_root"), 1)
            evac("kv", 1, kv[:, 3, :, :])
            act.wait_ge(sem("kc_pe"), 1)
            A(gu[:, 1, :], ps[:, 4, 0:HKV * NB], ACT.Sqrt, bias=tiny[:, 0:1], scale=1.0 / HD).then_inc(sem("kcrs"), 1)
            act.wait_ge(ev_act, EV0["kv"] + 2)
            A(ksq[:, :, :, :], kv[:, 2:4, :, :], ACT.Square).then_inc(sem("ksq_r"), 1)
            evac("kv", 2, vt[:, 0, :, :])
            act.wait_ge(sem("k_sum"), 1)
            A(qkr[:, 2, :], ps[0:H, 4, 0:T], ACT.Sqrt, bias=tiny[0:H, 0:1], scale=1.0 / HD).then_inc(sem("k_root"), 1)
            evac("kv", 3, vt[:, 1, :, :])
            for b in range(2):
                for e in range(2):
                    act.wait_ge(sem("kd_ready"), 2 * b + e + 1)
                    own, other = (slice(HD * x, HD * x + HD) for x in (e, 1 - e))
                    view = kd[:, b, :, :].rearrange("p (m a) t -> p m a t", a=2)
                    A(view[other, :, e, :], view[own, :, e, :], ACT.Copy).then_inc(sem("kd_copied"), 1)
            act.wait_ge(sem("csub"), 1)
            A(Sc[:, :, :, 0:16], Sc[:, :, :, 0:16], ACT.Exp).then_inc(sem("cexp"), 1)
            act.wait_ge(sem("pct_pe"), 1)
            A(PcT[:, :, :, :].rearrange("p q j n -> p q (j n)"), ps[:, 4:6, :], ACT.Copy).then_inc(sem("pct_r"), 1)
            items = [(j, q, b) for j in range(HKV) for q in range(TT) for b in range(2)]

            def exps(n):
                j, q, b = items[n]
                w = (q + 1) * P
                act.wait_ge(sem("mx_ready"), n + 1)
                for i in range(4):
                    hd = 4 * j + i
                    o = A(SB[n % 4][:, i, 0:w], SB[n % 4][:, i, 0:w], ACT.Exp, bias=nmx[:, n % 4, i:i + 1],
                          accum_out=den[:, q, b, hd:hd + 1])
                    step(o)
                settle()
                act.sem_inc(sem("p_ready"), 1)

            def pt_copy(n):
                j, q, b = items[n]
                act.wait_ge(sem("t_pe"), n + 1)
                if n >= 2:
                    act.wait_ge(sem("pv_pe"), n - 1)
                A(PT[:, n % 2, :, 0:q + 1, :].rearrange("p i s t -> p s i t"),
                  ps[:, 4:5 + q, :].rearrange("p s (i t) -> p s i t", t=P), ACT.Copy).then_inc(sem("pt_read"), 1)

            def out_upper(g):
                j, q = g // 2, g % 2
                act.wait_ge(sem("o_read"), g + 1)
                A(xh[1][:, 2 * j:2 * j + 2, q * P:(q + 1) * P], Of[:, g % 2, :, :], ACT.Copy).then_inc(sem("att_upper"), 1)

            for n in range(len(items) + 2):
                if n < len(items):
                    exps(n)
                if n >= 2:
                    pt_copy(n - 2)
                if n >= 7 and n % 2 == 1:
                    out_upper((n - 7) // 2)
            for g in range(len(items) // 2 - 2, len(items) // 2):
                out_upper(g)
            for j in range(8):
                ahead(U0["o1"] + j)
            norm_act(3)
            x_parts(2)
            mlp_act("b1", "b2", 16)
            for q in range(TT):
                act.wait_ge(sem("fin_pe"), q + 1)
                A(otok[:, q, :].rearrange("p (b n) -> p b n", b=2), ps[:, 4 + 2 * q:6 + 2 * q, :], ACT.Copy)\
                    .then_inc(sem("out_ready"), 1)

        @block.vector
        def _(dve):
            v = nc.vector
            down = sem("dve_step")
            cnt = [0]

            def step(ins):
                cnt[0] += 1
                ins.then_inc(down, 1)

            def settle():
                dve.wait_ge(down, cnt[0])

            def rest(slot, hi_count):
                dve.wait_ge(hi_ready, hi_count)
                v.tensor_tensor(wlo[:, slot, :], raw[:, slot, :], whi[:, slot, :].bitcast(f32), ALU.subtract)\
                    .then_inc(lo_ready, 1)

            def ahead(u):
                if u + RING < NU:
                    rest((u + RING) % RING, u + RING + 1)

            v.memset(tiny[:, 0:1], EPS).then_inc(sem("eps_set"), 1)
            v.memset(tiny[:, 1:2], GN_EPS).then_inc(sem("eps_set"), 1)
            v.memset(tiny[:, 3:4], HD * EPS).then_inc(sem("eps_set"), 1)
            dve.wait_ge(sem("par_t"), 1)
            v.tensor_copy(par[:, 0:NPAR], ps[:, 5, 0:NPAR]).then_inc(sem("par_r"), 1)
            dve.wait_ge(sem("par_r"), 1)

            def lower(src, x, n):
                part = slice(2 * n, 2 * n + 2)
                dve.wait_ge(sem("xh_ready"), XH0[x] + n + 1)
                v.tensor_tensor(xl[0][:, part, :], src[:, part, :], xh[0][:, part, :].bitcast(f32), ALU.subtract)\
                    .then_inc(sem("xl_dve"), 1)

            def mix_pair(mu, dst, n):
                for k in (2 * n, 2 * n + 1):
                    step(v.scalar_tensor_tensor(dst[:, k, :], dx[:, k, :], pv(f"mu{mu}", k), xn[:, k, :], ALU.mult, ALU.add))
                settle()
                dve.sem_inc(sem("mix_ready"), 1)

            def norm_dve(i, g):
                x = ["r", "a", "nsa", "b"][i]
                if i == 0:
                    dve.wait_ge(ev_act, 4)
                    rest(0, 1)
                    rest(1, 2)
                dve.wait_ge(sem("rs_ready"), i + 1)
                step(v.reciprocal(ri[:, :], rs[:, :]))
                settle()
                for n in range(4):
                    part = slice(2 * n, 2 * n + 2)
                    for k in (2 * n, 2 * n + 1):
                        step(v.scalar_tensor_tensor(xn[:, k, :], h[:, k, :], pv(g, k), ri[:, :], ALU.mult, ALU.mult))
                    settle()
                    if i:
                        dve.sem_inc(sem("xn_ready"), 1)
                    else:
                        step(v.tensor_tensor(dx[:, part, 1:T], xn[:, part, 0:T - 1], xn[:, part, 1:T], ALU.subtract))
                        step(v.tensor_scalar(dx[:, part, 0:1], xn[:, part, 0:1], -1.0, None, ALU.mult))
                        settle()
                        mix_pair(0, mix[1], n)
                    if n and i:
                        lower(xn, x, n - 1)
                dve.sem_inc(sem("xn_done"), 1)
                if i:
                    lower(xn, x, 3)

            norm_dve(0, "mix0")

            def mixing(mu, dst):
                for n in range(4):
                    mix_pair(mu, dst, n)

            def ahead2(name, j):
                ahead(U0[name] + j)
                ahead(U0[name] + j + 1)

            for u in range(2, RING):
                rest(u, u + 1)
            mix_pair(2, mix[0], 0)
            mix_pair(2, mix[0], 1)
            ahead2("r", 0)
            mix_pair(2, mix[0], 2)
            mix_pair(2, mix[0], 3)
            ahead2("r", 2)
            dve.wait_ge(sem("xl_pool"), 4)
            mixing(1, mix[1])
            dve.wait_ge(sem("xh_ready"), XH0["k"] + 4)
            dve.wait_ge(sem("xl_pool"), 6)
            mixing(4, mix[0])
            ahead2("r", 4)
            ahead2("r", 6)
            dve.wait_ge(sem("lora_h"), 1)
            mixing(5, mix[1])
            dve.wait_ge(sem("lora_h"), 2)
            mixing(3, mix[0])
            for j in range(8):
                ahead(U0["k"] + j)

            def wide(name):
                return par[:, pcol[name]:pcol[name] + FT].unsqueeze(2).broadcast_to([P, FT, T])

            dve.wait_ge(sem("lora_h"), 3)
            dve.wait_ge(ev_act, EV0["k"] + 4)
            v.tensor_tensor(KK[:, :, :], K[:, :, :], wide("k_k"), ALU.mult).then_inc(sem("kk_raw"), 1)
            dve.wait_ge(ev_act, EV0["up"] + 4)
            dve.wait_ge(sem("cst_rest"), 16)
            for k in range(FT):
                step(v.tensor_tensor_scan(CSm[:, k, :], cc("chunk"), Sg[:, k, :], 0.0, ALU.mult, ALU.add))
            settle()
            dve.sem_inc(sem("cs_ready"), 1)
            dve.wait_ge(ev_act, EV0["up"] + 8)
            dve.wait_ge(sem("kk_raw"), 1)
            for k in range(FT):
                step(v.tensor_scalar(t11[:, k, :], Ai[:, k, :], 1.0, pv("k_a", k), ALU.subtract, ALU.mult))
            settle()
            step(v.scalar_tensor_tensor(K[:, :, :], t11[:, :, :], 1.0, K[:, :, :], ALU.add, ALU.mult))
            settle()
            dve.wait_ge(sem("kk_root"), 1)
            step(v.tensor_scalar(kkr[:, 1, :], kkr[:, 0, :], 1e-12, None, ALU.max))
            settle()
            v.reciprocal(kkr[:, 1, :], kkr[:, 1, :]).then_inc(sem("kk_inv"), 1)
            for k in range(FT):
                step(v.scalar_tensor_tensor(t11[:, k, :], R[:, k, :], pv("r_k", k), K[:, k, :], ALU.mult, ALU.mult))
            settle()
            dve.sem_inc(sem("rk"), 1)
            ch = lambda x: x[:, :, :].rearrange("p k (c n) -> p (k c) n", n=C)
            arv = lambda x, n: x[:, :, :, n, :].rearrange("p k c n -> p (k c) n")
            dve.wait_ge(ev_act, EV0["up"] + 12)
            dve.wait_ge(sem("e1_ready"), 1)
            step(v.tensor_tensor(arv(AR, 1), ch(R), ch(E1), ALU.mult))
            step(v.tensor_copy(PC[:, :, :], E1[:, :, :].rearrange("p k (c n) -> p k c n", n=C)[:, :, :, C - 1]))
            dve.wait_ge(sem("kk_spread"), 1)
            v.tensor_tensor(KK[:, :, :].rearrange("p (b k) t -> p b (k t)", b=4), KK[:, :, :].rearrange("p (b k) t -> p b (k t)", b=4),
                            ps[:, 4:8, :], ALU.mult).then_inc(sem("kkn_used"), 1)
            ahead2("v", 0)
            dve.wait_ge(sem("e2_ready"), 1)
            step(v.tensor_tensor(arv(BK, 1), ch(K), ch(E2), ALU.mult))
            settle()
            dve.sem_inc(sem("rk_done"), 1)
            dve.sem_inc(sem("bk_ready"), 1)
            dve.sem_inc(sem("ar_ready"), 1)
            dve.wait_ge(sem("e3_ready"), 1)
            dve.wait_ge(sem("kkn_used"), 1)
            step(v.scalar_tensor_tensor(arv(AR, 0), ch(KK), -1.0, ch(E3), ALU.mult, ALU.mult))
            settle()
            dve.sem_inc(sem("ar_ready"), 1)
            ahead2("v", 2)
            ahead2("v", 4)
            ahead2("v", 6)
            dve.wait_ge(sem("bk_ready"), 2)
            dve.wait_ge(sem("bkT"), 2)
            v.tensor_copy(BKT[:, 1, :].rearrange("p (b n) -> p b n", b=2), ps[:, 6:8, :]).then_inc(sem("bkt_dve"), 1)
            dve.wait_ge(sem("vT"), 2)
            for n in range(2):
                v.tensor_copy(UV[HD:P, 2 + n, :].rearrange("p (b n) -> p b n", b=2),
                              ps[HD * n:HD * n + HD, 2:4, :]).then_inc(sem("bkt_dve"), 1)

            def mask_g(half):
                for n in range(8):
                    dve.wait_ge(sem("g_done"), 8 * half + n + 1)
                    if n == 0 and half == 0:
                        for s in range(2):
                            dve.wait_ge(sem(f"inv_pool{s}"), 4 * NPAIR)
                    v.tensor_tensor(Gs[half][:, n, :, :], ps[:, n, :].rearrange("p (c n) -> p c n", c=NCH),
                                    cc("gmask").unsqueeze(1).broadcast_to([P, NCH, 2 * C]), ALU.mult)\
                        .then_inc(sem("g_masked"), 1)

            dve.wait_ge(sem("zeroed"), 2)
            for pair in range(NPAIR):
                for n in (0, 1, 2, 3, 4, 6, 8):
                    for s in range(2):
                        done = sem(f"inv_dve{s}")
                        dve.wait_ge(sem(f"inv_pe{s}"), 9 * pair + n + 1)
                        b = 4 * s + 2 * ((n + pair) % 2)
                        wide_ = ps[:, b:b + 2, :].rearrange("p b (k a n) -> p (b k) a n", a=2, n=C)
                        power, more = wide_[:, :, 0, :], wide_[:, :, 1, :]
                        prod = DP[s][:, :, 1, :]

                        def halves(e):
                            return slice(HD * e, HD * e + HD)

                        def diagonal(e):
                            return LT[s][halves(e), :, e * C:(e + 1) * C]

                        def turn_over(src):
                            for e in range(2):
                                v.transpose(diagonal(e), src[halves(e)]).then_inc(done, 1)

                        if n <= 2:
                            dve.wait_ge(sem(f"inv_act{s}"), 5 * pair + n + 1)
                        if n == 0:
                            for e in range(2):
                                v.tensor_tensor(diagonal(e), Lr[s][halves(e), :, :],
                                                cc("lmask16", HD * e, HD * e + HD).unsqueeze(1).broadcast_to([HD, NP_, C]),
                                                ALU.mult).then_inc(done, 1)
                            for e in range(2):
                                dve.wait_ge(done, 20 * pair + e + 1)
                                v.transpose(DP[s][halves(e), :, 0, :], diagonal(e)).then_inc(done, 1)
                            dve.wait_ge(done, 20 * pair + 4)
                            v.tensor_tensor(prod, DP[s][:, :, 0, :], cc("eye64").unsqueeze(1).broadcast_to([P, NP_, C]),
                                            ALU.add).then_inc(done, 1)
                        elif n == 1:
                            turn_over(DP[s][:, :, 0, :])
                        elif n in (2, 3):
                            turn_over(DP[s][:, :, 0, :] if n == 2 else power)
                            v.tensor_tensor(prod, prod, more, ALU.add).then_inc(done, 1)
                        elif n in (4, 6):
                            v.tensor_tensor(prod, prod, more if n == 4 else power, ALU.add).then_inc(done, 1)
                            dve.wait_ge(done, 20 * pair + {4: 14, 6: 17}[n])
                            turn_over(prod)
                        else:
                            p0 = (2 * pair + s) * NP_
                            v.tensor_tensor(Rinv[:, p0:p0 + NP_, :], prod, power, ALU.add).then_inc(done, 1)
            mask_g(0)
            mask_g(1)

            def gn_rstd(c):
                dve.wait_ge(sem("y_std"), c + 1)
                step(v.reciprocal(rst[:, 0:C], rst[:, C:2 * C]))
                settle()
                v.tensor_tensor(rsb[:, :, :], rst[:, 0:C].unsqueeze(1).broadcast_to([H, FT, C]),
                                spread[:, D:D + FT].unsqueeze(2).broadcast_to([H, FT, C]), ALU.mult).then_inc(sem("y_rstd"), 1)

            def gn_scale(c):
                dve.wait_ge(sem("rstd_pe"), c + 1)
                if c >= 2:
                    dve.wait_ge(sem("yh_ready"), c - 1)
                    dve.wait_ge(sem("yl_ready"), c - 1)
                dve.wait_ge(sem("yc"), c + 1)
                v.tensor_tensor(YF[c % 2][:, :, :], YC[:, :, :],
                                ps[:, 7, :].rearrange("p (k n) -> p k n", n=C), ALU.mult).then_inc(sem("y_scaled"), 1)

            for c in range(NCH):
                if c >= 2:
                    gn_scale(c - 2)
                for half in range(2):
                    dve.wait_ge(sem(f"xs_pe{half}"), c + 1)
                    if c == 0:
                        dve.wait_ge(sem("u_zero"), 1)
                    v.tensor_copy(XS[half][HD:P, :, 1, :], ps[HD:P, 3 * half, 0:GW].rearrange("p (k n) -> p k n", n=C))\
                        .then_inc(sem(f"x_odd{half}"), 1)
                dve.wait_ge(sem("u_pe1"), c + 1)
                v.tensor_copy(UV[0:HD, c, 512:1024], ps[0:HD, 4, :]).then_inc(sem("u_sb1"), 1)
                if c < NCH - 1:
                    for half in range(2):
                        dve.wait_ge(sem(f"s_pe{half}"), c + 1)
                        s_in = ps[:, 3 * half, 0:GW].rearrange("p (k n) -> p k n", n=C)
                        pc = PC[:, half * 4:half * 4 + 4, c:c + 1].broadcast_to([P, FT // 2, C])
                        if c:
                            step(v.tensor_tensor(STt[half][:, :, :], s_in, ST[half][(c - 1) % 2][:, :, :], ALU.add))
                            settle()
                            s_in = STt[half][:, :, :]
                        if c >= 2:
                            dve.wait_ge(sem(f"y_pe{half}"), c)
                        v.tensor_tensor(ST[half][c % 2][:, :, :], s_in, pc, ALU.mult).then_inc(sem(f"st_ready{half}"), 1)
                        dve.wait_ge(sem(f"st_ready{half}"), c + 1)
                if c:
                    gn_rstd(c - 1)
            gn_scale(NCH - 2)
            gn_rstd(NCH - 1)
            gn_scale(NCH - 1)
            tok = slice((NCH - 1) * C, T)
            y = YF[(NCH - 1) % 2][:, :, :]
            dve.wait_ge(sem("gate_folded"), 3)
            dve.wait_ge(sem("y_scaled"), NCH)
            v.tensor_tensor(y, y, Gt[:, :, tok], ALU.mult).then_inc(sem("y_last"), 1)
            dve.wait_ge(sem("y_last"), 1)
            v.tensor_tensor(y, y, t11[:, :, tok], ALU.add).then_inc(sem("y_last"), 1)
            dve.wait_ge(sem("yh_ready"), NCH)
            v.tensor_tensor(yl[:, :, tok], y, yh[:, :, tok].bitcast(f32), ALU.subtract).then_inc(sem("yl_last"), 1)

            def residual(name):
                for g in range(4):
                    dve.wait_ge(unit_used, U0[name] + 2 * g + 2)
                    v.tensor_tensor(h[:, 2 * g:2 * g + 2, :], h[:, 2 * g:2 * g + 2, :],
                                    ps[:, 2 * (g % 2):2 * (g % 2) + 2, 0:T], ALU.add).then_inc(ev_dve, 1)
                    ahead(U0[name] + 2 * g)
                    ahead(U0[name] + 2 * g + 1)

            def mlp_dve(n1, n2, base_):
                def turn(i, gg, steady):
                    dve.wait_ge(ev_act, i * 2 + (EV0[n1] + gg + 1))
                    v.tensor_tensor(s2[:, gg, :, :], rl[:, gg, :, :], rl[:, gg, :, :], ALU.mult).then_inc(sem("s2_ready"), 1)
                    dve.wait_ge(sem("hh_ready"), i * 2 + (base_ + gg + 1))
                    dve.wait_ge(sem("s2_ready"), i * 2 + (base_ + gg + 1))
                    dve.sem_inc(sem("sq_used"), 1)
                    v.tensor_tensor(hl[:, ds(i * 4 + 2 * gg, 2), :], s2[:, gg, :, :],
                                    hh[:, ds(i * 4 + 2 * gg, 2), :].bitcast(f32), ALU.subtract).then_inc(sem("hid_ready"), 1)
                    for j in range(2):
                        u = U0[n1] + 2 * gg + j + RING
                        rest(2 * gg + j, i * 4 + (u + 1))

                with dve.Fori(0, 8) as i:
                    for gg in range(2):
                        turn(i, gg, True)
                for g in range(4):
                    for j in range(8):
                        ahead(U0[n2] + 8 * g + j)
                    dve.wait_ge(unit_used, U0[n2] + 8 * g + 8)
                    v.tensor_tensor(h[:, 2 * g:2 * g + 2, :], h[:, 2 * g:2 * g + 2, :],
                                    ps[:, 2 * (g % 2):2 * (g % 2) + 2, 0:T], ALU.add).then_inc(ev_dve, 1)

            residual("o0")
            norm_dve(1, "mlp0")
            mlp_dve("a1", "a2", 0)
            norm_dve(2, "mix1")

            for j in range(4):
                ahead(U0["kc"] + j)
            ahead2("q", 0)
            dve.wait_ge(sem("gate_pe"), 1)
            v.tensor_copy(pec[:, :], ps[:, 5, 0:2 * CB]).then_inc(sem("pe_col"), 1)
            dve.wait_ge(sem("pe_col"), 1)
            dve.wait_ge(ev_act, EV0["kc"] + 2)
            for b in range(2):
                for j in range(HKV):
                    e, m = j % 2, j // 2
                    for half in range(2):
                        src = kv[HD * e:HD * e + HD, b, m, CS * half:CS * half + CS * NB].rearrange("p (n l) -> p l n", l=CS)
                        emb = pec[HD * e:HD * e + HD, b * CB + CS * half:b * CB + CS * half + CS].unsqueeze(2)\
                            .broadcast_to([HD, CS, NB])
                        step(v.tensor_tensor(Zc[HD * half:HD * half + HD, b, :, j * NB:(j + 1) * NB], src, emb, ALU.add))
                ahead2("q", 2 + 2 * b)
            settle()
            dve.sem_inc(sem("zc"), 1)
            dve.wait_ge(sem("cmp_pe"), 1)
            step(v.tensor_copy(ht[:, :, :], ps[0:HKV * NB, 4, 0:2 * P].rearrange("p (b n) -> p b n", b=2)))
            settle()
            step(v.tensor_tensor(gt[:, :, :], ht[:, :, :], ht[:, :, :], ALU.mult))
            settle()
            step(v.tensor_scalar(gt[:, :, :], gt[:, :, :], GELU_B, 1.0, ALU.mult, ALU.add))
            settle()
            v.tensor_tensor(gt[:, :, :], gt[:, :, :], ht[:, :, :], ALU.mult).then_inc(sem("gelu_in"), 1)
            dve.wait_ge(sem("gelu_sig"), 1)
            v.tensor_tensor(ht[:, :, :], ht[:, :, :], gt[:, :, :], ALU.mult).then_inc(sem("hid_rows"), 1)
            ahead2("q", 6)
            dve.wait_ge(sem("rows_T"), 2)
            dve.wait_ge(sem("zeroed"), 11)
            step(v.tensor_copy(hid[:, 0, :], ps[:, 5, 0:HKV * NB]))
            step(v.tensor_copy(hpad[:, :, :, 0:NB], ps[:, 5, 64:64 + HKV * NB].rearrange("p (j n) -> p j n", n=NB).unsqueeze(2)
                               .broadcast_to([P, HKV, 4, NB])))
            settle()
            dve.sem_inc(sem("hid_k"), 1)
            ahead2("kv", 0)
            dve.wait_ge(sem("q_root"), 1)
            v.reciprocal(qkr[:, 1, :], qkr[:, 0, :]).then_inc(sem("q_inv"), 1)
            ahead2("kv", 2)

            def scale_q(half):
                x = Qn[:, 4 * half:4 * half + 4, :].rearrange("p (b k) t -> p b (k t)", b=2)
                dve.wait_ge(sem("q_spread"), half + 1)
                v.scalar_tensor_tensor(x, x, pv("qn"), ps[:, 6:8, :], ALU.mult, ALU.mult).then_inc(sem("q_scaled"), 1)

            dve.wait_ge(sem("qsq"), 1)
            scale_q(0)
            dve.wait_ge(sem("kcrs"), 1)
            step(v.reciprocal(gu[:, 1, :], gu[:, 1, :]))
            settle()
            dve.wait_ge(sem("zeroed"), 12)
            for e in range(2):
                q = slice(HD * e, HD * e + HD)
                view = lambda x: x.rearrange("p (j n) -> p j n", n=NB)
                v.scalar_tensor_tensor(kcm[q, :, e, 0:NB], view(ps[q, 5, 0:HKV * NB]), par[q, pcol["kn0"]:pcol["kn0"] + 1],
                                       view(gu[q, 1, :]), ALU.mult, ALU.mult).then_inc(sem("kcm_r"), 1)
            ahead2("kv", 4)
            scale_q(1)
            dve.wait_ge(sem("k_root"), 1)
            v.reciprocal(qkr[:, 3, :], qkr[:, 2, :]).then_inc(sem("k_inv"), 1)
            ahead2("kv", 6)
            dve.wait_ge(sem("k_spread"), 1)
            for b in range(2):
                for e in range(2):
                    src = slice(HD * e, HD * e + HD)
                    g = par[src, pcol[f"kn{b + 1}"]:pcol[f"kn{b + 1}"] + 1]
                    dst = kd[src, b, :, :].rearrange("p (m a) t -> p m a t", a=2)[:, :, e, :]
                    v.scalar_tensor_tensor(dst, kv[src, 2 + b, :, :], g, ps[src, 4 + b, :].rearrange("p (m t) -> p m t", t=T),
                                           ALU.mult, ALU.mult).then_inc(sem("kd_ready"), 1)
            adc = cc("adc").rearrange("p (q h n) -> p q h n", q=TT, n=16)
            dve.wait_ge(sem("sc_pe"), 1)
            step(v.tensor_tensor(Sc[:, :, :, 0:NB], ps[:, 6, :].rearrange("p (q h n) -> p q h n", q=TT, n=16)[:, :, :, 0:NB],
                                 adc[:, :, :, 0:NB], ALU.add))
            settle()
            step(v.tensor_reduce(csm[:, 0, :, :], Sc[:, :, :, 0:NB], AXX, ALU.max))
            settle()
            step(v.tensor_scalar(csm[:, 0, :, :], csm[:, 0, :, :], FLOOR, None, ALU.max))
            settle()
            cb = lambda n: csm[:, n, :, :].unsqueeze(3).broadcast_to([P, TT, H, NB])
            v.tensor_tensor(Sc[:, :, :, 0:NB], Sc[:, :, :, 0:NB], cb(0), ALU.subtract).then_inc(sem("csub"), 1)
            dve.wait_ge(sem("cexp"), 1)
            step(v.tensor_reduce(csm[:, 1, :, :], Sc[:, :, :, 0:NB], AXX, ALU.add))
            settle()
            step(v.tensor_scalar(csm[:, 1, :, :], csm[:, 1, :, :], 1e-30, None, ALU.max))
            settle()
            step(v.reciprocal(csm[:, 2, :, :], csm[:, 1, :, :]))
            settle()
            gv = gat[:, :, :].rearrange("p q (h b) -> p q h b", b=3)
            dve.wait_ge(sem("gates_r"), 2)
            step(v.tensor_tensor(csm[:, 3, :, :], csm[:, 2, :, :], gv[:, :, :, 0], ALU.mult))
            settle()
            step(v.tensor_tensor(Sc[:, :, :, 0:NB], Sc[:, :, :, 0:NB], cb(3), ALU.mult))
            step(v.memset(Sc[:, :, :, NB:16], 0.0))
            settle()
            dve.sem_inc(sem("pc_ready"), 1)

            items = [(j, q, b) for j in range(HKV) for q in range(TT) for b in range(2)]
            dist = cc("dist")

            def soft(n):
                j, q, b = items[n]
                w = (q + 1) * P
                d = dist[:, 0:P] if q == 0 else dist[:, P:P + T]
                dve.wait_ge(sem("s_pe2"), n + 1)
                if n >= 4:
                    dve.wait_ge(sem("t_pe"), n - 3)
                for i in range(4):
                    step(v.scalar_tensor_tensor(SB[n % 4][:, i, 0:w], d, -SLOPES[4 * j + i],
                                                ps[:, 2 * (n % 2) + i % 2, (i // 2) * T:(i // 2) * T + w], ALU.mult, ALU.add))
                settle()
                dve.sem_inc(sem("s_read"), 1)
                step(v.tensor_reduce(nmx[:, n % 4, :], SB[n % 4][:, :, 0:w], AXX, ALU.max))
                settle()
                v.tensor_scalar(nmx[:, n % 4, :], nmx[:, n % 4, :], -1.0, None, ALU.mult).then_inc(sem("mx_ready"), 1)

            def coefficient(n):
                j, q, b = items[n]
                hs = slice(4 * j, 4 * j + 4)
                c_ = cof[:, q, b, hs]
                dve.wait_ge(sem("p_ready"), n + 1)
                step(v.tensor_scalar(c_, den[:, q, b, hs], 1e-30, None, ALU.max))
                settle()
                step(v.reciprocal(c_, c_))
                settle()
                v.tensor_tensor(c_, c_, gv[:, q, hs, 1 + b], ALU.mult).then_inc(sem("cof_ready"), 1)

            def take_out(g):
                dve.wait_ge(sem("pv_pe"), 2 * g + 2)
                if g >= 2:
                    dve.wait_ge(sem("att_upper"), g - 1)
                    dve.wait_ge(sem("att_lower"), g - 1)
                for e in range(2):
                    step(v.tensor_copy(Of[HD * e:HD * e + HD, g % 2, :, :],
                                       ps[0:HD, 6 + g % 2, :].rearrange("p (k a t) -> p k a t", a=2, t=P)[:, :, e, :]))
                settle()
                dve.sem_inc(sem("o_read"), 1)

            def out_lower(g):
                j, q = g // 2, g % 2
                part = (slice(None), slice(2 * j, 2 * j + 2), slice(q * P, (q + 1) * P))
                dve.wait_ge(sem("att_upper"), g + 1)
                v.tensor_tensor(xl[1][part], Of[:, g % 2, :, :], xh[1][part].bitcast(f32), ALU.subtract)\
                    .then_inc(sem("att_lower"), 1)

            NI = len(items)
            for n in range(NI + 1):
                if n < NI:
                    soft(n)
                if n >= 1:
                    coefficient(n - 1)
                if n >= 6 and n % 2 == 0:
                    take_out((n - 6) // 2)
                if n >= 8 and n % 2 == 0:
                    out_lower((n - 8) // 2)
            for g in range(NI // 2 - 2, NI // 2):
                take_out(g)
                out_lower(g - 1)
            out_lower(NI // 2 - 1)
            residual("o1")
            norm_dve(3, "mlp1")
            mlp_dve("b1", "b2", 16)

        @block.gpsimd
        def _(pool):
            g = nc.gpsimd

            def lower(dst, src, hi, x):
                w = XL0[x][2]
                for n in range(w):
                    part = slice(n * FT // w, (n + 1) * FT // w)
                    pool.wait_ge(sem("xh_ready"), XH0[x] + (n + 1) * 4 // w)
                    g.tensor_tensor(dst[:, part, :], src[:, part, :], hi[:, part, :].bitcast(f32), ALU.subtract)\
                        .then_inc(sem("xl_pool"), 1)

            lower(xl[0], mix[1], xh[0], "r")
            lower(xl[1], mix[0], xh[1], "k")
            lower(xl[0], mix[0], xh[0], "v")
            pool.wait_ge(sem("cs_ready"), 1)
            g.tensor_tensor(Sg[:, :, :], CSm[:, :, :], Sg[:, :, :], ALU.subtract).then_inc(sem("ex_ready"), 1)
            pool.wait_ge(sem("kkn_used"), 1)
            g.tensor_tensor(Ai[:, :, :], KK[:, :, :], Ai[:, :, :], ALU.mult).then_inc(sem("b_ready"), 1)
            pool.wait_ge(sem("e2_ready"), 1)
            pool.wait_ge(sem("b_ready"), 1)
            g.tensor_tensor(BK[:, :, :, 0, :].rearrange("p k c n -> p (k c) n"),
                            Ai[:, :, :].rearrange("p k (c n) -> p (k c) n", n=C),
                            E2[:, :, :].rearrange("p k (c n) -> p (k c) n", n=C), ALU.mult).then_inc(sem("bk_ready"), 1)
            pool.wait_ge(sem("bk_ready"), 2)
            pool.wait_ge(sem("rk_copied"), 1)
            pool.wait_ge(ev_act, EV0["v"] + 4)
            g.tensor_tensor(t11[:, :, :], t11[:, :, :], V[:, :, :], ALU.mult).then_inc(sem("bonus"), 1)
            pool.wait_ge(sem("bonus"), 1)
            pool.wait_ge(sem("ar_ready"), 2)
            for x in LT + E32 + E64:
                g.memset(x[:, :, :], 0.0).then_inc(sem("zeroed"), 1)
            pool.wait_ge(sem("zeroed"), 6)
            for pair in range(NPAIR):
                for s in range(2):
                    pool.wait_ge(sem(f"inv_act{s}"), 5 * pair + 1)
                    if pair:
                        pool.wait_ge(sem(f"inv_pe{s}"), 9 * pair)
                    for dst, name in ((E32[s], "lmask32"), (E64[s], "lmask64")):
                        for e in range(2):
                            q = slice(HD * e, HD * e + HD)
                            g.tensor_tensor(dst[q, :, e * C:(e + 1) * C], Lr[s][q, :, :],
                                            cc(name, HD * e, HD * e + HD).unsqueeze(1).broadcast_to([HD, NP_, C]), ALU.mult)\
                                .then_inc(sem(f"inv_pool{s}"), 1)
            pool.wait_ge(sem("rk_done"), 1)
            for s in range(2):
                pool.wait_ge(sem(f"inv_pool{s}"), 4 * NPAIR)
            for half in range(2):
                g.memset(XS[half][:, :, :, :], 0.0).then_inc(sem("zeroed"), 1)
            pool.wait_ge(sem("zeroed"), 8)
            g.memset(UV[0:HD, :, :], 0.0).then_inc(sem("u_zero"), 1)
            def wide(name):
                return par[:, pcol[name]:pcol[name] + FT].unsqueeze(2).broadcast_to([P, FT, T])

            fold = sem("gate_folded")
            g.tensor_tensor(t11[:, :, :], t11[:, :, :], wide("ln_b"), ALU.add).then_inc(fold, 1)
            pool.wait_ge(fold, 1)
            g.tensor_tensor(t11[:, :, :], t11[:, :, :], Gt[:, :, :], ALU.mult).then_inc(fold, 1)
            pool.wait_ge(fold, 2)
            g.tensor_tensor(Gt[:, :, :], Gt[:, :, :], wide("ln_w"), ALU.mult).then_inc(fold, 1)
            pool.wait_ge(fold, 3)
            for c in range(NCH - 1):
                pool.wait_ge(sem("y_scaled"), c + 1)
                tok = slice(c * C, (c + 1) * C)
                y = YF[c % 2][:, :, :]
                g.tensor_tensor(y, y, Gt[:, :, tok], ALU.mult).then_inc(sem("y_gated"), 1)
                pool.wait_ge(sem("y_gated"), 2 * c + 1)
                g.tensor_tensor(y, y, t11[:, :, tok], ALU.add).then_inc(sem("y_gated"), 1)
                pool.wait_ge(sem("yh_ready"), c + 1)
                g.tensor_tensor(yl[:, :, tok], y, yh[:, :, tok].bitcast(f32), ALU.subtract).then_inc(sem("yl_ready"), 1)
            pool.wait_ge(sem("gate_pe"), 1)
            for x in (hpad[:, :, :, :], vblk[:, :, :], Sc[:, :, :, :], kcm[:, :, :, :]):
                g.memset(x, 0.0).then_inc(sem("zeroed"), 1)
            for n, (q, b) in enumerate([(q, b) for _ in range(HKV) for q in range(TT) for b in range(2)]):
                w = (q + 1) * P
                j = n // 4
                pool.wait_ge(sem("cof_ready"), n + 1)
                x = SB[n % 4][:, :, 0:w]
                g.tensor_tensor(x, x, cof[:, q, b, 4 * j:4 * j + 4].unsqueeze(2).broadcast_to([P, 4, w]), ALU.mult)\
                    .then_inc(sem("p_scaled"), 1)

    return nc


_INS = ["x", "mix_norm", "mlp_norm", "mlp_w1", "mlp_w2", "rwkv_mu", "rwkv_w_in", "rwkv_w0", "rwkv_w1", "rwkv_w2",
        "rwkv_a0", "rwkv_a1", "rwkv_a2", "rwkv_g1", "rwkv_g2", "rwkv_k_k", "rwkv_k_a", "rwkv_r_k", "rwkv_ln_w",
        "rwkv_ln_b", "rwkv_w_out", "nsa_w_in", "nsa_cmp_pe", "nsa_cmp_w1", "nsa_cmp_w2", "nsa_q_norm", "nsa_k_norm",
        "nsa_w_out"]


def kernel(**inputs):
    import concourse.bacc as bacc
    from concourse.bass_utils import run_bass_kernel_spmd

    nc = bacc.Bacc("TRN2", target_bir_lowering=False, num_devices=1)
    arrays, aps = {}, {}
    for name in _INS:
        a = np.ascontiguousarray(inputs[name])
        arrays[f"in_{name}"] = a
        aps[name] = nc.dram_tensor(f"in_{name}", a.shape, mybir.dt.from_np(a.dtype), kind="ExternalInput").ap()
    consts, at = constants()
    assert at == CONST_AT and consts.shape[1] == CONST_N
    arrays["in_consts"] = consts
    aps["consts"] = nc.dram_tensor("in_consts", consts.shape, mybir.dt.float32, kind="ExternalInput").ap()
    n = np.arange(H)[:, None]
    spread = np.concatenate([np.arange(D)[None, :] // HD == n, np.arange(FT)[None, :] == n // 2,
                             np.arange(P)[None, :] // HD == n % 2], 1).astype(np.float32)
    arrays["in_spread"] = spread
    aps["spread"] = nc.dram_tensor("in_spread", spread.shape, mybir.dt.float32, kind="ExternalInput").ap()
    out = nc.dram_tensor("out_0", (1, T, D), mybir.dt.float32, kind="ExternalOutput").ap()
    rwkv_nsa_trunk(nc, aps, out)
    r = run_bass_kernel_spmd(nc, [arrays], core_ids=[0])
    return r.results[0]["out_0"]
```
